# Optimizing a Trainium2 kernel written in Bass

```python
import jax, jax.numpy as jnp
from jax import lax
import numpy as np
import math

D_MODEL = 1024
BATCH = 1
SEQ = 256
DEPTH = 2

N_MIXERS = 3
PLE_DIM = 256
D_FF = 4 * D_MODEL
RMS_EPS = 1e-6
SC_WIDTH = 3
ATTN_HEAD_DIM = 128
ATTN_HEADS_PER_GROUP = D_MODEL // ATTN_HEAD_DIM
DILATED_PATTERNS = ((128, 1), (512, 4), (2048, 16))
N_ATTN_GROUPS = len(DILATED_PATTERNS)
ROPE_THETA = 500000.0
ROPE_DIM = ATTN_HEAD_DIM // 4
D_RNN = 1280
N_LRU_BLOCKS = 10
LRU_BLOCK = D_RNN // N_LRU_BLOCKS
LRU_CONV_WIDTH = 4
LRU_C = 8.0

N_LAYERS_A = len(range(0, DEPTH, N_MIXERS))
N_LAYERS_B = len(range(1, DEPTH, N_MIXERS))
N_LAYERS_C = len(range(2, DEPTH, N_MIXERS))


def rmsnorm(x, g):
    xf = x.astype(jnp.float32)
    y = xf * lax.rsqrt(jnp.mean(xf * xf, axis=-1, keepdims=True) + RMS_EPS)
    return (y * g.astype(jnp.float32)).astype(x.dtype)

def causal_depthwise_conv(x, w):
    k_width, ch = w.shape
    return lax.conv_general_dilated(
        x, w[:, None, :].astype(x.dtype), window_strides=(1,),
        padding=[(k_width - 1, 0)], dimension_numbers=('NWC', 'WIO', 'NWC'),
        feature_group_count=ch)

def partial_rotary(x, positions):
    half = ROPE_DIM // 2
    inv_freq = ROPE_THETA ** (-2.0 * jnp.arange(half, dtype=jnp.float32) / ROPE_DIM)
    ang = positions.astype(jnp.float32)[..., None] * inv_freq
    cos = jnp.cos(ang)[:, :, None, :]
    sin = jnp.sin(ang)[:, :, None, :]
    xf = x.astype(jnp.float32)
    x1 = xf[..., :half]
    x2 = xf[..., half:ROPE_DIM]
    out = jnp.concatenate([x1 * cos - x2 * sin, x2 * cos + x1 * sin, xf[..., ROPE_DIM:]], axis=-1)
    return out.astype(x.dtype)

def dilated_window_attention(q, k, v, window, dilation):
    b_, s_, h_, dh = q.shape
    n_back = window // dilation
    blk = n_back
    sub_len = s_ // dilation
    n_blk = -(-sub_len // blk)
    sub_pad = n_blk * blk

    def to_sub(t):
        t = t.reshape(b_, sub_len, dilation, h_, dh).transpose(0, 2, 1, 3, 4)
        t = t.reshape(b_ * dilation, sub_len, h_, dh)
        t = jnp.pad(t, ((0, 0), (0, sub_pad - sub_len), (0, 0), (0, 0)))
        return t.reshape(b_ * dilation, n_blk, blk, h_, dh)

    def with_prev(t):
        prev = jnp.pad(t[:, :-1], ((0, 0), (1, 0), (0, 0), (0, 0), (0, 0)))
        return jnp.concatenate([prev, t], axis=2)

    qb = to_sub(q)
    kk = with_prev(to_sub(k))
    vv = with_prev(to_sub(v))
    s = jnp.einsum('nbqhd,nbkhd->nbhqk', qb, kk,
                   preferred_element_type=jnp.float32) * (dh ** -0.5)
    qi = jnp.arange(blk)[:, None]
    kj = jnp.arange(2 * blk)[None, :]
    rel = blk + qi - kj
    band = (rel >= 0) & (rel <= n_back)
    k_pos = jnp.arange(n_blk)[:, None, None] * blk - blk + kj[None]
    valid = band[None] & (k_pos >= 0)
    s = jnp.where(valid[None, :, None], s, -jnp.inf)
    lse = jax.nn.logsumexp(s, axis=-1)
    probs = jnp.exp(s - lse[..., None])
    o = jnp.einsum('nbhqk,nbkhd->nbqhd', probs, vv.astype(jnp.float32))

    def from_sub(t):
        t = t.reshape((b_, dilation, sub_pad) + t.shape[3:])[:, :, :sub_len]
        t = jnp.moveaxis(t, 1, 2)
        return t.reshape((b_, s_) + t.shape[3:])

    return from_sub(o), from_sub(jnp.swapaxes(lse, 2, 3))

def short_conv_mixer(h, w_in, w_conv, w_out):
    gate_b, gate_c, xin = jnp.split(h @ w_in, 3, axis=-1)
    y = gate_b * causal_depthwise_conv(gate_c * xin, w_conv)
    return y @ w_out

def dilated_attention_mixer(h, positions, w_qkv, w_o):
    b_, s_, _ = h.shape
    g_, hh, dh = N_ATTN_GROUPS, ATTN_HEADS_PER_GROUP, ATTN_HEAD_DIM
    qkv = (h @ w_qkv).reshape(b_, s_, 3, g_ * hh, dh)
    q = partial_rotary(qkv[:, :, 0], positions).reshape(b_, s_, g_, hh, dh)
    k = partial_rotary(qkv[:, :, 1], positions).reshape(b_, s_, g_, hh, dh)
    v = qkv[:, :, 2].reshape(b_, s_, g_, hh, dh)
    outs, lses = [], []
    for g, (window, dilation) in enumerate(DILATED_PATTERNS):
        o_g, lse_g = dilated_window_attention(q[:, :, g], k[:, :, g], v[:, :, g], window, dilation)
        outs.append(o_g)
        lses.append(lse_g)
    weights = jax.nn.softmax(jnp.stack(lses, axis=0), axis=0)
    o = jnp.sum(weights[..., None] * jnp.stack(outs, axis=0), axis=0)
    return o.reshape(b_, s_, hh * dh).astype(h.dtype) @ w_o

def rglru_mixer(h, w_in, conv_w, conv_b, w_a, b_a, w_x, b_x, lam, w_out):
    b_, s_, _ = h.shape
    gate, xr = jnp.split(h @ w_in, 2, axis=-1)
    xr = causal_depthwise_conv(xr, conv_w) + conv_b
    xb = xr.reshape(b_, s_, N_LRU_BLOCKS, LRU_BLOCK)
    r_gate = jax.nn.sigmoid(jnp.einsum('bsnj,njk->bsnk', xb, w_a).reshape(b_, s_, D_RNN) + b_a)
    i_gate = jax.nn.sigmoid(jnp.einsum('bsnj,njk->bsnk', xb, w_x).reshape(b_, s_, D_RNN) + b_x)
    log_a = -LRU_C * r_gate.astype(jnp.float32) * jax.nn.softplus(-lam.astype(jnp.float32))
    a = jnp.exp(log_a)
    mult = jnp.sqrt(-jnp.expm1(2.0 * log_a))
    u = mult * (i_gate * xr).astype(jnp.float32)

    def combine(left, right):
        a_l, u_l = left
        a_r, u_r = right
        return a_l * a_r, a_r * u_l + u_r

    _, hs = lax.associative_scan(combine, (a, u), axis=1)
    y = hs.astype(h.dtype) * jax.nn.gelu(gate)
    return y @ w_out

def squared_relu_mlp(h, w_up, w_down):
    return jnp.square(jax.nn.relu(h @ w_up)) @ w_down

def first_inputs(seed: int = 0) -> dict:
    key = jax.random.key(seed)
    ks = iter(jax.random.split(key, 40))

    def nrm(shape, fan_in):
        return jax.random.normal(next(ks), shape, jnp.float32) * (fan_in ** -0.5)

    def gain(shape):
        return 1.0 + 0.05 * jax.random.normal(next(ks), shape, jnp.float32)

    def bias(shape):
        return 0.1 * jax.random.normal(next(ks), shape, jnp.float32)

    attn_width = N_ATTN_GROUPS * ATTN_HEADS_PER_GROUP * ATTN_HEAD_DIM
    u = jax.random.uniform(next(ks), (N_LAYERS_C, D_RNN), jnp.float32, 0.9, 0.999)
    sig = u ** (1.0 / LRU_C)
    return {
        'x': jax.random.normal(next(ks), (BATCH, SEQ, D_MODEL), jnp.float32),
        'p': jax.random.normal(next(ks), (DEPTH, BATCH, SEQ, PLE_DIM), jnp.float32),
        'positions': (jnp.arange(SEQ, dtype=jnp.int32)[None, :]
                      + jax.random.randint(next(ks), (BATCH, 1), 0, 1024, jnp.int32)),
        'norm_mix': gain((DEPTH, D_MODEL)),
        'norm_mlp': gain((DEPTH, D_MODEL)),
        'norm_ple': gain((DEPTH, D_MODEL)),
        'norm_final': gain((D_MODEL,)),
        'sc_w_in': nrm((N_LAYERS_A, D_MODEL, 3 * D_MODEL), D_MODEL),
        'sc_w_conv': nrm((N_LAYERS_A, SC_WIDTH, D_MODEL), SC_WIDTH),
        'sc_w_out': nrm((N_LAYERS_A, D_MODEL, D_MODEL), D_MODEL),
        'attn_w_qkv': nrm((N_LAYERS_B, D_MODEL, 3 * attn_width), D_MODEL),
        'attn_w_o': nrm((N_LAYERS_B, ATTN_HEADS_PER_GROUP * ATTN_HEAD_DIM, D_MODEL),
                        ATTN_HEADS_PER_GROUP * ATTN_HEAD_DIM),
        'lru_w_in': nrm((N_LAYERS_C, D_MODEL, 2 * D_RNN), D_MODEL),
        'lru_conv_w': nrm((N_LAYERS_C, LRU_CONV_WIDTH, D_RNN), LRU_CONV_WIDTH),
        'lru_conv_b': bias((N_LAYERS_C, D_RNN)),
        'lru_w_a': nrm((N_LAYERS_C, N_LRU_BLOCKS, LRU_BLOCK, LRU_BLOCK), LRU_BLOCK),
        'lru_b_a': bias((N_LAYERS_C, D_RNN)),
        'lru_w_x': nrm((N_LAYERS_C, N_LRU_BLOCKS, LRU_BLOCK, LRU_BLOCK), LRU_BLOCK),
        'lru_b_x': bias((N_LAYERS_C, D_RNN)),
        'lru_lambda': jnp.log(sig) - jnp.log1p(-sig),
        'lru_w_out': nrm((N_LAYERS_C, D_RNN, D_MODEL), D_RNN),
        'mlp_w_up': nrm((DEPTH, D_MODEL, D_FF), D_MODEL),
        'mlp_w_down': nrm((DEPTH, D_FF, D_MODEL), D_FF),
        'ple_w_gate': nrm((DEPTH, D_MODEL, D_MODEL), D_MODEL),
        'ple_w_proj': nrm((DEPTH, PLE_DIM, D_MODEL), PLE_DIM),
    }

def first_block(x, p, positions, norm_mix, norm_mlp, norm_ple, norm_final,
              sc_w_in, sc_w_conv, sc_w_out, attn_w_qkv, attn_w_o,
              lru_w_in, lru_conv_w, lru_conv_b, lru_w_a, lru_b_a, lru_w_x, lru_b_x,
              lru_lambda, lru_w_out, mlp_w_up, mlp_w_down, ple_w_gate, ple_w_proj):
    h = x
    for i in range(DEPTH):
        kind, j = i % N_MIXERS, i // N_MIXERS
        hn = rmsnorm(h, norm_mix[i])
        if kind == 0:
            mixed = short_conv_mixer(hn, sc_w_in[j], sc_w_conv[j], sc_w_out[j])
        elif kind == 1:
            mixed = dilated_attention_mixer(hn, positions, attn_w_qkv[j], attn_w_o[j])
        else:
            mixed = rglru_mixer(hn, lru_w_in[j], lru_conv_w[j], lru_conv_b[j], lru_w_a[j],
                                lru_b_a[j], lru_w_x[j], lru_b_x[j], lru_lambda[j], lru_w_out[j])
        h = h + mixed
        h = h + squared_relu_mlp(rmsnorm(h, norm_mlp[i]), mlp_w_up[i], mlp_w_down[i])
        ple_gate = jax.nn.sigmoid(rmsnorm(h, norm_ple[i]) @ ple_w_gate[i])
        h = h + ple_gate * (p[i].astype(h.dtype) @ ple_w_proj[i])
    return rmsnorm(h, norm_final)


N_A_LAYERS = DEPTH // 2
N_B_LAYERS = DEPTH - N_A_LAYERS
D_FF_2 = 2816

S5_GROUP_CH = 16
S5_GROUPS = D_MODEL // S5_GROUP_CH
S5_STATE = 64
DT_MIN = 0.001
DT_MAX = 0.1

N_HEADS = 16
HEAD_DIM = D_MODEL // N_HEADS
N_KV_HEADS = 4
Q_PER_KV = N_HEADS // N_KV_HEADS
CMP_LEN = 32
CMP_STRIDE = 16
CMP_HIDDEN = 2 * HEAD_DIM
SEL_LEN = 64
SEL_TOPN = 8
WIN = 512
WIN_QB = 128
SEL_QB = 64
N_BRANCH = 3
ATTN_SCALE = HEAD_DIM ** -0.5

NUM_BUCKETS = 32
MAX_DISTANCE = 128

NEG_INF = -1e30
BIG = 1e9


def _rmsnorm(x, g):
    xf = x.astype(jnp.float32)
    y = xf * lax.rsqrt(jnp.mean(xf * xf, axis=-1, keepdims=True) + RMS_EPS)
    return (y * g.astype(jnp.float32)).astype(x.dtype)

def _swiglu(x, w_in, w_out):
    a, b = jnp.split(x @ w_in, 2, axis=-1)
    return (jax.nn.silu(a) * b) @ w_out

def _rel_bucket(dist):
    n = jnp.maximum(dist, 0)
    max_exact = NUM_BUCKETS // 2
    logv = jnp.log(jnp.maximum(n, 1).astype(jnp.float32) / max_exact) / math.log(MAX_DISTANCE / max_exact)
    large = jnp.minimum(max_exact + (logv * (NUM_BUCKETS - max_exact)).astype(jnp.int32), NUM_BUCKETS - 1)
    return jnp.where(n < max_exact, n, large)

def _masked_softmax(logits, mask):
    return jax.nn.softmax(jnp.where(mask, logits, NEG_INF), axis=-1)

def _s5_mixer(u, a_re, a_im, log_dt, b_re, b_im, c_re, c_im, d_skip, w_glu):
    bsz, seq, _ = u.shape
    ug = u.reshape(bsz, seq, S5_GROUPS, S5_GROUP_CH)
    dt = jnp.exp(log_dt)[:, None]
    mag = jnp.exp(a_re * dt)
    ab_re = mag * jnp.cos(a_im * dt)
    ab_im = mag * jnp.sin(a_im * dt)
    den = a_re * a_re + a_im * a_im
    z_re = ((ab_re - 1.0) * a_re + ab_im * a_im) / den
    z_im = (ab_im * a_re - (ab_re - 1.0) * a_im) / den
    bb_re = z_re[..., None] * b_re - z_im[..., None] * b_im
    bb_im = z_re[..., None] * b_im + z_im[..., None] * b_re
    bu_re = jnp.einsum('bsgh,gph->bsgp', ug, bb_re)
    bu_im = jnp.einsum('bsgh,gph->bsgp', ug, bb_im)
    shape = (1, seq, S5_GROUPS, S5_STATE)
    la_re = jnp.broadcast_to(ab_re, shape)
    la_im = jnp.broadcast_to(ab_im, shape)

    def combine(e1, e2):
        ar1, ai1, br1, bi1 = e1
        ar2, ai2, br2, bi2 = e2
        return (ar2 * ar1 - ai2 * ai1,
                ar2 * ai1 + ai2 * ar1,
                ar2 * br1 - ai2 * bi1 + br2,
                ar2 * bi1 + ai2 * br1 + bi2)

    _, _, x_re, x_im = lax.associative_scan(combine, (la_re, la_im, bu_re, bu_im), axis=1)
    y = (jnp.einsum('bsgp,ghp->bsgh', x_re, c_re) - jnp.einsum('bsgp,ghp->bsgh', x_im, c_im)
         + d_skip * ug)
    y = jax.nn.gelu(y.reshape(bsz, seq, D_MODEL))
    return y * jax.nn.sigmoid(y @ w_glu)

def _shared_kv(h, kv_norm, w_kv, k_norm_cmp, k_norm_slc, k_norm_win,
               cmp_pos_k, cmp_pos_v, cmp_k_w1, cmp_k_w2, cmp_v_w1, cmp_v_w2):
    bsz, seq, _ = h.shape
    kv = (_rmsnorm(h, kv_norm) @ w_kv).reshape(bsz, seq, 2 * N_BRANCH, N_KV_HEADS, HEAD_DIM)
    n_cmp = (seq - CMP_LEN) // CMP_STRIDE + 1
    blk = jnp.arange(n_cmp)[:, None] * CMP_STRIDE + jnp.arange(CMP_LEN)[None, :]

    def compress(src, pos, w1, w2):
        blocks = src[:, blk] + pos[None, None, :, None, :]
        hid = jax.nn.gelu(jnp.einsum('bclgd,ldh->bcgh', blocks, w1))
        return jnp.einsum('bcgh,hd->bcgd', hid, w2)

    k_cmp = _rmsnorm(compress(kv[:, :, 0], cmp_pos_k, cmp_k_w1, cmp_k_w2), k_norm_cmp)
    v_cmp = compress(kv[:, :, 1], cmp_pos_v, cmp_v_w1, cmp_v_w2)
    k_slc = _rmsnorm(kv[:, :, 2], k_norm_slc)
    v_slc = kv[:, :, 3]
    k_win = _rmsnorm(kv[:, :, 4], k_norm_win)
    v_win = kv[:, :, 5]
    return (k_cmp, v_cmp, k_slc, v_slc, k_win, v_win)

def _compressed_branch(q, k_cmp, v_cmp, rel_bias):
    seq = q.shape[1]
    n_cmp = k_cmp.shape[1]
    n_sel = seq // SEL_LEN
    t = jnp.arange(seq)
    c_start = jnp.arange(n_cmp) * CMP_STRIDE
    dist = t[:, None] - (c_start + CMP_LEN - 1)[None, :]
    valid = dist >= 0
    bias = rel_bias[_rel_bucket(dist)].transpose(2, 0, 1).reshape(N_KV_HEADS, Q_PER_KV, seq, n_cmp)
    logits = jnp.einsum('bsgrd,bcgd->bgrsc', q, k_cmp).astype(jnp.float32) * ATTN_SCALE + bias
    p = _masked_softmax(logits, valid) * jnp.any(valid, axis=-1)[:, None].astype(jnp.float32)
    o = jnp.einsum('bgrsc,bcgd->bsgrd', p.astype(v_cmp.dtype), v_cmp)
    j_start = jnp.arange(n_sel) * SEL_LEN
    ov = jnp.clip(jnp.minimum(c_start[:, None] + CMP_LEN, j_start[None, :] + SEL_LEN)
                  - jnp.maximum(c_start[:, None], j_start[None, :]), 0, None)
    overlap = ov.astype(jnp.float32) / CMP_LEN
    p_slc = jnp.einsum('bgrsc,cj->bgsj', p, overlap)
    return o, p_slc

def _select_blocks(p_slc):
    seq, n_sel = p_slc.shape[2], p_slc.shape[3]
    k = min(SEL_TOPN, n_sel)
    t = jnp.arange(seq)[:, None]
    j = jnp.arange(n_sel)[None, :]
    cur = t // SEL_LEN
    forced = (j == 0) | (j == cur) | (j == cur - 1)
    causal = j * SEL_LEN <= t
    score = jnp.where(forced, BIG, jnp.where(causal, p_slc, -BIG))
    _, idx = lax.top_k(score, k)
    return idx

def _selected_branch(q, k_slc, v_slc, idx, rel_bias):
    bsz, seq = q.shape[0], q.shape[1]
    n_top = idx.shape[-1]
    kl = n_top * SEL_LEN
    n_ch = seq // SEL_QB
    kst = k_slc.transpose(0, 2, 1, 3)
    vst = v_slc.transpose(0, 2, 1, 3)
    table = rel_bias.reshape(NUM_BUCKETS, N_KV_HEADS, Q_PER_KV).transpose(1, 0, 2)
    gather = jax.vmap(jax.vmap(lambda a, i: a[i]))
    qc = q.reshape(bsz, n_ch, SEL_QB, N_KV_HEADS, Q_PER_KV, HEAD_DIM).transpose(1, 0, 2, 3, 4, 5)
    ic = idx.reshape(bsz, N_KV_HEADS, n_ch, SEL_QB, n_top).transpose(2, 0, 1, 3, 4)

    def step(args):
        ci, qb, ib = args
        tok = (ib[..., None] * SEL_LEN + jnp.arange(SEL_LEN)).reshape(bsz, N_KV_HEADS, SEL_QB * kl)
        kg = gather(kst, tok).reshape(bsz, N_KV_HEADS, SEL_QB, kl, HEAD_DIM)
        vg = gather(vst, tok).reshape(bsz, N_KV_HEADS, SEL_QB, kl, HEAD_DIM)
        tok = tok.reshape(bsz, N_KV_HEADS, SEL_QB, kl)
        qpos = ci * SEL_QB + jnp.arange(SEL_QB)
        dist = qpos[None, None, :, None] - tok
        bias = table[jnp.arange(N_KV_HEADS)[None, :, None, None], _rel_bucket(dist)]
        logits = (jnp.einsum('bqgrd,bgqkd->bgrqk', qb, kg).astype(jnp.float32) * ATTN_SCALE
                  + bias.transpose(0, 1, 4, 2, 3))
        p = _masked_softmax(logits, (dist >= 0)[:, :, None])
        return jnp.einsum('bgrqk,bgqkd->bqgrd', p.astype(vg.dtype), vg)

    out = lax.map(step, (jnp.arange(n_ch), qc, ic))
    return out.transpose(1, 0, 2, 3, 4, 5).reshape(bsz, seq, N_KV_HEADS, Q_PER_KV, HEAD_DIM)

def _window_branch(q, k_win, v_win, rel_bias):
    bsz, seq = q.shape[0], q.shape[1]
    n_blk = seq // WIN_QB
    span = WIN + WIN_QB
    kp = jnp.pad(k_win, ((0, 0), (WIN, 0), (0, 0), (0, 0)))
    vp = jnp.pad(v_win, ((0, 0), (WIN, 0), (0, 0), (0, 0)))
    dist = WIN + jnp.arange(WIN_QB)[:, None] - jnp.arange(span)[None, :]
    band = (dist >= 0) & (dist < WIN)
    bias = rel_bias[_rel_bucket(dist)].transpose(2, 0, 1).reshape(N_KV_HEADS, Q_PER_KV, WIN_QB, span)
    qb_all = q.reshape(bsz, n_blk, WIN_QB, N_KV_HEADS, Q_PER_KV, HEAD_DIM).transpose(1, 0, 2, 3, 4, 5)

    def step(args):
        bi, qb = args
        start = bi * WIN_QB
        kb = lax.dynamic_slice_in_dim(kp, start, span, axis=1)
        vb = lax.dynamic_slice_in_dim(vp, start, span, axis=1)
        kpos = start - WIN + jnp.arange(span)
        mask = band & (kpos >= 0)[None, :]
        logits = jnp.einsum('bqgrd,bkgd->bgrqk', qb, kb).astype(jnp.float32) * ATTN_SCALE + bias
        p = _masked_softmax(logits, mask)
        return jnp.einsum('bgrqk,bkgd->bqgrd', p.astype(vb.dtype), vb)

    out = lax.map(step, (jnp.arange(n_blk), qb_all))
    return out.transpose(1, 0, 2, 3, 4, 5).reshape(bsz, seq, N_KV_HEADS, Q_PER_KV, HEAD_DIM)

def _nsa_mixer(u, kv, w_qg, q_norm, w_o, rel_bias):
    k_cmp, v_cmp, k_slc, v_slc, k_win, v_win = kv
    bsz, seq, _ = u.shape
    qg = u @ w_qg
    q = _rmsnorm(qg[..., :N_HEADS * HEAD_DIM].reshape(bsz, seq, N_KV_HEADS, Q_PER_KV, HEAD_DIM), q_norm)
    gates = jax.nn.sigmoid(qg[..., N_HEADS * HEAD_DIM:].reshape(bsz, seq, N_KV_HEADS, Q_PER_KV, N_BRANCH))
    o_cmp, p_slc = _compressed_branch(q, k_cmp, v_cmp, rel_bias)
    idx = _select_blocks(p_slc)
    o_slc = _selected_branch(q, k_slc, v_slc, idx, rel_bias)
    o_win = _window_branch(q, k_win, v_win, rel_bias)
    o = gates[..., 0:1] * o_cmp + gates[..., 1:2] * o_slc + gates[..., 2:3] * o_win
    return o.reshape(bsz, seq, D_MODEL) @ w_o

def second_inputs(seed: int = 0) -> dict:
    key = jax.random.key(seed)
    ks = iter(jax.random.split(key, 40))

    def nrm(shape, scale):
        return jax.random.normal(next(ks), shape, jnp.float32) * scale

    def gain(shape):
        return 1.0 + nrm(shape, 0.02)

    na, nb = N_A_LAYERS, N_B_LAYERS
    g, p, ch = S5_GROUPS, S5_STATE, S5_GROUP_CH
    return {
        'x': nrm((BATCH, SEQ, D_MODEL), 1.0),
        'rel_bias': nrm((NUM_BUCKETS, N_HEADS), 0.5),
        'ffn1_norm': gain((DEPTH, D_MODEL)),
        'ffn1_w_in': nrm((DEPTH, D_MODEL, 2 * D_FF_2), D_MODEL ** -0.5),
        'ffn1_w_out': nrm((DEPTH, D_FF_2, D_MODEL), D_FF_2 ** -0.5),
        'mix_norm': gain((DEPTH, D_MODEL)),
        'ffn2_norm': gain((DEPTH, D_MODEL)),
        'ffn2_w_in': nrm((DEPTH, D_MODEL, 2 * D_FF_2), D_MODEL ** -0.5),
        'ffn2_w_out': nrm((DEPTH, D_FF_2, D_MODEL), D_FF_2 ** -0.5),
        's5_a_re': -0.5 + nrm((na, g, p), 0.01),
        's5_a_im': jnp.pi * jnp.arange(p, dtype=jnp.float32)[None, None, :] + nrm((na, g, p), 0.01),
        's5_log_dt': jax.random.uniform(next(ks), (na, g), jnp.float32, math.log(DT_MIN), math.log(DT_MAX)),
        's5_b_re': nrm((na, g, p, ch), (2.0 * ch) ** -0.5),
        's5_b_im': nrm((na, g, p, ch), (2.0 * ch) ** -0.5),
        's5_c_re': nrm((na, g, ch, p), (2.0 * p) ** -0.5),
        's5_c_im': nrm((na, g, ch, p), (2.0 * p) ** -0.5),
        's5_d': nrm((na, g, ch), 1.0),
        's5_w_glu': nrm((na, D_MODEL, D_MODEL), D_MODEL ** -0.5),
        'kv_norm': gain((D_MODEL,)),
        'w_kv': nrm((D_MODEL, 2 * N_BRANCH * N_KV_HEADS * HEAD_DIM), D_MODEL ** -0.5),
        'k_norm_cmp': gain((HEAD_DIM,)),
        'k_norm_slc': gain((HEAD_DIM,)),
        'k_norm_win': gain((HEAD_DIM,)),
        'cmp_pos_k': nrm((CMP_LEN, HEAD_DIM), 0.1),
        'cmp_pos_v': nrm((CMP_LEN, HEAD_DIM), 0.1),
        'cmp_k_w1': nrm((CMP_LEN, HEAD_DIM, CMP_HIDDEN), (CMP_LEN * HEAD_DIM) ** -0.5),
        'cmp_k_w2': nrm((CMP_HIDDEN, HEAD_DIM), CMP_HIDDEN ** -0.5),
        'cmp_v_w1': nrm((CMP_LEN, HEAD_DIM, CMP_HIDDEN), (CMP_LEN * HEAD_DIM) ** -0.5),
        'cmp_v_w2': nrm((CMP_HIDDEN, HEAD_DIM), CMP_HIDDEN ** -0.5),
        'w_qg': nrm((nb, D_MODEL, N_HEADS * HEAD_DIM + N_BRANCH * N_HEADS), D_MODEL ** -0.5),
        'q_norm': gain((nb, HEAD_DIM)),
        'w_o': nrm((nb, D_MODEL, D_MODEL), D_MODEL ** -0.5),
    }

def second_block(x, rel_bias, ffn1_norm, ffn1_w_in, ffn1_w_out, mix_norm, ffn2_norm, ffn2_w_in, ffn2_w_out,
              s5_a_re, s5_a_im, s5_log_dt, s5_b_re, s5_b_im, s5_c_re, s5_c_im, s5_d, s5_w_glu,
              kv_norm, w_kv, k_norm_cmp, k_norm_slc, k_norm_win, cmp_pos_k, cmp_pos_v,
              cmp_k_w1, cmp_k_w2, cmp_v_w1, cmp_v_w2, w_qg, q_norm, w_o):
    h = x
    kv = None
    for layer in range(DEPTH):
        h = h + 0.5 * _swiglu(_rmsnorm(h, ffn1_norm[layer]), ffn1_w_in[layer], ffn1_w_out[layer])
        u = _rmsnorm(h, mix_norm[layer])
        if layer < N_A_LAYERS:
            a = layer
            h = h + _s5_mixer(u, s5_a_re[a], s5_a_im[a], s5_log_dt[a], s5_b_re[a], s5_b_im[a],
                              s5_c_re[a], s5_c_im[a], s5_d[a], s5_w_glu[a])
        else:
            b = layer - N_A_LAYERS
            h = h + _nsa_mixer(u, kv, w_qg[b], q_norm[b], w_o[b], rel_bias)
        h = h + 0.5 * _swiglu(_rmsnorm(h, ffn2_norm[layer]), ffn2_w_in[layer], ffn2_w_out[layer])
        if layer == N_A_LAYERS - 1:
            kv = _shared_kv(h, kv_norm, w_kv, k_norm_cmp, k_norm_slc, k_norm_win,
                            cmp_pos_k, cmp_pos_v, cmp_k_w1, cmp_k_w2, cmp_v_w1, cmp_v_w2)
    return h


def setup_inputs(seed=0):
    out = dict(first_inputs(seed))
    for name, value in second_inputs(seed + 1).items():
        if name != "x":
            out[name + "_2"] = value
    return out


def reference(
    x, p, positions, norm_mix, norm_mlp, norm_ple, norm_final, sc_w_in, sc_w_conv, sc_w_out,
    attn_w_qkv, attn_w_o, lru_w_in, lru_conv_w, lru_conv_b, lru_w_a, lru_b_a, lru_w_x, lru_b_x,
    lru_lambda, lru_w_out, mlp_w_up, mlp_w_down, ple_w_gate, ple_w_proj, rel_bias_2,
    ffn1_norm_2, ffn1_w_in_2, ffn1_w_out_2, mix_norm_2, ffn2_norm_2, ffn2_w_in_2, ffn2_w_out_2,
    s5_a_re_2, s5_a_im_2, s5_log_dt_2, s5_b_re_2, s5_b_im_2, s5_c_re_2, s5_c_im_2, s5_d_2,
    s5_w_glu_2, kv_norm_2, w_kv_2, k_norm_cmp_2, k_norm_slc_2, k_norm_win_2, cmp_pos_k_2,
    cmp_pos_v_2, cmp_k_w1_2, cmp_k_w2_2, cmp_v_w1_2, cmp_v_w2_2, w_qg_2, q_norm_2, w_o_2,
):
    x = first_block(
        x, p, positions, norm_mix, norm_mlp, norm_ple, norm_final, sc_w_in, sc_w_conv, sc_w_out,
        attn_w_qkv, attn_w_o, lru_w_in, lru_conv_w, lru_conv_b, lru_w_a, lru_b_a, lru_w_x,
        lru_b_x, lru_lambda, lru_w_out, mlp_w_up, mlp_w_down, ple_w_gate, ple_w_proj,
    )
    return second_block(
        x, rel_bias_2, ffn1_norm_2, ffn1_w_in_2, ffn1_w_out_2, mix_norm_2, ffn2_norm_2,
        ffn2_w_in_2, ffn2_w_out_2, s5_a_re_2, s5_a_im_2, s5_log_dt_2, s5_b_re_2, s5_b_im_2,
        s5_c_re_2, s5_c_im_2, s5_d_2, s5_w_glu_2, kv_norm_2, w_kv_2, k_norm_cmp_2, k_norm_slc_2,
        k_norm_win_2, cmp_pos_k_2, cmp_pos_v_2, cmp_k_w1_2, cmp_k_w2_2, cmp_v_w1_2, cmp_v_w2_2,
        w_qg_2, q_norm_2, w_o_2,
    )


_drawn_inputs = setup_inputs


def setup_inputs(seed=0):
    import zlib

    import numpy as np

    out = dict(_drawn_inputs(seed))
    spreads = {}
    factors = {'norm_ple': 6.722,
     'ffn1_norm_2': 4.868,
     'mix_norm_2': 6.149,
     'ffn2_norm_2': 5.469,
     's5_a_re_2': 64.0,
     's5_log_dt_2': 2.776,
     's5_b_re_2': 3.462,
     's5_b_im_2': 3.427,
     's5_c_re_2': 3.407,
     's5_c_im_2': 3.342,
     'kv_norm_2': 8.0,
     'k_norm_cmp_2': 34.627,
     'k_norm_slc_2': 8.0,
     'k_norm_win_2': 8.0,
     'cmp_pos_k_2': 8.0,
     'q_norm_2': 8.0,
     'cmp_pos_v_2': 8.0}
    for name, (base, spread) in spreads.items():
        noise = np.random.default_rng([zlib.crc32(name.encode()), seed]).standard_normal(out[name].shape)
        drawn = base * np.exp(spread * noise) if base else spread * noise
        out[name] = __import__('jax').numpy.asarray(drawn.astype(out[name].dtype))
    for name, factor in factors.items():
        out[name] = (out[name] * factor).astype(out[name].dtype)
    return out
```

```python
import math
from contextlib import ExitStack

import numpy as np

import concourse.bass as bass
from concourse import mybir

ALU = mybir.AluOpType
ACT = mybir.ActivationFunctionType
AX = mybir.AxisListType
F32 = mybir.dt.float32
F32R = mybir.dt.float32r
BF16 = mybir.dt.bfloat16
I32 = mybir.dt.int32

P = 128
SEQ = 256
D = 1024
KC = D // P
TT = SEQ // P
PAIRS = KC // 2
EPS = 1e-6
D_FF = 4096
MLP_PAIRS = D_FF // 256
D_FF2 = 2816
FFN_PAIRS = D_FF2 // 256
PLE = 256
UNIT = 2048
RING = 3

DH = 128
GROUPS = ((128, 1), (512, 4), (2048, 16))
NG = len(GROUPS)
HEADS = D // DH
HEAD_PAIRS = HEADS // 2
ROPE = DH // 4
THETA = 500000.0
SCALE = DH ** -0.5
NEG = -1e30

S5_CH, S5_STATE = 16, 64
S5_G = D // S5_CH
ST = S5_G * S5_STATE // P
EB = 4

NH, HD, KVH = 16, 64, 4
REP = NH // KVH
CL, CS = 32, 16
NCMP = (SEQ - CL) // CS + 1
NBUCKET, MAXDIST = 32, 128
NDIST = SEQ + P - 1
NSCALE = HD ** -0.5
NQ = NH // 2

STAGES = [("sc_in", 12), ("sc_out", 4), ("mlp0", 32), ("ple0", 5), ("qkv", 36), ("wo", 4), ("mlp1", 32),
          ("ple1", 5), ("ffn0", 33), ("glu", 4), ("ffn1", 33), ("kv", 6), ("ffn2", 33), ("qg", 4),
          ("nwo", 4), ("ffn3", 33)]
BASE = {}
_at = 0
for _name, _n in STAGES:
    BASE[_name] = _at
    _at += _n
NU = _at

R_IN, R_SC, R_MLP0, R_PLE0, R_WO, R_MLP1, R_PLE1, R_FIN, R_FFN0, R_GLU, R_FFN1, R_FFN2, R_NWO, R_FFN3 = range(14)
XUSE = [R_IN, R_SC, R_MLP0, R_PLE0, R_WO, R_MLP1, R_FIN, R_GLU, R_FFN1, "kv", R_FFN2, R_NWO]
XBUF = {R_IN: 0, R_SC: 0, R_MLP0: 1, R_PLE0: 0, R_WO: 0, R_MLP1: 1, R_FIN: 0, R_GLU: 0, R_FFN1: 1, "kv": 0,
        R_FFN2: 1, R_NWO: 1}
XBASE = {r: PAIRS * n for n, r in enumerate(XUSE)}
HID_BASE = {"mlp0": 0, "mlp1": 16, "ffn0": 32, "ffn1": 43, "ffn2": 54, "ffn3": 65}

VCOL = {}
_at = 0
for _name, _n in [("mix0", 8), ("mlp0", 8), ("ple0", 8), ("mix1", 8), ("mlp1", 8), ("ple1", 8), ("final", 8),
                  ("ffn0", 8), ("s5mix", 8), ("ffn1", 8), ("kvn", 8), ("ffn2", 8), ("nsamix", 8), ("ffn3", 8),
                  ("conv", 24), ("s5d", 8), ("qn", 1), ("kcn", 1), ("ksn", 1), ("kwn", 1),
                  ("are", ST), ("aim", ST), ("ldt", ST)]:
    VCOL[_name] = _at
    _at += _n
NVEC = _at
GAIN = {R_IN: "mix0", R_SC: "mlp0", R_MLP0: "ple0", R_PLE0: "mix1", R_WO: "mlp1", R_MLP1: "ple1",
        R_FIN: "ffn0", R_GLU: "ffn1", R_FFN1: "kvn", "kv": "ffn2", R_FFN2: "nsamix", R_NWO: "ffn3"}

CCOL = {}
_at = 0
for _name, _n in [("ident", P), ("half", P), ("mask0", NG * P), ("mask1", NG * SEQ), ("anyc", TT), ("invf", 1),
                  ("sgn", 1)]:
    CCOL[_name] = _at
    _at += _n
NCON = _at
TWO_PI_1 = 6.28125
TWO_PI_2 = float(np.float32(2 * math.pi - 6.28125))
TWO_PI_3 = 2 * math.pi - 6.28125 - TWO_PI_2
ROUND = 1.5 * 2.0 ** 23
S5_HALVINGS = 6


def head_order():
    return [(2 * a + half) * REP + r for a in range(KVH // 2) for r in range(REP) for half in range(2)]



SEM_NAMES = (
    "con_landed", "h_landed", "misc_landed", "p_landed", "e_stored", "e_landed0", "e_landed1", "bias_stored",
    "tbl_landed", "cmpw_landed", "pos_landed", "wg_landed", "bias_in_landed", "out_stored",
    "hi_ready", "lo_ready", "unit_done",
    "fill_done",
    "h_ready", "xh_ready", "xl_ready", "sq_ready", "sq_used", "acc_done", "sum_ready", "var_ready", "rst_ready",
    "diag_ready", "bcast_ready", "rs_ready", "rs2_ready", 
    "c_copied", "v_raw", "v_ready", "tap_done", "b_scaled", "y_ready", "y_hi", "y_lo",
    "relu_ready", "act_ready", "a_scaled", "b_gated", "silu_ready", "prod_ready", "hid_hi_ready", "hid_lo_ready",
    "p_hi_ready", "p_lo_ready", "gate_scaled", "gate_ready", "gated",
    "rope_step", "sin_ready", "rope_ready", "rope_rs", "swapped", "qk_main", "sin_part", "qk_ready", "v_copied",
    "s_done", "masked", "max_done", "bias_ready", "exp_done", "rden_ready", "pt_done", "pt_copied", "pv_done",
    "o_scaled", "ot_done", "o_hi", "o_lo",
    "sm_dve", "sm_act", "bb_ready", "bt_done", "bt_ready", "ct_ready", "e_step", "e_base",
    "u5_ready", "bu_done", "turned", "drive", "z_ready", "turned_back", "y_done", "y_in", "gelu_done", "g_hi",
    "g_lo",
    "src_ready", "k_scaled", "k_sq", "k_sum", "k_mean", "k_ln", "k_exp", "k_step", "k_ready", "vs_ready", "blk_ready",
    "hid_done", "hg_ready", "w2_done", "vc_ready", "bv_done", "bv_copied", "cb_done", "cb_ready",
    "rel_ready",
    "wg_hi_ready", "wg_lo_ready", "gate_done", "gate_sig", "gate_all", "q_staged", "n_s", "n_log",
    "n_max", "n_exp", "n_rec", "n_fac", "n_t", "n_ta", "n_tv", "n_pv", "n_part", "n_ot", "n_hi", "n_lo",
)


S5_R = 27


def program(nc, A):
    with ExitStack() as ctx:
        def sb(name, shape, dt=F32, scope=ctx):
            return scope.enter_context(nc.sbuf_tensor(name, shape, dt))

        raw = sb("raw", [P, RING, UNIT])
        w_hi = sb("w_hi", [P, RING, UNIT], F32R)
        w_lo = sb("w_lo", [P, RING, UNIT], F32R)
        x_hi = [sb(f"x_hi{i}", [P, KC, SEQ], F32R) for i in range(2)]
        x_lo = [sb(f"x_lo{i}", [P, KC, SEQ], F32R) for i in range(2)]
        h = sb("h", [P, KC, SEQ])
        vec = sb("vec", [P, NVEC])
        con = sb("con", [P, NCON])
        rs = sb("rs", [P, 2, SEQ])
        rs_tok = sb("rs_tok", [P, TT])
        var_tok = sb("var_tok", [P, TT])
        diag = sb("diag", [P, TT, P])
        sq = sb("sq", [P, 2, 2, SEQ])
        ssum = sb("ssum", [P, 2, SEQ])
        ones = sb("ones", [P, P])
        nhalf = sb("nhalf", [P, TT])
        zero = sb("zero", [P, 512], BF16)
        ta = sb("ta", [P, 2, SEQ])
        tb = sb("tb", [P, 2, SEQ])
        tc = sb("tc", [P, 2, SEQ])
        halfpi = sb("halfpi", [P, 1])
        hid_hi = sb("hid_hi", [P, 2, SEQ], F32R)
        hid_lo = sb("hid_lo", [P, 2, SEQ], F32R)

        with ExitStack() as first:
            p_in = sb("p_in", [P, 2, SEQ], scope=first)
            p_hi = sb("p_hi", [P, 2, SEQ], F32R, scope=first)
            p_lo = sb("p_lo", [P, 2, SEQ], F32R, scope=first)
            bt = sb("bt", [P, KC, 2, P], scope=first)
            ct = sb("ct", [P, 3, ST, 32], scope=first)
            mag = sb("mag", [P, ST], scope=first)
            with ExitStack() as s:
                vp = sb("vp", [P, 2, SEQ + 2], scope=s)
                yc = sb("yc", [P, 2, SEQ], scope=s)
                rs2 = sb("rs2", [P, 2, SEQ], scope=s)
                e_tab = sb("e_tab", [P, EB, 2, SEQ], scope=s)
                e_t1 = sb("e_t1", [P, EB, 2, P], scope=s)
                e_t2 = sb("e_t2", [P, EB, 2, P], scope=s)
                e_one = sb("e_one", [P, ST, 2], scope=s)
                s5b = sb("s5b", [P, 2, ST, S5_CH], scope=s)
                bb = sb("bb", [P, 2, ST, 32], scope=s)
                sm = sb("sm", [P, 16, ST], scope=s)
            with ExitStack() as s:
                posi = sb("posi", [P, SEQ], I32, scope=s)
                ang = sb("ang", [P, 3, SEQ], scope=s)
                rope_c = sb("rope_c", [P, SEQ], scope=s)
                rope_s = sb("rope_s", [P, SEQ], scope=s)
                cos_rs = sb("cos_rs", [P, SEQ], scope=s)
                sin_rs = sb("sin_rs", [P, SEQ], scope=s)
                swap = sb("swap", [32, 2, SEQ], scope=s)
                qk = sb("qk", [P, 2, NG, 2, SEQ], scope=s)
                vv = sb("vv", [P, TT, NG, 2 * DH], scope=s)
                lg0 = sb("lg0", [P, NG, P], scope=s)
                lg1 = sb("lg1", [P, NG, SEQ], scope=s)
                pt = sb("pt", [P, 3, 3 * P], scope=s)
                nmax = sb("nmax", [P, TT], scope=s)
                nbias = sb("nbias", [P, TT], scope=s)
                den = sb("den", [P, TT], scope=s)
                rden = sb("rden", [P, TT], scope=s)
                ot = sb("ot", [P, TT, DH], scope=s)
            with ExitStack() as s:
                e_ring = sb("e_ring", [P, 2, EB, 2, SEQ], scope=s)
                u5 = sb("u5", [P, KC, SEQ], scope=s)
                y5 = sb("y5", [P, KC, SEQ], scope=s)
                z5 = sb("z5", [P, 2, 2, SEQ], scope=s)
                n1 = sb("n1", [P, 2, SEQ], scope=s)
                n2 = sb("n2", [P, 2, SEQ], scope=s)
        with ExitStack() as s:
            src = sb("src", [P, 2, 2, SEQ], scope=s)
            ks = sb("ks", [P, 2, 2, SEQ], scope=s)
            vs = sb("vs", [P, 2, TT, KVH * HD], scope=s)
            kcmp = sb("kcmp", [P, 2, NCMP], scope=s)
            vcmp = sb("vcmp", [NCMP, KVH, HD], scope=s)
            cmp_bias = sb("cmp_bias", [P, TT * NCMP, NH], scope=s)
            tbl = sb("tbl", [P, NH, SEQ], scope=s)
            gate = sb("gate", [P, TT, 3 * NH], scope=s)
            with ExitStack() as t:
                w1 = sb("w1", [P, CL, 2 * HD], scope=t)
                blk = sb("blk", [P, CL, 2, NCMP], scope=t)
                w2 = sb("w2", [P, 2, HD], scope=t)
                hg = sb("hg", [P, 2, 2 * NCMP], scope=t)
                posc = sb("posc", [P, 2, CL], scope=t)
                rel = sb("rel", [NBUCKET + 1, NH], scope=t)
                oh = sb("oh", [NBUCKET + 1, NDIST], scope=t)
                bv = sb("bv", [NH, NDIST], scope=t)
            with ExitStack() as t:
                ohc = sb("ohc", [NBUCKET + 1, TT * NCMP, P], scope=t)
            with ExitStack() as t:
                q2 = sb("q2", [P, NQ, SEQ], scope=t)
                qst = sb("qst", [P, 2, SEQ], scope=t)
                wg = sb("wg", [P, KC, 3 * NH], scope=t)
                wg_hi = sb("wg_hi", [P, KC, 3 * NH], F32R, scope=t)
                wg_lo = sb("wg_lo", [P, KC, 3 * NH], F32R, scope=t)
                lg = sb("lg", [P, 2, 2, 3 * P], scope=t)
                lgc = sb("lgc", [P, 2, TT, NCMP], scope=t)
                ptn = sb("ptn", [P, 2, 2, 3 * P], scope=t)
                ptc = sb("ptc", [NCMP, 2, SEQ], scope=t)
                nm = sb("nm", [P, 2, 3, TT], scope=t)
                dn = sb("dn", [P, 2, 3, TT], scope=t)
                fac = sb("fac", [P, 2, 3, TT], scope=t)
                oc = sb("oc", [P, 2, TT, 2, HD], scope=t)

        psum = ctx.enter_context(nc.psum_tensor("psum", [P, 8, 512], F32))
        DB = [psum[:, b] for b in range(4)]
        U = [psum[:, 4], psum[:, 5]]
        MB = psum[:, 6]
        XB = psum[:, 7]
        U3 = [U[0], U[1], XB]

        def two(ap):
            return ap.rearrange("p (c t) -> p c t", c=2)

        sem = {name: ctx.enter_context(nc.semaphore(name)) for name in SEM_NAMES}
        raw_landed = [ctx.enter_context(nc.semaphore(f"raw_landed{i}")) for i in range(RING)]

        def col(name, c=0, n=1):
            return vec[:, VCOL[name] + c:VCOL[name] + c + n]

        def cst(name, n):
            return con[:, CCOL[name]:CCOL[name] + n]

        ident = cst("ident", P)

        def hbase(r):
            return PAIRS * (r - 1)

        def chunk(ap, c, n=1):
            return ap[:, bass.ds(c, n), :]

        block = ctx.enter_context(nc.Block())

        @block.sync
        def _(sp):
            sp.dma_start(con[:], A["con"]).then_inc(sem["con_landed"], 16)
            for u in range(RING):
                sp.dma_start(raw[:, u], A["weights"][u]).then_inc(raw_landed[u], 16)
            full = NU // RING
            with sp.Fori(1, full) as k:
                for u in range(RING):
                    sp.wait_ge(sem["lo_ready"], RING * k + (u + 1 - RING))
                    sp.dma_start(raw[:, u:u + 1], A["weights"][bass.ds(RING * k + u, 1)]
                                 .rearrange("o p n -> p o n")).then_inc(raw_landed[u], 16)
            for g in range(RING * full, NU):
                sp.wait_ge(sem["lo_ready"], g + 1 - RING)
                sp.dma_start(raw[:, g % RING], A["weights"][g]).then_inc(raw_landed[g % RING], 16)
            out_v = A["out"].rearrange("(c p) t -> p c t", p=P)
            for m in range(PAIRS):
                sp.wait_ge(sem["h_ready"], hbase(R_FFN3) + m + 1)
                sp.dma_start(out_v[:, 2 * m:2 * m + 2, :], h[:, 2 * m:2 * m + 2, :]).then_inc(sem["out_stored"], 16)
            sp.wait_ge(sem["out_stored"], 16 * PAIRS)

        @block.tensor
        def _(pe):
            def exact(out, a, b, start, stop):
                (a_hi, a_lo), (b_hi, b_lo) = a, b
                nc.tensor.matmul(out, a_hi, b_hi, start=start, stop=False, skip_group_check=True)
                nc.tensor.matmul(out, a_hi, b_lo, start=False, stop=False, skip_group_check=True)
                return nc.tensor.matmul(out, a_lo, b_hi, start=False, stop=stop, skip_group_check=True)

            def slot(g0):
                s = g0 % RING
                return w_hi[:, s], w_lo[:, s]

            def wide(ws, c, m):
                return tuple(w[:, c * 256 + m * P:c * 256 + (m + 1) * P] for w in ws)

            RES = {"sc_out": R_SC, "wo": R_WO, "glu": R_GLU, "nwo": R_NWO}
            PB = [XB, DB[0], DB[1], DB[2]]

            def up_unit(g0, k, x, bank, arrive=None, mid=None):
                pe.wait_ge(sem["lo_ready"], g0 + 1 + RING * k)
                ws = slot(g0)
                for m in range(2):
                    for c in range(KC):
                        if arrive is not None and m == 0 and c % 2 == 0:
                            pe.wait_ge(arrive[0], arrive[1] + arrive[2] * (c // 2 + 1))
                        last = exact(bank[:, m * SEQ:(m + 1) * SEQ], wide(ws, c, m),
                                     (x_hi[x][:, c], x_lo[x][:, c]), c == 0, c == KC - 1)
                    if m == 0 and mid is not None:
                        mid()
                last.then_inc(sem["unit_done"], 1)

            def token_unit(g0, k, x, bank, mid=None):
                pe.wait_ge(sem["lo_ready"], g0 + 1 + RING * k)
                wh, wl = slot(g0)
                for t in range(TT):
                    for c in range(KC):
                        last = exact(bank[:, t * 256:(t + 1) * 256],
                                     tuple(xx[x][:, c, t * P:(t + 1) * P] for xx in (x_hi, x_lo)),
                                     (wh[:, c * 256:(c + 1) * 256], wl[:, c * 256:(c + 1) * 256]),
                                     c == 0, c == KC - 1)
                    if t == 0 and mid is not None:
                        mid()
                last.then_inc(sem["unit_done"], 1)

            def down_unit(g0, k, hid_count, tell=False):
                pe.wait_ge(sem["lo_ready"], g0 + 1 + RING * k)
                pe.wait_ge(sem["hid_lo_ready"], hid_count)
                wh, wl = slot(g0)
                for m in range(KC):
                    for c in range(2):
                        cols = slice(c * D + m * P, c * D + (m + 1) * P)
                        last = exact(DB[m // 2][:, (m % 2) * SEQ:(m % 2 + 1) * SEQ], (wh[:, cols], wl[:, cols]),
                                     (hid_hi[:, c], hid_lo[:, c]), False, c == 1)
                    if tell and m % 2 and m < KC - 1:
                        last.then_inc(sem["acc_done"], 1)
                last.then_inc(sem["unit_done"], 1)

            def clear_sums():
                for b in range(4):
                    nc.tensor.matmul(DB[b], zero[:, 0:P], zero[:], start=True, stop=False, skip_group_check=True)

            def norm_sum(n):
                pe.wait_ge(sem["sq_used"], 3 * (n + 1))
                pe.wait_ge(sem["rs_ready"], n)
                for t in range(TT):
                    for q in range(2):
                        last = nc.tensor.matmul(MB[:, t:t + 1], ssum[:, q, t * P:(t + 1) * P], ones[:, 0:1],
                                                start=q == 0, stop=q == 1, skip_group_check=True)
                last.then_inc(sem["sum_ready"], 1)

            def norm_bcast(n):
                pe.wait_ge(sem["diag_ready"], n + 1)
                nc.tensor.matmul(MB[:, SEQ:2 * SEQ], ones[:], diag[:].rearrange("p t q -> p (t q)"),
                                 start=True, stop=True, skip_group_check=True).then_inc(sem["bcast_ready"], 1)

            def residual_units(stage, x, arrive, mid=None):
                for m in range(PAIRS):
                    if m >= 2:
                        pe.wait_ge(sem["h_ready"], hbase(RES[stage]) + m - 1)
                    up_unit(BASE[stage] + m, 0, x, U[m % 2], arrive if m == 0 else None, mid if m == 0 else None)
                pe.wait_ge(sem["h_ready"], hbase(RES[stage]) + PAIRS - 1)

            def mlp(l, n):
                name = f"mlp{l}"
                g, hb, x = BASE[name], HID_BASE[name], XBUF[n]
                up_unit(g, 0, x, U[0], (sem["xl_ready"], XBASE[n], 1), lambda: norm_sum(n))
                norm_bcast(n)
                clear_sums()
                with pe.Fori(0, (MLP_PAIRS - 1) // RING) as k:
                    for t in range(RING):
                        pe.wait_ge(sem["relu_ready"], MLP_PAIRS * l + RING * k + t + 1)
                        up_unit(g + 1 + 2 * t, 2 * k, x, U[0])
                        down_unit(g + 2 + 2 * t, 2 * k, hb + RING * k + t + 1)
                down_unit(g + 2 * MLP_PAIRS - 1, 0, hb + MLP_PAIRS, tell=True)

            def ffn(f, n, normed=True, r=None):
                name = f"ffn{f}"
                r = n if r is None else r
                g, hb, x = BASE[name], HID_BASE[name], XBUF[r]
                up_unit(g, 0, x, U[0], (sem["xl_ready"], XBASE[r], 1), (lambda: norm_sum(n)) if normed else None)
                if normed:
                    norm_bcast(n)
                up_unit(g + 1, 0, x, U[1])
                clear_sums()
                with pe.Fori(0, FFN_PAIRS - 1) as k:
                    pe.wait_ge(sem["a_scaled"], FFN_PAIRS * f + k + 1)
                    up_unit(g + 2, k, x, U[0])
                    pe.wait_ge(sem["b_gated"], FFN_PAIRS * f + k + 1)
                    up_unit(g + 3, k, x, U[1])
                    down_unit(g + 4, k, hb + k + 1)
                down_unit(g + 3 * FFN_PAIRS - 1, 0, hb + FFN_PAIRS, tell=True)

            def ple(l, n):
                name = f"ple{l}"
                g = BASE[name]
                pe.wait_ge(sem["lo_ready"], g + 1)
                pe.wait_ge(sem["p_lo_ready"], l + 1)
                wh, wl = slot(g)
                for m in range(PAIRS):
                    if m:
                        pe.wait_ge(sem["h_ready"], hbase(n) + m)
                    for q in range(2):
                        for c in range(2):
                            cols = slice(c * D + (2 * m + q) * P, c * D + (2 * m + q + 1) * P)
                            last = exact(PB[m][:, q * SEQ:(q + 1) * SEQ], (wh[:, cols], wl[:, cols]),
                                         (p_hi[:, c], p_lo[:, c]), c == 0, c == 1)
                last.then_inc(sem["unit_done"], 1)
                for m in range(PAIRS):
                    if m >= 2:
                        pe.wait_ge(sem["gate_scaled"], PAIRS * l + m - 1)
                    if m == 1:
                        norm_bcast(n)
                    up_unit(g + 1 + m, 0, XBUF[n], U[m % 2], (sem["xl_ready"], XBASE[n], 1) if m == 0 else None,
                            (lambda: norm_sum(n)) if m == 0 else None)
                pe.wait_ge(sem["gate_scaled"], PAIRS * (l + 1) - 1)

            pe.wait_ge(sem["fill_done"], 4)
            pe.wait_ge(sem["con_landed"], 16)
            n = R_IN

            def conv_triple(g0, k, j, first):
                if not first:
                    pe.wait_ge(sem["c_copied"], j)
                up_unit(g0, k, 0, U[0], (sem["xl_ready"], XBASE[n], 1) if first else None,
                        (lambda: norm_sum(n)) if first else None)
                if first:
                    norm_bcast(n)
                else:
                    pe.wait_ge(sem["v_raw"], j)
                up_unit(g0 + 1, k, 0, U[1])
                if not first:
                    pe.wait_ge(sem["b_scaled"], j)
                up_unit(g0 + 2, k, 0, XB)

            conv_triple(0, 0, 0, True)
            with pe.Fori(0, PAIRS - 1) as k:
                conv_triple(3, k, k + 1, False)
            pe.wait_ge(sem["c_copied"], PAIRS)
            residual_units("sc_out", 1, (sem["y_lo"], 0, 1))

            pe.wait_ge(sem["bb_ready"], 4)
            pe.wait_ge(sem["h_ready"], hbase(R_SC) + 1)
            for c in range(KC):
                for ri in range(2):
                    n_ = 2 * c + ri
                    last = nc.tensor.transpose(DB[n_ // 4][:, (n_ % 4) * P:(n_ % 4 + 1) * P],
                                               bb[:, ri, 4 * c:4 * c + 4, :].rearrange("p j q -> p (j q)"), ident)
            last.then_inc(sem["bt_done"], 1)
            pe.wait_ge(sem["bt_ready"], 4)

            mlp(0, R_SC)
            ple(0, R_MLP0)

            n = R_PLE0
            g = BASE["qkv"]
            TBK = [DB[3], MB]

            def turn(hd, side, b):
                if b == 0:
                    pe.wait_ge(sem["exp_done"], 2 * (hd + 1))
                pe.wait_ge(sem["pt_copied"], 3 * hd + b - 1 if side or b else 3 * hd)
                for gr in range(NG):
                    part = lg0[:, gr, :] if b == 0 else lg1[:, gr, (b - 1) * P:b * P]
                    last = nc.tensor.transpose(TBK[(NG * side + b) % 2][:, gr * P:(gr + 1) * P], part, ident)
                last.then_inc(sem["pt_done"], 1)

            def values(hd, side):
                pe.wait_ge(sem["pt_copied"], 3 * (hd + 1))
                pe.wait_ge(sem["o_scaled"], 2 * hd)
                if side:
                    pe.wait_ge(sem["o_lo"], hd)
                else:
                    pe.wait_ge(sem["masked"], 2 * (hd + 2))
                dims = slice(side * DH, (side + 1) * DH)
                for gr in range(NG):
                    nc.tensor.matmul(DB[2][:, SEQ:SEQ + DH], pt[:, 0, gr * P:(gr + 1) * P], vv[:, 0, gr, dims],
                                     start=gr == 0, stop=gr == NG - 1, skip_group_check=True)
                for b in range(2):
                    for gr in range(NG):
                        last = nc.tensor.matmul(DB[2][:, SEQ + DH:SEQ + 2 * DH], pt[:, 1 + b, gr * P:(gr + 1) * P],
                                                vv[:, b, gr, dims], start=b == 0 and gr == 0,
                                                stop=b == 1 and gr == NG - 1, skip_group_check=True)
                last.then_inc(sem["pv_done"], 1)

            def turn_out(hd):
                pe.wait_ge(sem["o_scaled"], 2 * (hd + 1))
                for t in range(TT):
                    last = nc.tensor.transpose(DB[2][:, t * P:(t + 1) * P], ot[:, t, :], ident)
                last.then_inc(sem["ot_done"], 1)

            def scores_of(i, side):
                pe.wait_ge(sem["qk_ready"], 6 * i + 3 * side + 3)
                hd = 2 * i + side
                pe.wait_ge(sem["masked"], 2 * hd)
                if side == 0:
                    pe.wait_ge(sem["o_lo"], hd)
                for gr in range(NG):
                    nc.tensor.matmul(DB[0][:, gr * P:(gr + 1) * P], qk[:, side, gr, 0, 0:P], qk[:, side, gr, 1, 0:P],
                                     start=True, stop=True, skip_group_check=True)
                for gr in range(NG):
                    bank = DB[1 + gr // 2][:, (gr % 2) * SEQ:(gr % 2 + 1) * SEQ]
                    last = nc.tensor.matmul(bank, qk[:, side, gr, 0, P:SEQ], qk[:, side, gr, 1, :],
                                            start=True, stop=True, skip_group_check=True)
                last.then_inc(sem["s_done"], 1)

            def attend(i, u):
                a, b = 2 * i, 2 * i + 1
                if u == 0:
                    scores_of(i, 1)
                    turn(a, 0, 0)
                    turn(a, 0, 1)
                elif u == 1:
                    turn(a, 0, 2)
                elif u == 2:
                    values(a, 0)
                    turn(b, 1, 0)
                elif u == 3:
                    turn(b, 1, 1)
                    turn_out(a)
                elif u == 4:
                    turn(b, 1, 2)
                elif u == 5:
                    values(b, 1)
                elif u == 6:
                    turn_out(b)

            def qkv_units(k, i, before, first):
                for u in range(9):
                    bank = U3[u % 3]
                    if not first:
                        if u < 3:
                            pe.wait_ge(sem["v_copied"], 3 * i + u - 2)
                        else:
                            pe.wait_ge(sem["swapped"], 6 * i + u - 2)
                    elif u >= 3:
                        pe.wait_ge(sem["swapped"], u - 2)
                    if u < 6:
                        up_unit(g + u, k, XBUF[n], bank, (sem["xl_ready"], XBASE[n], 1) if first and u == 0 else None,
                                (lambda: norm_sum(n)) if first and u == 0 else None)
                        if first and u == 0:
                            norm_bcast(n)
                    else:
                        token_unit(g + u, k, XBUF[n], bank)
                    if before is not None:
                        attend(before, u)

            qkv_units(0, 0, None, True)
            with pe.Fori(0, HEAD_PAIRS - 1) as k:
                scores_of(k, 0)
                qkv_units(3 * k + 3, k + 1, k, False)
            scores_of(HEAD_PAIRS - 1, 0)
            pe.wait_ge(sem["v_copied"], 3 * HEAD_PAIRS)
            for u in range(7):
                attend(HEAD_PAIRS - 1, u)
            residual_units("wo", 1, (sem["o_lo"], 0, 2))

            mlp(1, R_WO)
            ple(1, R_MLP1)

            norm_sum(R_PLE1)
            norm_bcast(R_PLE1)
            ffn(0, R_FIN)

            norm_sum(R_FFN0)
            norm_bcast(R_FFN0)

            def drive(j):
                c, q = j // 4, 32 * (j % 4)
                pe.wait_ge(sem["u5_ready"], c + 1)
                if j >= 2:
                    pe.wait_ge(sem["drive"], j - 1)
                for ri in range(2):
                    last = nc.tensor.matmul(U[j % 2][:, ri * SEQ:(ri + 1) * SEQ], bt[q:q + 32, c, ri, :],
                                            u5[q:q + 32, c, :], start=True, stop=True, skip_group_check=True)
                last.then_inc(sem["bu_done"], 1)

            def outputs(j):
                c, q = j // 4, 32 * (j % 4)
                pe.wait_ge(sem["turned_back"], 2 * (j + 1))
                if c >= 4 and j % 4 == 0:
                    pe.wait_ge(sem["y_in"], c - 3)
                out = DB[c % 4][q:q + 32, 0:SEQ]
                nc.tensor.matmul(out, ct[:, 0, j, :], n1[:, 0], start=True, stop=False, skip_group_check=True)
                nc.tensor.matmul(out, ct[:, 1, j, :], n2[:, 0], start=False, stop=False, skip_group_check=True)
                nc.tensor.matmul(out, ct[:, 2, j, :], n1[:, 1], start=False, stop=False, skip_group_check=True)
                nc.tensor.matmul(out, ct[:, 2, j, :], n2[:, 1], start=False, stop=True,
                                 skip_group_check=True).then_inc(sem["y_done"], 1)

            drive(0)
            for j in range(ST):
                if j + 1 < ST:
                    drive(j + 1)
                outputs(j)
            residual_units("glu", 1, (sem["g_lo"], 0, 2))
            ffn(1, R_GLU)

            pe.wait_ge(sem["bias_in_landed"], 48)
            pe.wait_ge(sem["rel_ready"], 1)
            for i in range(TT * NCMP):
                last = nc.tensor.matmul(MB[:, i * NH:(i + 1) * NH], ohc[:, i, :], rel[:], start=True, stop=True,
                                        skip_group_check=True)
            last.then_inc(sem["cb_done"], 1)
            pe.wait_ge(sem["rs_ready"], R_GLU + 1)
            nc.tensor.matmul(XB[0:NH, 0:NDIST], rel[:], oh[:], start=True, stop=True,
                             skip_group_check=True).then_inc(sem["bv_done"], 1)

            n, g, x = R_FFN1, BASE["kv"], XBUF[R_FFN1]

            def head_sum(count, width):
                pe.wait_ge(sem["k_sq"], count)
                nc.tensor.matmul(XB[:, 0:width], cst("half", P), tb[:].rearrange("p c t -> p (c t)")[:, 0:width],
                                 start=True, stop=True, skip_group_check=True).then_inc(sem["k_sum"], 1)

            def compress(kind):
                pe.wait_ge(sem["blk_ready"], kind + 1)
                pe.wait_ge(sem["cmpw_landed"], 16 * (kind + 3))
                for half in range(2):
                    rows = slice(half * HD, (half + 1) * HD)
                    for l in range(CL):
                        last = nc.tensor.matmul([MB, U[0]][half][:, 0:2 * NCMP], w1[rows, l, :],
                                                blk[rows, l, :, :].rearrange("p c n -> p (c n)"),
                                                start=l == 0, stop=l == CL - 1, skip_group_check=True)
                    last.then_inc(sem["hid_done"], 1)

            pe.wait_ge(sem["cb_ready"], 1)
            up_unit(g, 0, x, U[0], (sem["xl_ready"], XBASE[n], 1), lambda: norm_sum(n))
            norm_bcast(n)
            up_unit(g + 1, 0, x, U[1])
            pe.wait_ge(sem["src_ready"], 1)
            up_unit(g + 2, 0, x, U[0])
            pe.wait_ge(sem["src_ready"], 2)
            token_unit(g + 3, 0, x, U[1])
            pe.wait_ge(sem["bv_copied"], 1)
            head_sum(1, 512)
            pe.wait_ge(sem["k_scaled"], 1)
            up_unit(g + 4, 0, x, U[0])
            pe.wait_ge(sem["vs_ready"], 1)
            token_unit(g + 5, 0, x, U[1])
            head_sum(2, 512)
            compress(0)
            pe.wait_ge(sem["hg_ready"], 1)
            for half in range(2):
                rows = slice(half * HD, (half + 1) * HD)
                last = nc.tensor.matmul(MB[rows, 128:128 + 2 * NCMP], w2[:, 0, :], hg[:, half, :],
                                        start=True, stop=True, skip_group_check=True)
            last.then_inc(sem["w2_done"], 1)
            head_sum(3, 2 * NCMP)
            compress(1)
            pe.wait_ge(sem["hg_ready"], 2)
            for kh in range(KVH):
                a, half = kh // 2, kh % 2
                last = nc.tensor.matmul(MB[0:NCMP, 256 + kh * HD:256 + (kh + 1) * HD],
                                        hg[:, half, a * NCMP:(a + 1) * NCMP], w2[:, 1, :],
                                        start=True, stop=True, skip_group_check=True)
            last.then_inc(sem["w2_done"], 1)
            ffn(2, R_FFN1, normed=False, r="kv")

            n, g, x = R_FFN2, BASE["qg"], XBUF[R_FFN2]
            for u in range(4):
                if u >= 2:
                    pe.wait_ge(sem["k_scaled"], u + 2)

                def between(u=u):
                    if u == 0:
                        norm_sum(n)
                    else:
                        head_sum(3 + u, 512)
                up_unit(g + u, 0, x, U[u % 2], (sem["xl_ready"], XBASE[n], 1) if u == 0 else None, between)
                if u == 0:
                    norm_bcast(n)
            pe.wait_ge(sem["wg_lo_ready"], 1)
            pe.wait_ge(sem["k_scaled"], 6)
            for t in range(TT):
                for c in range(KC):
                    last = exact(U[0][:, t * 64:t * 64 + 3 * NH],
                                 tuple(xx[x][:, c, t * P:(t + 1) * P] for xx in (x_hi, x_lo)),
                                 (wg_hi[:, c, :], wg_lo[:, c, :]), c == 0, c == KC - 1)
            last.then_inc(sem["gate_done"], 1)
            head_sum(7, 512)

            pe.wait_ge(sem["gate_all"], 1)

            def n_scores(hd, a, l):
                if l >= 2:
                    pe.wait_ge(sem["n_log"], hd - 1)
                b, rows = l % 2, slice((l % 2) * HD, (l % 2 + 1) * HD)
                q = qst[rows, l // 2]
                for br in range(2):
                    bank = DB[2 * br + b]
                    nc.tensor.matmul(bank[:, 0:P], q[:, 0:P], ks[rows, br, a, 0:P], start=True, stop=True,
                                     skip_group_check=True)
                    nc.tensor.matmul(bank[:, P:P + SEQ], q[:, P:SEQ], ks[rows, br, a, :], start=True, stop=True,
                                     skip_group_check=True)
                for t in range(TT):
                    last = nc.tensor.matmul(DB[b][:, 3 * P + t * NCMP:3 * P + (t + 1) * NCMP],
                                            q[:, t * P:(t + 1) * P], kcmp[rows, a, :], start=True, stop=True,
                                            skip_group_check=True)
                last.then_inc(sem["n_s"], 1)

            def n_turn(hd, l, chunks):
                b = l % 2
                pe.wait_ge(sem["n_lo"], chunks)
                pe.wait_ge(sem["n_exp"], hd + 1)
                pe.wait_ge(sem["n_tv"], hd)
                pe.wait_ge(sem["n_ta"], hd)
                for br in range(2):
                    for j in range(3):
                        last = nc.tensor.transpose(U[br][:, j * P:(j + 1) * P], lg[:, b, br, j * P:(j + 1) * P],
                                                   ident)
                for t in range(TT):
                    last = nc.tensor.transpose(MB[0:NCMP, t * P:(t + 1) * P], lgc[:, b, t, :], ident)
                last.then_inc(sem["n_t"], 1)

            def n_values(hd, a, l):
                b, kh = l % 2, 2 * a + l % 2
                pe.wait_ge(sem["n_tv"], hd + 1)
                pe.wait_ge(sem["n_ta"], hd + 1)
                pe.wait_ge(sem["n_part"], 3 * hd)
                dims = slice(kh * HD, (kh + 1) * HD)

                def out(br, t):
                    at = (br * TT + t) * HD
                    return XB[:, at:at + HD]
                for t in range(TT):
                    nc.tensor.matmul(out(0, t), ptc[:, b, t * P:(t + 1) * P], vcmp[:, kh, :], start=True, stop=True,
                                     skip_group_check=True)
                for br in range(2):
                    pb_ = ptn[:, b, br]
                    nc.tensor.matmul(out(1 + br, 0), pb_[:, 0:P], vs[:, br, 0, dims], start=True, stop=True,
                                     skip_group_check=True)
                    nc.tensor.matmul(out(1 + br, 1), pb_[:, P:2 * P], vs[:, br, 0, dims], start=True, stop=False,
                                     skip_group_check=True)
                    last = nc.tensor.matmul(out(1 + br, 1), pb_[:, 2 * P:3 * P], vs[:, br, 1, dims], start=False,
                                            stop=True, skip_group_check=True)
                last.then_inc(sem["n_pv"], 1)

            def n_turn_out(ch, cc):
                pe.wait_ge(sem["n_part"], 6 * ch + 6)
                pe.wait_ge(sem["n_lo"], ch)
                for t in range(TT):
                    last = nc.tensor.transpose(MB[:, SEQ + t * P:SEQ + (t + 1) * P],
                                               oc[:, cc, t].rearrange("p e d -> p (e d)"), ident)
                last.then_inc(sem["n_ot"], 1)

            for a in range(KVH // 2):
                with pe.Fori(0, 2) as k:
                    h0 = 4 * k + 8 * a
                    pe.wait_ge(sem["q_staged"], 2 * k + 4 * a + 2)
                    pe.wait_ge(sem["n_log"], h0)
                    for l in range(5):
                        if l < 4:
                            n_scores(h0 + l, a, l)
                        if l >= 1:
                            n_turn(h0 + l - 1, l - 1, 2 * k + 4 * a + (l - 1) // 2)
                            n_values(h0 + l - 1, a, l - 1)
                        if l in (2, 4):
                            n_turn_out(2 * k + 4 * a + l // 2 - 1, l // 2 - 1)
            residual_units("nwo", 0, (sem["n_lo"], 0, 2))
            ffn(3, R_NWO)

        @block.scalar
        def _(act):
            copy = lambda out, in_, **kw: nc.scalar.activation(out, in_, ACT.Copy, **kw)

            def done(g0, k=0):
                act.wait_ge(sem["unit_done"], g0 + 1 + RING * k)

            def split(g0, k=0):
                g = g0 + RING
                if isinstance(k, int) and g + RING * k >= NU:
                    return
                act.wait_ge(sem["unit_done"], g0 + 1 + RING * k)
                act.wait_ge(raw_landed[g % RING], 16 * (g // RING + 1) + 16 * k)
                copy(w_hi[:, g % RING], raw[:, g % RING]).then_inc(sem["hi_ready"], 1)

            def x_high(r, m, waits=True):
                for q in range(2):
                    c = 2 * m + q
                    last = copy(x_hi[XBUF[r]][:, c], h[:, c], scale=col(GAIN[r], c))
                last.then_inc(sem["xh_ready"], 1)

            def squares(r, m):
                if r > 0 or m >= 2:
                    act.wait_ge(sem["sq_used"], 3 * r + (m - 1 if m < 2 else 1))
                nc.scalar.activation(sq[:, m % 2], h[:, 2 * m:2 * m + 2], ACT.Square).then_inc(sem["sq_ready"], 1)

            def residual(r, m, x=True):
                act.wait_ge(sem["h_ready"], hbase(r) + m + 1)
                if x:
                    x_high(r, m)
                squares(r, m)

            def norm(n):
                act.wait_ge(sem["bcast_ready"], n + 1)
                for q in range(2):
                    last = copy(rs[:, q], MB[:, SEQ:2 * SEQ])
                last.then_inc(sem["rs_ready"], 1)

            def residual_stage(stage, r):
                for m in range(PAIRS):
                    done(BASE[stage] + m)
                    residual(r, m)
                    split(BASE[stage] + m)

            def mlp(l, r):
                g, first = BASE[f"mlp{l}"], MLP_PAIRS * l

                def square(i):
                    act.wait_ge(sem["relu_ready"], first + i + 1)
                    nc.scalar.activation(tb[:], ta[:], ACT.Square).then_inc(sem["act_ready"], 1)

                def high(i):
                    act.wait_ge(sem["act_ready"], first + i + 1)
                    copy(hid_hi[:], tb[:]).then_inc(sem["hid_hi_ready"], 1)

                act.wait_ge(sem["p_landed"], 16 * (l + 1))
                if l:
                    act.wait_ge(sem["unit_done"], BASE["ple0"] + 1)
                copy(p_hi[:], p_in[:]).then_inc(sem["p_hi_ready"], 1)
                norm(r)
                square(0)
                high(0)
                split(g)
                with act.Fori(0, (MLP_PAIRS - 1) // RING) as k:
                    for t in range(RING):
                        i = RING * k + t + 1
                        square(i)
                        split(g + 1 + 2 * t, 2 * k)
                        done(g + 2 + 2 * t, 2 * k)
                        high(i)
                        split(g + 2 + 2 * t, 2 * k)
                last = g + 2 * MLP_PAIRS - 1
                for m in range(PAIRS):
                    residual(R_MLP0 if l == 0 else R_MLP1, m)
                split(last)

            def ffn(f, r, n, x=True):
                g, first = BASE[f"ffn{f}"], FFN_PAIRS * f

                def silu(i):
                    act.wait_ge(sem["a_scaled"], first + i + 1)
                    nc.scalar.activation(tb[:], ta[:], ACT.Silu).then_inc(sem["silu_ready"], 1)

                def high(i):
                    act.wait_ge(sem["prod_ready"], first + i + 1)
                    copy(hid_hi[:], tc[:]).then_inc(sem["hid_hi_ready"], 1)

                if n is not None:
                    norm(n)
                silu(0)
                split(g)
                high(0)
                split(g + 1)

                def pair(k):
                    silu(k + 1)
                    split(g + 2, k)
                    split(g + 3, k)
                    done(g + 4, k)
                    high(k + 1)
                    split(g + 4, k)

                with act.Fori(0, FFN_PAIRS - 1 - (f == 3)) as k:
                    pair(k)
                if f == 3:
                    pair(FFN_PAIRS - 2)
                if r != R_FFN3:
                    for m in range(PAIRS):
                        residual(r, m, x)
                split(g + 3 * FFN_PAIRS - 1)

            def ple(l, n, r, x=True):
                g = BASE[f"ple{l}"]
                split(g)
                norm(n)
                for m in range(PAIRS):
                    act.wait_ge(sem["gate_scaled"], PAIRS * l + m + 1)
                    nc.scalar.activation(tb[:], ta[:], ACT.Sigmoid).then_inc(sem["gate_ready"], 1)
                    residual(r, m, x)
                    split(g + 1 + m)

            h_v = A["x"].rearrange("(c p) t -> p c t", p=P)
            act.dma_start(vec[:], A["vec"]).then_inc(sem["misc_landed"], 16)
            act.dma_start(h[:], h_v).then_inc(sem["h_landed"], 16)
            act.dma_start(p_in[:], A["p"][0].rearrange("(c p) t -> p c t", p=P)).then_inc(sem["p_landed"], 16)
            act.dma_start(s5b[:], A["s5b"]).then_inc(sem["misc_landed"], 16)
            act.wait_ge(sem["fill_done"], 7)
            for ri in range(2):
                for g2 in range(2):
                    rows = slice(g2 * S5_STATE, (g2 + 1) * S5_STATE)
                    act.dma_start(ct[rows, 2 * ri, :, g2 * S5_CH:(g2 + 1) * S5_CH],
                                  A["s5c"][rows, ri]).then_inc(sem["misc_landed"], 16)
            act.wait_ge(sem["misc_landed"], 96)
            act.wait_ge(sem["h_landed"], 16)
            for m in range(2):
                x_high(R_IN, m)
                squares(R_IN, m)
            for g in range(1):
                act.wait_ge(raw_landed[g], 16)
                copy(w_hi[:, g], raw[:, g]).then_inc(sem["hi_ready"], 1)
            for m in range(2, PAIRS):
                x_high(R_IN, m)
                squares(R_IN, m)
            for g in range(1, RING):
                act.wait_ge(raw_landed[g], 16)
                copy(w_hi[:, g], raw[:, g]).then_inc(sem["hi_ready"], 1)

            def conv_triple(g0, k, j):
                done(g0, k)
                copy(tb[:], two(U[0])).then_inc(sem["c_copied"], 1)
                split(g0, k)
                split(g0 + 1, k)
                act.wait_ge(sem["y_ready"], j + 1)
                copy(x_hi[1][:, bass.ds(2 * j, 2), :], tc[:]).then_inc(sem["y_hi"], 1)
                split(g0 + 2, k)

            norm(R_IN)
            conv_triple(0, 0, 0)
            with act.Fori(0, PAIRS - 1) as k:
                conv_triple(3, k, k + 1)
            residual_stage("sc_out", R_SC)

            act_fn = nc.scalar.activation
            act_fn(sm[:, 0], col("ldt", 0, ST), ACT.Exp).then_inc(sem["sm_act"], 1)
            act.wait_ge(sem["sm_dve"], S5_R)
            act_fn(sm[:, 8], sm[:, 5], ACT.Abs).then_inc(sem["sm_act"], 1)
            act_fn(sm[:, 7], sm[:, 5], ACT.Sin).then_inc(sem["sm_act"], 1)
            act.wait_ge(sem["sm_act"], 3)
            act_fn(sm[:, 6], sm[:, 8], ACT.Sin, scale=-1.0, bias=halfpi[:]).then_inc(sem["sm_act"], 1)
            copy(ct[:, 1], ct[:, 0], scale=-1.0).then_inc(sem["ct_ready"], 1)
            copy(ct[:, 2], ct[:, 2], scale=-1.0).then_inc(sem["ct_ready"], 1)
            act.wait_ge(sem["bt_done"], 1)
            for b in range(4):
                copy(bt[:, 2 * b:2 * b + 2].rearrange("p c r s -> p (c r s)"), DB[b]).then_inc(sem["bt_ready"], 1)

            mlp(0, R_SC)
            act.wait_ge(sem["e_stored"], 16 * (ST // EB))
            act.dma_start(posi[:], A["positions"].partition_broadcast(P)).then_inc(sem["pos_landed"], 16)
            ple(0, R_MLP0, R_PLE0)
            act.wait_ge(sem["p_lo_ready"], 1)
            act.dma_start(p_in[:], A["p"][1].rearrange("(c p) t -> p c t", p=P)).then_inc(sem["p_landed"], 16)

            act.wait_ge(sem["rope_step"], 6)
            act_fn(ang[:, 0], ang[:, 1], ACT.Abs).then_inc(sem["sin_ready"], 1)
            act_fn(rope_s[:], ang[:, 1], ACT.Sin).then_inc(sem["sin_ready"], 1)
            act.wait_ge(sem["sin_ready"], 2)
            act_fn(rope_c[:], ang[:, 0], ACT.Sin, scale=-1.0, bias=halfpi[:]).then_inc(sem["sin_ready"], 1)

            g = BASE["qkv"]

            def exps(hd):
                act.wait_ge(sem["bias_ready"], hd + 1)
                act_fn(lg0[:], lg0[:], ACT.Exp, scale=SCALE, bias=nbias[:, 0:1],
                       accum_out=den[:, 0:1]).then_inc(sem["exp_done"], 1)
                act_fn(lg1[:], lg1[:], ACT.Exp, scale=SCALE, bias=nbias[:, 1:2],
                       accum_out=den[:, 1:2]).then_inc(sem["exp_done"], 1)

            TBK = [DB[3], MB]

            def pt_copy(hd, side, b):
                act.wait_ge(sem["pt_done"], 3 * hd + b + 1)
                if b == 0:
                    act.wait_ge(sem["pv_done"], hd)
                copy(pt[:, b], TBK[(NG * side + b) % 2][:, 0:NG * P]).then_inc(sem["pt_copied"], 1)

            def scale_out(hd):
                act.wait_ge(sem["pv_done"], hd + 1)
                act.wait_ge(sem["rden_ready"], hd + 1)
                act.wait_ge(sem["ot_done"], hd)
                for t in range(TT):
                    copy(ot[:, t], DB[2][:, SEQ + t * DH:SEQ + (t + 1) * DH],
                         scale=rden[:, t:t + 1]).then_inc(sem["o_scaled"], 1)

            def out_high(hd):
                act.wait_ge(sem["ot_done"], hd + 1)
                copy(x_hi[1][:, bass.ds(hd, 1), :].rearrange("p o t -> p (o t)"),
                     DB[2][:, 0:SEQ]).then_inc(sem["o_hi"], 1)

            def value_copy(g0, k, i, gr):
                done(g0, k)
                if gr == 0:
                    act.wait_ge(sem["pv_done"], 2 * i)
                bank = U3[(6 + gr) % 3]
                for t in range(TT):
                    last = copy(vv[:, t, gr], bank[:, t * SEQ:(t + 1) * SEQ], scale=rs_tok[:, t:t + 1])
                last.then_inc(sem["v_copied"], 1)

            def attend(i, u):
                a, b = 2 * i, 2 * i + 1
                if u == 0:
                    pt_copy(a, 0, 0)
                    pt_copy(a, 0, 1)
                elif u == 1:
                    pt_copy(a, 0, 2)
                    exps(b)
                elif u == 2:
                    scale_out(a)
                    pt_copy(b, 1, 0)
                elif u == 3:
                    pt_copy(b, 1, 1)
                    out_high(a)
                elif u == 4:
                    pt_copy(b, 1, 2)
                elif u == 5:
                    scale_out(b)
                elif u == 6:
                    out_high(b)

            def qkv_units(k, i, before):
                for u in range(9):
                    if u >= 6:
                        value_copy(g + u, k, i, u - 6)
                    split(g + u, k)
                    if before is not None:
                        attend(before, u)

            norm(R_PLE0)
            qkv_units(0, 0, None)
            with act.Fori(0, HEAD_PAIRS - 1) as k:
                exps(2 * k)
                qkv_units(3 * k + 3, k + 1, k)
            exps(2 * (HEAD_PAIRS - 1))
            for u in range(7):
                attend(HEAD_PAIRS - 1, u)
            residual_stage("wo", R_WO)

            mlp(1, R_WO)
            ple(1, R_MLP1, R_PLE1, x=False)
            norm(R_PLE1)
            for m in range(PAIRS):
                residual(R_FIN, m)
            ffn(0, R_FFN0, R_FIN, x=False)

            def load_rotation(b):
                if b >= 2:
                    act.wait_ge(sem["turned_back"], 2 * EB * (b - 1))
                act.dma_start(e_ring[:, b % 2].rearrange("p j r t -> p (j r t)"),
                              A["e_table"][b]).then_inc([sem["e_landed0"], sem["e_landed1"]][b % 2], 16)

            load_rotation(0)
            load_rotation(1)
            norm(R_FFN0)

            def gelu(c):
                act.wait_ge(sem["y_in"], c + 1)
                act_fn(y5[:, c], ta[:, 0], ACT.Gelu_apprx_tanh).then_inc(sem["gelu_done"], 1)
                act.wait_ge(sem["gelu_done"], c + 1)
                copy(x_hi[1][:, c], y5[:, c]).then_inc(sem["g_hi"], 1)

            for j in range(ST):
                if j % EB == EB - 1 and j // EB + 2 < ST // EB:
                    load_rotation(j // EB + 2)
                if j % 4 == 1 and j >= 5:
                    gelu(j // 4 - 1)
            gelu(KC - 1)
            for m in range(PAIRS):
                done(BASE["glu"] + m)
                act_fn(tb[:], two(U[m % 2]), ACT.Sigmoid).then_inc(sem["gate_ready"], 1)
                residual(R_GLU, m)
                split(BASE["glu"] + m)

            act.dma_start(ohc[:], A["onehot_cmp"]).then_inc(sem["bias_in_landed"], 16)
            act.dma_start(oh[:], A["onehot"]).then_inc(sem["bias_in_landed"], 16)
            act.dma_start(rel[0:NBUCKET], A["rel_bias"]).then_inc(sem["bias_in_landed"], 16)
            ffn(1, R_FFN1, R_GLU)

            g = BASE["kv"]
            act.wait_ge(sem["bv_done"], 1)
            copy(bv[:], XB[0:NH, 0:NDIST]).then_inc(sem["bv_copied"], 1)
            act.wait_ge(sem["bv_copied"], 1)
            act.dma_start(A["bias_rows"], bv[:].unsqueeze(1).broadcast_to([NH, P, NDIST])).then_inc(sem["bias_stored"], 16)
            act.dma_start(posc[:], A["cmp_pos"]).then_inc(sem["cmpw_landed"], 16)
            act.dma_start(w2[:], A["cmp_w2"]).then_inc(sem["cmpw_landed"], 16)
            act.wait_ge(sem["cmpw_landed"], 32)
            act.dma_start(w1[:], A["cmp_w1"][0]).then_inc(sem["cmpw_landed"], 16)
            norm(R_FFN1)
            act.wait_ge(sem["bias_stored"], 16)
            rows_ = bass.AP(A["bias_rows"].tensor, P - 1, [[NDIST - 1, P], [P * NDIST, NH], [1, SEQ]])
            act.dma_start(tbl[:], rows_).then_inc(sem["tbl_landed"], 16)

            def key_norm_act(count, width, part):
                flat = [t_[:].rearrange("p c t -> p (c t)")[:, 0:width] for t_ in (ta, tb, tc)]
                if part == 0:
                    act.wait_ge(sem["k_scaled"], count)
                    act_fn(flat[1], flat[0], ACT.Square).then_inc(sem["k_sq"], 1)
                else:
                    act.wait_ge(sem["k_mean"], count)
                    act_fn(flat[1], flat[2], ACT.Ln).then_inc(sem["k_ln"], 1)
                    act.wait_ge(sem["k_ln"], count)
                    act_fn(flat[1], flat[1], ACT.Exp, scale=-0.5).then_inc(sem["k_exp"], 1)

            def values_copy(u, br):
                done(g + u)
                for t in range(TT):
                    last = copy(vs[:, br, t], U[1][:, t * SEQ:(t + 1) * SEQ], scale=rs_tok[:, t:t + 1])
                last.then_inc(sem["vs_ready"], 1)

            for m in range(PAIRS):
                x_high("kv", m)
            split(g)
            split(g + 1)
            key_norm_act(1, 512, 0)
            split(g + 2)
            values_copy(3, 0)
            split(g + 3)
            key_norm_act(1, 512, 1)
            key_norm_act(2, 512, 0)
            split(g + 4)
            values_copy(5, 1)
            split(g + 5)
            key_norm_act(2, 512, 1)

            def hidden(kind):
                act.wait_ge(sem["hid_done"], 2 * (kind + 1))
                for half in range(2):
                    last = act_fn(hg[:, half], [MB, U[0]][half][:, 0:2 * NCMP], ACT.Gelu_apprx_tanh)
                last.then_inc(sem["hg_ready"], 1)

            hidden(0)
            act.dma_start(w1[:], A["cmp_w1"][1]).then_inc(sem["cmpw_landed"], 16)
            key_norm_act(3, 2 * NCMP, 0)
            key_norm_act(3, 2 * NCMP, 1)
            act.wait_ge(sem["w2_done"], 1)
            hidden(1)
            act.wait_ge(sem["w2_done"], 2)
            copy(vcmp[:].rearrange("c k d -> c (k d)"), MB[0:NCMP, 256:512]).then_inc(sem["vc_ready"], 1)
            act.dma_start(wg[:], A["gate_w"]).then_inc(sem["wg_landed"], 16)
            ffn(2, R_FFN2, None)

            g = BASE["qg"]
            act.wait_ge(sem["wg_landed"], 16)
            copy(wg_hi[:], wg[:]).then_inc(sem["wg_hi_ready"], 1)
            norm(R_FFN2)
            for u in range(4):
                if u:
                    key_norm_act(3 + u, 512, 1)
                key_norm_act(4 + u, 512, 0)
                split(g + u)
            act.wait_ge(sem["gate_done"], 1)
            for t in range(TT):
                last = act_fn(gate[:, t], U[0][:, t * 64:t * 64 + 3 * NH], ACT.Sigmoid, scale=rs_tok[:, t:t + 1])
            last.then_inc(sem["gate_sig"], 1)
            key_norm_act(7, 512, 1)

            act.wait_ge(sem["k_ready"], 7)

            def n_copy(hd, l):
                b = l % 2
                act.wait_ge(sem["n_t"], hd + 1)
                if l:
                    act.wait_ge(sem["n_pv"], hd - 1)
                copy(ptn[:, b, 0], U[0][:, 0:3 * P])
                copy(ptc[:, b], MB[0:NCMP, 0:SEQ]).then_inc(sem["n_ta"], 1)

            def n_exp(hd, l):
                b = l % 2
                act.wait_ge(sem["n_max"], hd + 1)
                for t in range(TT):
                    act_fn(lgc[:, b, t], lgc[:, b, t], ACT.Exp, bias=nm[:, b, 0, t:t + 1],
                           accum_out=dn[:, b, 0, t:t + 1])
                for br in range(2):
                    act_fn(lg[:, b, br, 0:P], lg[:, b, br, 0:P], ACT.Exp, bias=nm[:, b, 1 + br, 0:1],
                           accum_out=dn[:, b, 1 + br, 0:1])
                    last = act_fn(lg[:, b, br, P:3 * P], lg[:, b, br, P:3 * P], ACT.Exp,
                                  bias=nm[:, b, 1 + br, 1:2], accum_out=dn[:, b, 1 + br, 1:2])
                last.then_inc(sem["n_exp"], 1)

            def n_high(ch):
                act.wait_ge(sem["n_ot"], ch + 1)
                copy(x_hi[0][:, bass.ds(ch, 1), :].rearrange("p o t -> p (o t)"),
                     MB[:, SEQ:2 * SEQ]).then_inc(sem["n_hi"], 1)

            for a in range(KVH // 2):
                with act.Fori(0, 2) as k:
                    h0 = 4 * k + 8 * a
                    act.wait_ge(sem["n_s"], h0)
                    act.wait_ge(sem["n_pv"], h0)
                    for cc in range(2):
                        copy(qst[:, cc], q2[:, bass.ds(2 * k + 4 * a + cc, 1), :]
                             .rearrange("p o t -> p (o t)")).then_inc(sem["q_staged"], 1)
                    for l in range(5):
                        if l >= 1:
                            n_copy(h0 + l - 1, l - 1)
                        if l < 4:
                            n_exp(h0 + l, l)
                        if l in (2, 4):
                            n_high(2 * k + 4 * a + l // 2 - 1)
            residual_stage("nwo", R_NWO)
            ffn(3, R_FFN3, R_NWO)

        @block.gpsimd
        def _(pool):
            def fill(ap, value):
                pool.memset(ap, value).then_inc(sem["fill_done"], 1)

            fill(ones[:], 1.0)
            fill(nhalf[:], -0.5)
            fill(zero[:], 0.0)
            fill(halfpi[:], math.pi / 2)
            fill(vp[:], 0.0)
            fill(bb[:], 0.0)
            fill(ct[:], 0.0)

            def add_squares(r):
                if r:
                    pool.wait_ge(sem["sum_ready"], min(r, 13))
                for m in range(3):
                    pool.wait_ge(sem["sq_ready"], PAIRS * r + m + 2)
                    if m == 0:
                        pool.tensor_tensor(ssum[:], sq[:, 0], sq[:, 1], ALU.add).then_inc(sem["sq_used"], 1)
                    else:
                        pool.wait_ge(sem["sq_used"], 3 * r + m)
                        pool.tensor_tensor(ssum[:], ssum[:], sq[:, (m + 1) % 2], ALU.add).then_inc(sem["sq_used"], 1)

            def norm(n):
                pool.wait_ge(sem["var_ready"], n + 1)
                pool.tensor_tensor(rs_tok[:], var_tok[:], nhalf[:], ALU.pow).then_inc(sem["rst_ready"], 1)

            def both(r):
                add_squares(r)
                norm(r)

            both(R_IN)
            both(R_SC)

            per = 1 + 5 * 8
            pool.wait_ge(sem["e_base"], 2)
            with pool.Fori(0, ST // EB) as b:
                pool.wait_ge(sem["e_stored"], 16 * b)
                pool.tensor_copy(e_tab[:, :, :, 0:1].rearrange("p j r o -> p j (r o)"),
                                 e_one[:, bass.ds(EB * b, EB), :]).then_inc(sem["e_step"], 1)
                for lv in range(8):
                    n = 1 << lv
                    lo, hi = e_tab[:, :, :, 0:n], e_tab[:, :, :, n:2 * n]
                    step = e_tab[:, :, :, n - 1:n]
                    at = 1 + 5 * lv
                    pool.wait_ge(sem["e_step"], per * b + at)
                    pool.tensor_tensor(e_t1[:, :, :, 0:n], lo, step[:, :, 0:1].broadcast_to([P, EB, 2, n]),
                                       ALU.mult).then_inc(sem["e_step"], 1)
                    pool.tensor_tensor(e_t2[:, :, 0, 0:n], lo[:, :, 1], step[:, :, 1].broadcast_to([P, EB, n]),
                                       ALU.mult).then_inc(sem["e_step"], 1)
                    pool.tensor_tensor(e_t2[:, :, 1, 0:n], lo[:, :, 0], step[:, :, 1].broadcast_to([P, EB, n]),
                                       ALU.mult).then_inc(sem["e_step"], 1)
                    pool.wait_ge(sem["e_step"], per * b + at + 3)
                    pool.tensor_tensor(hi[:, :, 0], e_t1[:, :, 0, 0:n], e_t2[:, :, 0, 0:n],
                                       ALU.subtract).then_inc(sem["e_step"], 1)
                    pool.tensor_tensor(hi[:, :, 1], e_t1[:, :, 1, 0:n], e_t2[:, :, 1, 0:n],
                                       ALU.add).then_inc(sem["e_step"], 1)
                pool.wait_ge(sem["e_step"], per * b + per)
                pool.dma_start(A["e_table"][bass.ds(b, 1)].rearrange("o p n -> p (o n)"),
                               e_tab[:].rearrange("p j r t -> p (j r t)")).then_inc(sem["e_stored"], 16)
            both(R_MLP0)
            both(R_PLE0)

            def rotate(i, u):
                side, gr = u // NG, u % NG
                n = 6 * i + u
                pool.wait_ge(sem["swapped"], n + 1)
                pool.tensor_tensor(swap[:], swap[:], sin_rs[0:32].unsqueeze(1).broadcast_to([32, 2, SEQ]),
                                   ALU.mult).then_inc(sem["sin_part"], 1)
                pool.wait_ge(sem["sin_part"], n + 1)
                pool.wait_ge(sem["qk_main"], n + 1)
                pool.tensor_tensor(qk[0:32, side, gr], qk[0:32, side, gr], swap[:],
                                   ALU.add).then_inc(sem["qk_ready"], 1)

            pool.wait_ge(sem["rope_rs"], 2)
            with pool.Fori(0, HEAD_PAIRS) as i:
                for u in range(6):
                    rotate(i, u)
            both(R_WO)
            both(R_MLP1)
            both(R_PLE1)
            both(R_FIN)
            both(R_FFN0)

            for j in range(ST):
                pool.wait_ge(sem["z_ready"], 2 * (j + 1))
                if j:
                    pool.wait_ge(sem["y_done"], j)
                e = e_ring[:, (j // EB) % 2, j % EB]
                z = z5[:, j % 2]
                pool.tensor_tensor(n1[:], z, e[:, 0:1].broadcast_to([P, 2, SEQ]), ALU.mult).then_inc(sem["turned_back"], 1)
                pool.tensor_tensor(n2[:, 0], z[:, 1], e[:, 1], ALU.mult)
                pool.tensor_tensor(n2[:, 1], z[:, 0], e[:, 1], ALU.mult).then_inc(sem["turned_back"], 1)
            both(R_GLU)
            both(R_FFN1)
            both(R_FFN2)
            both(R_NWO)

        @block.vector
        def _(dve):
            tt, stt, ts = dve.tensor_tensor, dve.scalar_tensor_tensor, dve.tensor_scalar
            rs_b = rs[:]

            def done(g0, k=0):
                dve.wait_ge(sem["unit_done"], g0 + 1 + RING * k)

            def split(g0, k=0):
                g = g0 + RING
                if isinstance(k, int) and g + RING * k >= NU:
                    return
                dve.wait_ge(sem["hi_ready"], g + 1 + RING * k)
                tt(w_lo[:, g % RING], raw[:, g % RING], w_hi[:, g % RING].bitcast(F32),
                   ALU.subtract).then_inc(sem["lo_ready"], 1)

            def x_low(r, m):
                dve.wait_ge(sem["xh_ready"], XBASE[r] + m + 1)
                for q in range(2):
                    c = 2 * m + q
                    last = stt(x_lo[XBUF[r]][:, c], h[:, c], col(GAIN[r], c), x_hi[XBUF[r]][:, c].bitcast(F32),
                               ALU.mult, ALU.subtract)
                last.then_inc(sem["xl_ready"], 1)

            def add(m, part, scale=1.0):
                pair = h[:, 2 * m:2 * m + 2]
                stt(pair, part, scale, pair, ALU.mult, ALU.add).then_inc(sem["h_ready"], 1)

            def norm(n):
                dve.wait_ge(sem["sum_ready"], n + 1)
                ts(var_tok[:], MB[:, 0:TT], 1.0 / D, EPS, ALU.mult, ALU.add).then_inc(sem["var_ready"], 1)
                dve.wait_ge(sem["rst_ready"], n + 1)
                tt(diag[:], ident.unsqueeze(1).broadcast_to([P, TT, P]),
                   rs_tok[:].unsqueeze(2).broadcast_to([P, TT, P]), ALU.mult).then_inc(sem["diag_ready"], 1)

            def residual_stage(stage, r):
                for m in range(PAIRS):
                    done(BASE[stage] + m)
                    add(m, two(U[m % 2]))
                    x_low(r, m)
                    split(BASE[stage] + m)

            def last_sums(g, r, scale, x):
                for m in range(PAIRS + 1):
                    if m < PAIRS:
                        if m < PAIRS - 1:
                            dve.wait_ge(sem["acc_done"], 3 * DOWN[r] + m + 1)
                        else:
                            done(g)
                        add(m, two(DB[m]), scale)
                    if m and x:
                        x_low(r, m - 1)

            DOWN = {R_MLP0: 0, R_MLP1: 1, R_FFN0: 2, R_FFN1: 3, R_FFN2: 4, R_FFN3: 5}

            def mlp(l, n, r):
                g, first, hb = BASE[f"mlp{l}"], MLP_PAIRS * l, HID_BASE[f"mlp{l}"]

                def relu(g0, k):
                    done(g0, k)
                    stt(ta[:], two(U[0]), 0.0, rs_b, ALU.max, ALU.mult).then_inc(sem["relu_ready"], 1)

                def low(i):
                    dve.wait_ge(sem["hid_hi_ready"], hb + i + 1)
                    tt(hid_lo[:], tb[:], hid_hi[:].bitcast(F32), ALU.subtract).then_inc(sem["hid_lo_ready"], 1)

                dve.wait_ge(sem["p_hi_ready"], l + 1)
                tt(p_lo[:], p_in[:], p_hi[:].bitcast(F32), ALU.subtract).then_inc(sem["p_lo_ready"], 1)
                norm(n)
                dve.wait_ge(sem["rs_ready"], n + 1)
                relu(g, 0)
                low(0)
                split(g)
                with dve.Fori(0, (MLP_PAIRS - 1) // RING) as k:
                    for t in range(RING):
                        relu(g + 1 + 2 * t, 2 * k)
                        split(g + 1 + 2 * t, 2 * k)
                        low(RING * k + t + 1)
                        split(g + 2 + 2 * t, 2 * k)
                last_sums(g + 2 * MLP_PAIRS - 1, r, 1.0, True)
                split(g + 2 * MLP_PAIRS - 1)

            def ffn(f, n, r, x=True):
                g, first, hb = BASE[f"ffn{f}"], FFN_PAIRS * f, HID_BASE[f"ffn{f}"]

                def first_half(g0, k):
                    done(g0, k)
                    tt(ta[:], two(U[0]), rs_b, ALU.mult).then_inc(sem["a_scaled"], 1)

                def second_half(g0, k, i):
                    done(g0, k)
                    tt(tc[:], two(U[1]), rs_b, ALU.mult).then_inc(sem["b_gated"], 1)
                    dve.wait_ge(sem["silu_ready"], first + i + 1)
                    dve.wait_ge(sem["b_gated"], first + i + 1)
                    tt(tc[:], tb[:], tc[:], ALU.mult).then_inc(sem["prod_ready"], 1)

                def low(i):
                    dve.wait_ge(sem["hid_hi_ready"], hb + i + 1)
                    tt(hid_lo[:], tc[:], hid_hi[:].bitcast(F32), ALU.subtract).then_inc(sem["hid_lo_ready"], 1)

                if n is not None:
                    norm(n)
                    dve.wait_ge(sem["rs_ready"], n + 1)
                first_half(g, 0)
                split(g)
                second_half(g + 1, 0, 0)
                low(0)
                split(g + 1)

                def pair(k):
                    first_half(g + 2, k)
                    split(g + 2, k)
                    second_half(g + 3, k, k + 1)
                    split(g + 3, k)
                    low(k + 1)
                    split(g + 4, k)

                with dve.Fori(0, FFN_PAIRS - 1 - (f == 3)) as k:
                    pair(k)
                if f == 3:
                    pair(FFN_PAIRS - 2)
                last_sums(g + 3 * FFN_PAIRS - 1, r, 0.5, x)
                split(g + 3 * FFN_PAIRS - 1)

            def gated(count, other, m):
                dve.wait_ge(sem["gate_ready"], count)
                tt(tc[:], tb[:], other, ALU.mult).then_inc(sem["gated"], 1)
                dve.wait_ge(sem["gated"], count)
                add(m, tc[:])

            def ple(l, n, r, x=True):
                g = BASE[f"ple{l}"]
                split(g)
                norm(n)
                dve.wait_ge(sem["rs_ready"], n + 1)
                for m in range(PAIRS):
                    done(g + 1 + m)
                    tt(ta[:], two(U[m % 2]), rs_b, ALU.mult).then_inc(sem["gate_scaled"], 1)
                    gated(PAIRS * l + m + 1, two([XB, DB[0], DB[1], DB[2]][m]), m)
                    if x:
                        x_low(r, m)
                    split(g + 1 + m)

            def first_split(g):
                dve.wait_ge(sem["hi_ready"], g + 1)
                tt(w_lo[:, g], raw[:, g], w_hi[:, g].bitcast(F32), ALU.subtract).then_inc(sem["lo_ready"], 1)

            for m in range(2):
                x_low(R_IN, m)
            first_split(0)
            for m in range(2, PAIRS):
                x_low(R_IN, m)
            for g in range(1, RING):
                first_split(g)

            norm(R_IN)
            dve.wait_ge(sem["rs_ready"], 1)
            tt(rs2[:], rs[:], rs[:], ALU.mult).then_inc(sem["rs2_ready"], 1)
            dve.wait_ge(sem["fill_done"], 7)
            dve.wait_ge(sem["rs2_ready"], 1)

            def conv_triple(g0, k, j):
                done(g0 + 1, k)
                v = vp[:, :, 2:SEQ + 2]
                dve.wait_ge(sem["c_copied"], j + 1)
                split(g0, k)
                tt(v, tb[:], two(U[1]), ALU.mult).then_inc(sem["v_raw"], 1)
                dve.wait_ge(sem["v_raw"], j + 1)
                tt(v, v, rs2[:], ALU.mult).then_inc(sem["v_ready"], 1)
                dve.wait_ge(sem["v_ready"], j + 1)
                for tap in range(3):
                    if tap:
                        dve.wait_ge(sem["tap_done"], 6 * j + 2 * tap)
                    for q in range(2):
                        w = vec[:, bass.ds(VCOL["conv"] + (2 - tap) * KC + q + 2 * j, 1)]
                        x_ = vp[:, q, 2 - tap:SEQ + 2 - tap]
                        if tap:
                            ins = stt(yc[:, q], x_, w, yc[:, q], ALU.mult, ALU.add)
                        else:
                            ins = ts(yc[:, q], x_, w, None, ALU.mult)
                        ins.then_inc(sem["tap_done"], 1)
                split(g0 + 1, k)
                done(g0 + 2, k)
                tt(tc[:], two(XB), rs_b, ALU.mult).then_inc(sem["b_scaled"], 1)
                dve.wait_ge(sem["b_scaled"], j + 1)
                dve.wait_ge(sem["tap_done"], 6 * j + 6)
                tt(tc[:], tc[:], yc[:], ALU.mult).then_inc(sem["y_ready"], 1)
                dve.wait_ge(sem["y_hi"], j + 1)
                yh = x_hi[1][:, bass.ds(2 * j, 2), :].bitcast(F32)
                tt(x_lo[1][:, bass.ds(2 * j, 2), :], tc[:], yh, ALU.subtract).then_inc(sem["y_lo"], 1)
                split(g0 + 2, k)

            conv_triple(0, 0, 0)
            with dve.Fori(0, PAIRS - 1) as k:
                conv_triple(3, k, k + 1)
            residual_stage("sc_out", R_SC)

            count = [0]

            def link(ins):
                ins.then_inc(sem["sm_dve"], 1)
                count[0] += 1
                dve.wait_ge(sem["sm_dve"], count[0])

            are, aim = col("are", 0, ST), col("aim", 0, ST)
            dve.wait_ge(sem["sm_act"], 1)
            link(tt(sm[:, 1], are, sm[:, 0], ALU.mult))
            link(ts(sm[:, 1], sm[:, 1], 2.0 ** -S5_HALVINGS, None, ALU.mult))
            link(dve.tensor_copy(sm[:, 2], sm[:, 1]))
            for n in (6, 5, 4, 3, 2):
                link(ts(sm[:, 2], sm[:, 2], 1.0 / n, 1.0, ALU.mult, ALU.add))
                link(tt(sm[:, 2], sm[:, 2], sm[:, 1], ALU.mult))
            for _ in range(S5_HALVINGS):
                link(stt(sm[:, 2], sm[:, 2], 2.0, sm[:, 2], ALU.add, ALU.mult))
            link(ts(mag[:], sm[:, 2], 1.0, None, ALU.add))
            link(tt(sm[:, 3], aim, sm[:, 0], ALU.mult))
            link(ts(sm[:, 4], sm[:, 3], 1.0 / (2 * math.pi), ROUND, ALU.mult, ALU.add))
            link(ts(sm[:, 4], sm[:, 4], -ROUND, None, ALU.add))
            link(stt(sm[:, 5], sm[:, 4], -TWO_PI_1, sm[:, 3], ALU.mult, ALU.add))
            link(stt(sm[:, 5], sm[:, 4], -TWO_PI_2, sm[:, 5], ALU.mult, ALU.add))
            link(stt(sm[:, 5], sm[:, 4], -TWO_PI_3, sm[:, 5], ALU.mult, ALU.add))
            link(ts(sm[:, 5], sm[:, 5], 3.1415925, -3.1415925, ALU.min, ALU.max))
            assert count[0] == S5_R
            dve.wait_ge(sem["sm_act"], 4)
            cosa, sina = sm[:, 6], sm[:, 7]
            dve.tensor_copy(e_one[:, :, 0], cosa).then_inc(sem["e_base"], 1)
            dve.tensor_copy(e_one[:, :, 1], sina).then_inc(sem["e_base"], 1)
            link(tt(sm[:, 9], mag[:], cosa, ALU.mult))
            link(tt(sm[:, 10], mag[:], sina, ALU.mult))
            link(ts(sm[:, 9], sm[:, 9], -1.0, None, ALU.add))
            link(tt(sm[:, 11], are, are, ALU.mult))
            link(tt(sm[:, 12], aim, aim, ALU.mult))
            link(tt(sm[:, 11], sm[:, 11], sm[:, 12], ALU.add))
            link(dve.reciprocal(sm[:, 12], sm[:, 11]))
            link(tt(sm[:, 13], sm[:, 9], are, ALU.mult))
            link(tt(sm[:, 14], sm[:, 10], aim, ALU.mult))
            link(tt(sm[:, 13], sm[:, 13], sm[:, 14], ALU.add))
            link(tt(sm[:, 13], sm[:, 13], sm[:, 12], ALU.mult))
            link(tt(sm[:, 14], sm[:, 10], are, ALU.mult))
            link(tt(sm[:, 15], sm[:, 9], aim, ALU.mult))
            link(tt(sm[:, 14], sm[:, 14], sm[:, 15], ALU.subtract))
            link(tt(sm[:, 14], sm[:, 14], sm[:, 12], ALU.mult))
            t_a = ta[:].rearrange("p c t -> p (c t)").rearrange("p (j q) -> p j q", q=S5_CH)
            t_b = tb[:].rearrange("p c t -> p (c t)").rearrange("p (j q) -> p j q", q=S5_CH)
            z_re = sm[:, 13].unsqueeze(2).broadcast_to([P, ST, S5_CH])
            z_im = sm[:, 14].unsqueeze(2).broadcast_to([P, ST, S5_CH])
            for ri, (x0, x1, op) in enumerate(((0, 1, ALU.subtract), (1, 0, ALU.add))):
                link(tt(t_a, s5b[:, x0], z_re, ALU.mult))
                link(tt(t_b, s5b[:, x1], z_im, ALU.mult))
                for g2 in range(2):
                    rows = slice(g2 * S5_STATE, (g2 + 1) * S5_STATE)
                    tt(bb[rows, ri, :, g2 * S5_CH:(g2 + 1) * S5_CH], t_a[rows], t_b[rows],
                       op).then_inc(sem["bb_ready"], 1)
                dve.wait_ge(sem["bb_ready"], 2 * (ri + 1))

            mlp(0, R_SC, R_MLP0)
            ple(0, R_MLP0, R_PLE0)

            def step(ins, n):
                ins.then_inc(sem["rope_step"], 1)
                dve.wait_ge(sem["rope_step"], n)

            dve.wait_ge(sem["pos_landed"], 16)
            step(dve.tensor_copy(ang[:, 0], posi[:]), 1)
            step(ts(ang[:, 1], ang[:, 0], cst("invf", 1), None, ALU.mult), 2)
            step(ts(ang[:, 2], ang[:, 1], 1.0 / (2 * math.pi), ROUND, ALU.mult, ALU.add), 3)
            step(ts(ang[:, 2], ang[:, 2], -ROUND, None, ALU.add), 4)
            dve.scalar_tensor_tensor(ang[:, 1], ang[:, 2], -TWO_PI_1, ang[:, 1], ALU.mult, ALU.add)\
                .then_inc(sem["rope_ready"], 1)
            dve.wait_ge(sem["rope_ready"], 1)
            stt(ang[:, 1], ang[:, 2], -TWO_PI_2, ang[:, 1], ALU.mult, ALU.add).then_inc(sem["rope_ready"], 1)
            dve.wait_ge(sem["rope_ready"], 2)
            step(stt(ang[:, 1], ang[:, 2], -TWO_PI_3, ang[:, 1], ALU.mult, ALU.add), 5)
            step(ts(ang[:, 1], ang[:, 1], 3.1415925, -3.1415925, ALU.min, ALU.max), 6)
            dve.wait_ge(sem["sin_ready"], 3)
            norm(R_PLE0)
            dve.wait_ge(sem["rs_ready"], R_PLE0 + 1)
            tt(cos_rs[:], rope_c[:], rs[:, 0], ALU.mult).then_inc(sem["rope_rs"], 1)
            stt(sin_rs[:], rope_s[:], cst("sgn", 1), rs[:, 0], ALU.mult, ALU.mult).then_inc(sem["rope_rs"], 1)
            dve.wait_ge(sem["rope_rs"], 2)

            g = BASE["qkv"]
            half_swap = [(p + ROPE // 2) % ROPE for p in range(ROPE)]

            def softmax_in(hd):
                dve.wait_ge(sem["s_done"], hd + 1)
                dve.wait_ge(sem["pt_done"], 3 * hd)
                tt(lg0[:].rearrange("p g k -> p (g k)"), DB[0][:, 0:NG * P], cst("mask0", NG * P),
                   ALU.add).then_inc(sem["masked"], 1)
                tt(lg1[:].rearrange("p g k -> p (g k)"), psum[:, 1:3].rearrange("p b n -> p (b n)")[:, 0:NG * SEQ],
                   cst("mask1", NG * SEQ), ALU.add).then_inc(sem["masked"], 1)
                dve.wait_ge(sem["masked"], 2 * (hd + 1))
                for t, part in enumerate((lg0, lg1)):
                    dve.tensor_reduce(nmax[:, t:t + 1], part[:], AX.XY, ALU.max,
                                      negate=True).then_inc(sem["max_done"], 1)
                dve.wait_ge(sem["max_done"], 2 * (hd + 1))
                ts(nbias[:], nmax[:], SCALE, None, ALU.mult).then_inc(sem["bias_ready"], 1)

            def denominators(hd):
                dve.wait_ge(sem["exp_done"], 2 * (hd + 1))
                dve.wait_ge(sem["o_scaled"], 2 * hd)
                dve.reciprocal(rden[:], den[:]).then_inc(sem["rden_ready"], 1)

            def out_low(hd):
                dve.wait_ge(sem["o_hi"], hd + 1)
                out = x_lo[1][:, bass.ds(hd, 1), :].rearrange("p o t -> p (o t)")
                hi = x_hi[1][:, bass.ds(hd, 1), :].rearrange("p o t -> p (o t)").bitcast(F32)
                tt(out, DB[2][:, 0:SEQ], hi, ALU.subtract).then_inc(sem["o_lo"], 1)

            def rope(g0, k, i, u, first):
                side, gr = u // NG, u % NG
                done(g0, k)
                dve.wait_ge(sem["qk_ready"], 6 * i + u)
                bank = two(U3[u % 3])
                if not first:
                    dve.wait_ge(sem["s_done"], 2 * i - 1 + side)
                tt(qk[:, side, gr], bank, cos_rs[:].unsqueeze(1).broadcast_to([P, 2, SEQ]),
                   ALU.mult).then_inc(sem["qk_main"], 1)
                dve.stream_shuffle(swap[:], bank[0:32], half_swap).then_inc(sem["swapped"], 1)

            def attend(i, u):
                a, b = 2 * i, 2 * i + 1
                if u == 0:
                    denominators(a)
                elif u == 1:
                    softmax_in(b)
                elif u == 3:
                    denominators(b)
                    out_low(a)
                elif u == 6:
                    out_low(b)

            def qkv_units(k, i, before, first):
                for u in range(9):
                    if u < 6:
                        rope(g + u, k, i, u, first)
                    split(g + u, k)
                    if before is not None:
                        attend(before, u)

            qkv_units(0, 0, None, True)
            with dve.Fori(0, HEAD_PAIRS - 1) as k:
                softmax_in(2 * k)
                qkv_units(3 * k + 3, k + 1, k, False)
            softmax_in(2 * (HEAD_PAIRS - 1))
            for u in range(7):
                attend(HEAD_PAIRS - 1, u)
            residual_stage("wo", R_WO)

            mlp(1, R_WO, R_MLP1)
            ple(1, R_MLP1, R_PLE1, x=False)

            norm(R_PLE1)
            dve.wait_ge(sem["rs_ready"], R_PLE1 + 1)
            for m in range(PAIRS + 1):
                if m < PAIRS:
                    for q in range(2):
                        c = 2 * m + q
                        last = stt(h[:, c], h[:, c], col("final", c), rs[:, 0], ALU.mult, ALU.mult)
                    last.then_inc(sem["h_ready"], 1)
                if m:
                    x_low(R_FIN, m - 1)
            ffn(0, R_FIN, R_FFN0, x=False)

            norm(R_FFN0)
            dve.wait_ge(sem["rs_ready"], R_FFN0 + 1)
            for c in range(KC):
                stt(u5[:, c], h[:, c], col("s5mix", c), rs[:, 0], ALU.mult, ALU.mult).then_inc(sem["u5_ready"], 1)

            def skip(c):
                dve.wait_ge(sem["y_done"], 4 * c + 4)
                stt(ta[:, 0], u5[:, c], col("s5d", c), DB[c % 4][:, 0:SEQ], ALU.mult,
                    ALU.add).then_inc(sem["y_in"], 1)

            def gelu_low(c):
                dve.wait_ge(sem["g_hi"], c + 1)
                tt(x_lo[1][:, c], y5[:, c], x_hi[1][:, c].bitcast(F32), ALU.subtract).then_inc(sem["g_lo"], 1)

            m1, m2 = tb, tc
            for j in range(ST):
                b = j // EB
                if j % EB == 0:
                    dve.wait_ge([sem["e_landed0"], sem["e_landed1"]][b % 2], 16 * (b // 2 + 1))
                e = e_ring[:, b % 2, j % EB]
                dve.wait_ge(sem["bu_done"], j + 1)
                if j:
                    dve.wait_ge(sem["z_ready"], 2 * j)
                bu = two(U[j % 2])
                tt(m1[:], bu, e[:, 0:1].broadcast_to([P, 2, SEQ]), ALU.mult).then_inc(sem["turned"], 1)
                tt(m2[:, 0], bu[:, 1], e[:, 1], ALU.mult).then_inc(sem["turned"], 1)
                tt(m2[:, 1], bu[:, 0], e[:, 1], ALU.mult).then_inc(sem["drive"], 1)
                dve.wait_ge(sem["turned"], 4 * j + 2)
                tt(m1[:, 0], m1[:, 0], m2[:, 0], ALU.add).then_inc(sem["turned"], 1)
                dve.wait_ge(sem["drive"], j + 1)
                tt(m1[:, 1], m1[:, 1], m2[:, 1], ALU.subtract).then_inc(sem["turned"], 1)
                if j >= 2:
                    dve.wait_ge(sem["turned_back"], 2 * (j - 1))
                decay = mag[:, j:j + 1].broadcast_to([P, SEQ])
                for ri in range(2):
                    dve.wait_ge(sem["turned"], 4 * j + 3 + ri)
                    dve.tensor_tensor_scan(z5[:, j % 2, ri], decay, m1[:, ri], 0.0, ALU.mult,
                                           ALU.add).then_inc(sem["z_ready"], 1)
                if j % 4 == 1 and j >= 5:
                    skip(j // 4 - 1)
                if j % 4 == 2 and j >= 6:
                    gelu_low(j // 4 - 1)
            skip(KC - 1)
            gelu_low(KC - 1)
            for m in range(PAIRS):
                done(BASE["glu"] + m)
                gated(2 * PAIRS + m + 1, y5[:, 2 * m:2 * m + 2], m)
                x_low(R_GLU, m)
                split(BASE["glu"] + m)
            ffn(1, R_GLU, R_FFN1)

            dve.wait_ge(sem["bias_in_landed"], 48)
            dve.memset(rel[NBUCKET:NBUCKET + 1], NEG).then_inc(sem["rel_ready"], 1)
            dve.wait_ge(sem["cb_done"], 1)
            dve.tensor_copy(cmp_bias[:].rearrange("p i n -> p (i n)"),
                            MB[:, 0:TT * NCMP * NH]).then_inc(sem["cb_ready"], 1)
            g = BASE["kv"]
            norm(R_FFN1)
            dve.wait_ge(sem["rs_ready"], R_FFN1 + 1)

            def blocks(kind):
                dve.wait_ge(sem["src_ready"], kind + 1)
                dve.wait_ge(sem["cmpw_landed"], 32)
                if kind:
                    dve.wait_ge(sem["hid_done"], 2)
                for a in range(2):
                    whole = src[:, kind, a, :]
                    windows = bass.AP(whole.tensor, whole.offset, [list(whole.ap[0]), [CS, NCMP], [1, CL]])
                    last = tt(blk[:, :, a, :].rearrange("p l n -> p n l"), windows,
                              posc[:, kind].unsqueeze(1).broadcast_to([P, NCMP, CL]), ALU.add)
                last.then_inc(sem["blk_ready"], 1)

            def flat(t_, width):
                return t_.rearrange("p c t -> p (c t)")[:, 0:width]

            def key_mean(n, width):
                dve.wait_ge(sem["k_sum"], n)
                ts(flat(tc[:], width), XB[:, 0:width], 1.0 / HD, EPS, ALU.mult, ALU.add).then_inc(sem["k_mean"], 1)

            def key_norm(n, width, gain, out):
                a, y, m_, t_ = (flat(v, width) for v in (ta[:], tb[:], tc[:], sq[:, 0]))
                dve.wait_ge(sem["k_exp"], n)
                tt(t_, y, y, ALU.mult).then_inc(sem["k_step"], 1)
                dve.wait_ge(sem["k_step"], 4 * n - 3)
                tt(t_, t_, m_, ALU.mult).then_inc(sem["k_step"], 1)
                dve.wait_ge(sem["k_step"], 4 * n - 2)
                ts(t_, t_, -0.5, 1.5, ALU.mult, ALU.add).then_inc(sem["k_step"], 1)
                dve.wait_ge(sem["k_step"], 4 * n - 1)
                tt(y, y, t_, ALU.mult).then_inc(sem["k_step"], 1)
                dve.wait_ge(sem["k_step"], 4 * n)
                stt(out, a, col(gain), y, ALU.mult, ALU.mult).then_inc(sem["k_ready"], 1)

            for kind in range(2):
                done(g + kind)
                tt(src[:, kind], two(U[kind]), rs_b, ALU.mult).then_inc(sem["src_ready"], 1)
                if kind == 0:
                    for m in range(PAIRS):
                        x_low("kv", m)
                    blocks(0)
                split(g + kind)
            done(g + 2)
            tt(ta[:], two(U[0]), rs_b, ALU.mult).then_inc(sem["k_scaled"], 1)
            split(g + 2)
            split(g + 3)
            key_mean(1, 512)
            key_norm(1, 512, "ksn", ks[:, 0].rearrange("p c t -> p (c t)"))
            done(g + 4)
            dve.wait_ge(sem["k_ready"], 1)
            tt(ta[:], two(U[0]), rs_b, ALU.mult).then_inc(sem["k_scaled"], 1)
            split(g + 4)
            split(g + 5)
            key_mean(2, 512)
            key_norm(2, 512, "kwn", ks[:, 1].rearrange("p c t -> p (c t)"))
            dve.wait_ge(sem["w2_done"], 1)
            dve.wait_ge(sem["k_ready"], 2)
            dve.tensor_copy(flat(ta[:], 2 * NCMP), MB[:, 128:128 + 2 * NCMP]).then_inc(sem["k_scaled"], 1)
            blocks(1)
            key_mean(3, 2 * NCMP)
            key_norm(3, 2 * NCMP, "kcn", kcmp[:].rearrange("p c n -> p (c n)"))
            dve.wait_ge(sem["k_ready"], 3)
            ffn(2, None, R_FFN2)

            g = BASE["qg"]
            dve.wait_ge(sem["wg_hi_ready"], 1)
            tt(wg_lo[:], wg[:], wg_hi[:].bitcast(F32), ALU.subtract).then_inc(sem["wg_lo_ready"], 1)
            norm(R_FFN2)
            dve.wait_ge(sem["rs_ready"], R_FFN2 + 1)

            def queries(u):
                key_mean(4 + u, 512)
                key_norm(4 + u, 512, "qn", q2[:, 2 * u:2 * u + 2].rearrange("p c t -> p (c t)"))

            for u in range(4):
                if u:
                    queries(u - 1)
                    dve.wait_ge(sem["k_ready"], 3 + u)
                done(g + u)
                tt(ta[:], two(U[u % 2]), rs_b, ALU.mult).then_inc(sem["k_scaled"], 1)
                split(g + u)
            dve.wait_ge(sem["gate_sig"], 1)
            for t in range(TT):
                last = ts(gate[:, t, 0:NH], gate[:, t, 0:NH], con[:, CCOL["anyc"] + t:CCOL["anyc"] + t + 1], None,
                          ALU.mult)
            last.then_inc(sem["gate_all"], 1)
            queries(3)

            dve.wait_ge(sem["tbl_landed"], 16)
            dve.wait_ge(sem["k_ready"], 7)
            dve.wait_ge(sem["gate_all"], 1)

            def logits(hd, l):
                b = l % 2
                dve.wait_ge(sem["n_s"], hd + 1)
                if l:
                    dve.wait_ge(sem["n_t"], hd - 1)
                near = tbl[:, bass.ds(hd, 1), P:2 * P].rearrange("p o k -> p (o k)")
                far = tbl[:, bass.ds(hd, 1), :].rearrange("p o k -> p (o k)")
                stt(lgc[:, b].rearrange("p t c -> p (t c)"), DB[b][:, 3 * P:3 * P + TT * NCMP], NSCALE,
                    cmp_bias[:, :, bass.ds(hd, 1)].rearrange("p i o -> p (i o)"), ALU.mult, ALU.add)
                for br in range(2):
                    bank = DB[2 * br + b]
                    stt(lg[:, b, br, 0:P], bank[:, 0:P], NSCALE, near, ALU.mult, ALU.add)
                    last = stt(lg[:, b, br, P:3 * P], bank[:, P:3 * P], NSCALE, far, ALU.mult, ALU.add)
                last.then_inc(sem["n_log"], 1)
                dve.wait_ge(sem["n_log"], hd + 1)
                dve.tensor_reduce(nm[:, b, 0, :], lgc[:, b], AX.X, ALU.max, negate=True)
                for br in range(2):
                    dve.tensor_reduce(nm[:, b, 1 + br, 0:1], lg[:, b, br, 0:P], AX.X, ALU.max, negate=True)
                    last = dve.tensor_reduce(nm[:, b, 1 + br, 1:2], lg[:, b, br, P:3 * P], AX.X, ALU.max, negate=True)
                last.then_inc(sem["n_max"], 1)

            def factors(hd, l):
                b = l % 2
                dve.wait_ge(sem["n_exp"], hd + 1)
                dve.reciprocal(fac[:, b].rearrange("p r t -> p (r t)"),
                               dn[:, b].rearrange("p r t -> p (r t)")).then_inc(sem["n_rec"], 1)
                dve.wait_ge(sem["n_rec"], hd + 1)
                of = gate[:].rearrange("p t (r n) -> p r t n", n=NH)[:, :, :, bass.ds(hd, 1)]
                tt(fac[:, b], fac[:, b], of.rearrange("p r t o -> p r (t o)"), ALU.mult).then_inc(sem["n_fac"], 1)

            def window_copy(hd, l):
                dve.wait_ge(sem["n_t"], hd + 1)
                if l:
                    dve.wait_ge(sem["n_pv"], hd - 1)
                dve.tensor_copy(ptn[:, l % 2, 1], U[1][:, 0:3 * P]).then_inc(sem["n_tv"], 1)

            def combine(hd, l):
                b, cc = l % 2, l // 2
                dve.wait_ge(sem["n_pv"], hd + 1)
                dve.wait_ge(sem["n_fac"], hd + 1)
                for br in range(3):
                    if br:
                        dve.wait_ge(sem["n_part"], 3 * hd + br)
                    for t in range(TT):
                        at = (br * TT + t) * HD
                        out = oc[:, cc, t, b]
                        f = fac[:, b, br, t:t + 1]
                        if br:
                            last = stt(out, XB[:, at:at + HD], f, out, ALU.mult, ALU.add)
                        else:
                            last = ts(out, XB[:, at:at + HD], f, None, ALU.mult)
                    last.then_inc(sem["n_part"], 1)

            def n_low(ch):
                dve.wait_ge(sem["n_hi"], ch + 1)
                out = x_lo[0][:, bass.ds(ch, 1), :].rearrange("p o t -> p (o t)")
                hi = x_hi[0][:, bass.ds(ch, 1), :].rearrange("p o t -> p (o t)").bitcast(F32)
                tt(out, MB[:, SEQ:2 * SEQ], hi, ALU.subtract).then_inc(sem["n_lo"], 1)

            for a in range(KVH // 2):
                with dve.Fori(0, 2) as k:
                    h0 = 4 * k + 8 * a
                    dve.wait_ge(sem["n_pv"], h0)
                    for l in range(5):
                        if l < 4:
                            logits(h0 + l, l)
                        if l >= 1:
                            factors(h0 + l - 1, l - 1)
                            window_copy(h0 + l - 1, l - 1)
                            combine(h0 + l - 1, l - 1)
                        if l in (2, 4):
                            n_low(2 * k + 4 * a + l // 2 - 1)
            residual_stage("nwo", R_NWO)
            ffn(3, R_NWO, R_FFN3, x=False)


def _wide(w):
    return w.reshape(KC, P, 256).transpose(1, 0, 2).reshape(P, UNIT)


def _deep(w):
    return w.reshape(2, P, D).transpose(1, 0, 2).reshape(P, UNIT)


def _units(i):
    w = i["sc_w_in"][0]
    for j in range(PAIRS):
        for part in (1, 2, 0):
            yield _wide(w[:, part * D + 256 * j:part * D + 256 * (j + 1)])

    def square(w):
        for m in range(PAIRS):
            yield _wide(w[:, 256 * m:256 * (m + 1)])

    def mlp(l):
        up, down = i["mlp_w_up"][l], i["mlp_w_down"][l]
        for n in range(MLP_PAIRS + 1):
            if n < MLP_PAIRS:
                yield _wide(up[:, 256 * n:256 * (n + 1)])
            if n:
                yield _deep(down[256 * (n - 1):256 * n])

    def ple(l):
        yield _deep(i["ple_w_proj"][l])
        yield from square(i["ple_w_gate"][l])

    def ffn(w_in, w_out):
        for n in range(FFN_PAIRS + 1):
            if n < FFN_PAIRS:
                yield _wide(w_in[:, 256 * n:256 * (n + 1)])
                yield _wide(w_in[:, D_FF2 + 256 * n:D_FF2 + 256 * (n + 1)])
            if n:
                yield _deep(w_out[256 * (n - 1):256 * n])

    yield from square(i["sc_w_out"][0])
    yield from mlp(0)
    yield from ple(0)
    w = i["attn_w_qkv"][0].reshape(D, 3, NG, HEADS, DH)
    for pair in range(HEAD_PAIRS):
        for side in range(2):
            for gr in range(NG):
                yield _wide(w[:, 0:2, gr, 2 * pair + side].reshape(D, 256))
        for gr in range(NG):
            yield _wide(w[:, 2, gr, 2 * pair:2 * pair + 2].reshape(D, 256))
    yield from square(i["attn_w_o"][0])
    yield from mlp(1)
    yield from ple(1)
    yield from ffn(i["ffn1_w_in_2"][0], i["ffn1_w_out_2"][0])
    yield from square(i["s5_w_glu_2"][0])
    yield from ffn(i["ffn2_w_in_2"][0], i["ffn2_w_out_2"][0])
    for u in range(6):
        yield _wide(i["w_kv_2"][:, 256 * u:256 * (u + 1)])
    yield from ffn(i["ffn1_w_in_2"][1], i["ffn1_w_out_2"][1])
    heads = head_order()
    wq = i["w_qg_2"][0][:, :D].reshape(D, NH, HD)[:, heads].reshape(D, D)
    yield from square(wq)
    yield from square(i["w_o_2"][0].reshape(NH, HD, D)[heads].reshape(D, D))
    yield from ffn(i["ffn2_w_in_2"][1], i["ffn2_w_out_2"][1])


def _constants():
    c = np.zeros((P, NCON), np.float32)
    put = lambda name, v: c.__setitem__((slice(None), slice(CCOL[name], CCOL[name] + v.shape[1])), v)
    put("ident", np.eye(P, dtype=np.float32))
    put("half", np.kron(np.eye(2), np.ones((HD, HD))).astype(np.float32))
    q, k = np.arange(SEQ)[:, None], np.arange(SEQ)[None, :]
    near, far = [], []
    for window, dil in GROUPS:
        ok = (k <= q) & ((q - k) % dil == 0) & ((q - k) // dil <= window // dil)
        m = np.where(ok, 0.0, NEG).astype(np.float32)
        near.append(m[:P, :P])
        far.append(m[P:])
    put("mask0", np.concatenate(near, 1))
    put("mask1", np.concatenate(far, 1))
    tok = np.arange(P)[:, None] + P * np.arange(TT)[None, :]
    put("anyc", (tok >= CL - 1).astype(np.float32))
    half = ROPE // 2
    inv = np.float32(THETA) ** (np.float32(-2.0) * np.arange(half, dtype=np.float32) / np.float32(ROPE))
    f, s = np.zeros((P, 1), np.float32), np.zeros((P, 1), np.float32)
    f[:half, 0] = f[half:ROPE, 0] = inv
    s[:half], s[half:ROPE] = -1.0, 1.0
    put("invf", f)
    put("sgn", s)
    return c


def _onehot(dist):
    n = np.maximum(dist, 0)
    exact = NBUCKET // 2
    logv = np.log(np.maximum(n, 1).astype(np.float32) / exact) / np.float32(math.log(MAXDIST / exact))
    large = np.minimum(exact + (logv * (NBUCKET - exact)).astype(np.int32), NBUCKET - 1)
    bucket = np.where(dist < 0, NBUCKET, np.where(n < exact, n, large))
    return (np.arange(NBUCKET + 1).reshape((-1,) + (1,) * dist.ndim) == bucket).astype(np.float32)


def _features(v):
    return v.reshape(KC, P).T


def _states(v):
    v = v.reshape((ST, P) + v.shape[2:])
    return v.transpose((1, 0) + tuple(range(2, v.ndim)))


def _layout(i):
    heads = head_order()
    vec = np.concatenate(
        [_features(v) for v in (i["norm_mix"][0], i["norm_mlp"][0], i["norm_ple"][0], i["norm_mix"][1],
                                i["norm_mlp"][1], i["norm_ple"][1], i["norm_final"], i["ffn1_norm_2"][0],
                                i["mix_norm_2"][0], i["ffn2_norm_2"][0], i["kv_norm_2"], i["ffn1_norm_2"][1],
                                i["mix_norm_2"][1], i["ffn2_norm_2"][1], *i["sc_w_conv"][0], i["s5_d_2"][0].reshape(-1))]
        + [np.concatenate([v, v]).reshape(P, 1) for v in (i["q_norm_2"][0], i["k_norm_cmp_2"], i["k_norm_slc_2"],
                                                          i["k_norm_win_2"])]
        + [_states(i["s5_a_re_2"][0]), _states(i["s5_a_im_2"][0]),
           _states(np.broadcast_to(i["s5_log_dt_2"][0][:, None], (S5_G, S5_STATE)))], 1)
    tok = np.arange(SEQ).reshape(TT, 1, P)
    block_end = (np.arange(NCMP) * CS + CL - 1).reshape(1, NCMP, 1)
    gate_w = i["w_qg_2"][0][:, D:].reshape(D, NH, 3)[:, heads].transpose(0, 2, 1).reshape(KC, P, 3 * NH)
    twice = lambda v: np.concatenate([v, v], 0)
    return {
        "x": i["x"][0].T,
        "p": i["p"][:, 0].transpose(0, 2, 1),
        "positions": i["positions"],
        "weights": np.stack(list(_units(i))),
        "vec": vec,
        "con": _constants(),
        "s5b": np.stack([_states(i["s5_b_re_2"][0]), _states(i["s5_b_im_2"][0])], 1),
        "s5c": np.stack([_states(i["s5_c_re_2"][0].transpose(0, 2, 1)), _states(i["s5_c_im_2"][0].transpose(0, 2, 1))],
                        1),
        "rel_bias": i["rel_bias_2"][:, heads],
        "onehot": _onehot(SEQ - 1 - np.arange(NDIST)),
        "onehot_cmp": _onehot(tok - block_end).reshape(NBUCKET + 1, TT * NCMP, P),
        "cmp_w1": np.stack([twice(w.transpose(1, 0, 2)) for w in (i["cmp_k_w1_2"], i["cmp_v_w1_2"])]),
        "cmp_w2": np.stack([i["cmp_k_w2_2"], i["cmp_v_w2_2"]], 1),
        "cmp_pos": np.stack([twice(i["cmp_pos_k_2"].T), twice(i["cmp_pos_v_2"].T)], 1),
        "gate_w": gate_w.transpose(1, 0, 2),
    }


def kernel(**inputs):
    from concourse import bacc
    from concourse.bass_utils import run_bass_kernel_spmd

    nc = bacc.Bacc("TRN2", target_bir_lowering=False, num_devices=1)
    arrays, A = {}, {}
    for name, a in _layout({k: np.asarray(v) for k, v in inputs.items()}).items():
        arrays[f"in_{name}"] = np.ascontiguousarray(a)
        A[name] = nc.dram_tensor(f"in_{name}", arrays[f"in_{name}"].shape, mybir.dt.from_np(a.dtype),
                                 kind="ExternalInput").ap()
    A["e_table"] = nc.dram_tensor("e_table", [ST // EB, P, EB * 2 * SEQ], F32, kind="Internal").ap()
    A["bias_rows"] = nc.dram_tensor("bias_rows", [NH, P, NDIST], F32, kind="Internal").ap()
    A["out"] = nc.dram_tensor("out", [D, SEQ], F32, kind="ExternalOutput").ap()
    program(nc, A)
    r = run_bass_kernel_spmd(nc, [arrays], core_ids=[0])
    return np.ascontiguousarray(np.asarray(r.results[0]["out"]).T).reshape(1, SEQ, D)
```

```python
import math
from contextlib import ExitStack

import numpy as np

import concourse.bass as bass
from concourse import mybir

ALU = mybir.AluOpType
ACT = mybir.ActivationFunctionType
AX = mybir.AxisListType
F32 = mybir.dt.float32
F32R = mybir.dt.float32r
BF16 = mybir.dt.bfloat16
I32 = mybir.dt.int32

P = 128
SEQ = 256
D = 1024
KC = D // P
TT = SEQ // P
PAIRS = KC // 2
EPS = 1e-6
D_FF = 4096
MLP_PAIRS = D_FF // 256
D_FF2 = 2816
FFN_PAIRS = D_FF2 // 256
PLE = 256
UNIT = 2048
RING = 3

DH = 128
GROUPS = ((128, 1), (512, 4), (2048, 16))
NG = len(GROUPS)
HEADS = D // DH
HEAD_PAIRS = HEADS // 2
ROPE = DH // 4
THETA = 500000.0
SCALE = DH ** -0.5
NEG = -1e30

S5_CH, S5_STATE = 16, 64
S5_G = D // S5_CH
ST = S5_G * S5_STATE // P
EB = 4
LB, LSLOTS = 2, 4

NH, HD, KVH = 16, 64, 4
REP = NH // KVH
CL, CS = 32, 16
NCMP = (SEQ - CL) // CS + 1
NBUCKET, MAXDIST = 32, 128
NDIST = SEQ + P - 1
NSCALE = HD ** -0.5
NQ = NH // 2

STAGES = [("sc_in", 12), ("sc_out", 4), ("mlp0", 32), ("ple0", 5), ("qkv", 36), ("wo", 4), ("mlp1", 32),
          ("ple1", 5), ("ffn0", 33), ("glu", 4), ("ffn1", 33), ("kv", 6), ("ffn2", 33), ("qg", 4),
          ("nwo", 4), ("ffn3", 33)]
BASE = {}
_at = 0
for _name, _n in STAGES:
    BASE[_name] = _at
    _at += _n
NU = _at

R_IN, R_SC, R_MLP0, R_PLE0, R_WO, R_MLP1, R_PLE1, R_FIN, R_FFN0, R_GLU, R_FFN1, R_FFN2, R_NWO, R_FFN3 = range(14)
XUSE = [R_IN, R_SC, R_MLP0, R_PLE0, R_WO, R_MLP1, R_FIN, R_GLU, R_FFN1, "kv", R_FFN2, R_NWO]
XBUF = {R_IN: 0, R_SC: 0, R_MLP0: 1, R_PLE0: 0, R_WO: 0, R_MLP1: 1, R_FIN: 0, R_GLU: 0, R_FFN1: 1, "kv": 0,
        R_FFN2: 1, R_NWO: 1}
XBASE = {r: PAIRS * n for n, r in enumerate(XUSE)}
HID_BASE = {"mlp0": 0, "mlp1": 16, "ffn0": 32, "ffn1": 43, "ffn2": 54, "ffn3": 65}

VCOL = {}
_at = 0
for _name, _n in [("mix0", 8), ("mlp0", 8), ("ple0", 8), ("mix1", 8), ("mlp1", 8), ("ple1", 8), ("final", 8),
                  ("ffn0", 8), ("s5mix", 8), ("ffn1", 8), ("kvn", 8), ("ffn2", 8), ("nsamix", 8), ("ffn3", 8),
                  ("conv", 24), ("s5d", 8), ("qn", 1), ("kcn", 1), ("ksn", 1), ("kwn", 1),
                  ("are", ST), ("aim", ST), ("ldt", ST)]:
    VCOL[_name] = _at
    _at += _n
NVEC = _at
GAIN = {R_IN: "mix0", R_SC: "mlp0", R_MLP0: "ple0", R_PLE0: "mix1", R_WO: "mlp1", R_MLP1: "ple1",
        R_FIN: "ffn0", R_GLU: "ffn1", R_FFN1: "kvn", "kv": "ffn2", R_FFN2: "nsamix", R_NWO: "ffn3"}

CCOL = {}
_at = 0
for _name, _n in [("ident", P), ("half", P), ("mask0", NG * P), ("mask1", NG * SEQ), ("anyc", TT), ("invf", 1),
                  ("sgn", 1)]:
    CCOL[_name] = _at
    _at += _n
NCON = _at
TWO_PI_1 = 6.28125
TWO_PI_2 = float(np.float32(2 * math.pi - 6.28125))
TWO_PI_3 = 2 * math.pi - 6.28125 - TWO_PI_2
ROUND = 1.5 * 2.0 ** 23
S5_HALVINGS = 6


def head_order():
    return [(2 * a + half) * REP + r for a in range(KVH // 2) for r in range(REP) for half in range(2)]



SEM_NAMES = (
    "con_landed", "vec_landed", "h_landed", "misc_landed", "p_landed", "e_stored", "bias_stored",
    "tbl_landed", "cmpw_landed", "pos_landed", "wg_landed", "bias_in_landed", "out_stored",
    "hi_ready", "lo_ready", "unit_done",
    "fill_done",
    "h_ready", "xh_ready", "xl_ready", "sq_ready", "sq_used", "acc_done", "sum_ready", "var_ready", "rst_ready",
    "diag_ready", "bcast_ready", "rs_ready", "rs2_ready",
    "c_copied", "v_raw", "v_ready", "tap_done", "b_scaled", "y_ready", "y_hi", "y_lo",
    "relu_ready", "act_ready", "a_scaled", "b_gated", "silu_ready", "prod_ready", "hid_hi_ready", "hid_lo_ready",
    "p_hi_ready", "p_lo_ready", "gate_scaled", "gate_ready", "gated",
    "rope_step", "sin_ready", "rope_ready", "rope_rs", "swapped", "qk_main", "sin_part", "qk_ready", "v_copied",
    "s_done", "masked", "max_done", "bias_ready", "exp_done", "rden_ready", "pt_done", "pt_copied", "pv_done",
    "o_scaled", "ot_done", "o_hi", "o_lo",
    "sm_dve", "sm_act", "bb_ready", "bt_done", "bt_ready", "ct_ready", "e_step",
    "u5_ready", "bu_done", "turned", "summed", "drive", "z_ready", "turned_back", "y_done", "y_in", "gelu_done", "g_hi",
    "g_lo",
    "src_ready", "k_scaled", "k_sq", "k_sum", "k_mean", "k_ln", "k_exp", "k_step", "k_ready", "vs_ready", "blk_ready",
    "hid_done", "hid_copied", "hid_turned", "hg_ready", "w2_done", "vc_ready", "bv_done", "bv_copied", "cb_ready",
    "rel_ready",
    "wg_hi_ready", "wg_lo_ready", "gate_done", "gate_sig", "gate_all", "n_s", "n_log",
    "n_max", "n_exp", "n_rec", "n_fac", "n_t", "n_ta", "n_tv", "n_pv", "n_part", "n_ot", "n_hi", "n_lo",
)


S5_R = 27


def program(nc, A):
    with ExitStack() as ctx:
        def sb(name, shape, dt=F32, scope=ctx):
            return scope.enter_context(nc.sbuf_tensor(name, shape, dt))

        raw = sb("raw", [P, RING, UNIT])
        w_hi = sb("w_hi", [P, RING, UNIT], F32R)
        w_lo = sb("w_lo", [P, RING, UNIT], F32R)
        x_hi = [sb(f"x_hi{i}", [P, KC, SEQ], F32R) for i in range(2)]
        x_lo = [sb(f"x_lo{i}", [P, KC, SEQ], F32R) for i in range(2)]
        h = sb("h", [P, KC, SEQ])
        vec = sb("vec", [P, NVEC])
        con = sb("con", [P, NCON])
        rs = sb("rs", [P, 2, SEQ])
        rs_tok = sb("rs_tok", [P, TT])
        var_tok = sb("var_tok", [P, TT])
        diag = sb("diag", [P, TT, P])
        sq = sb("sq", [P, 2, 2, SEQ])
        ssum = sb("ssum", [P, 2, SEQ])
        ones = sb("ones", [P, P])
        nhalf = sb("nhalf", [P, TT])
        zero = sb("zero", [P, 512], BF16)
        ta = sb("ta", [P, 2, SEQ])
        tb = sb("tb", [P, 2, SEQ])
        tc = sb("tc", [P, 2, SEQ])
        halfpi = sb("halfpi", [P, 1])
        hid_hi = sb("hid_hi", [P, 2, SEQ], F32R)
        hid_lo = sb("hid_lo", [P, 2, SEQ], F32R)

        with ExitStack() as first:
            p_in = sb("p_in", [P, 2, SEQ], scope=first)
            p_hi = sb("p_hi", [P, 2, SEQ], F32R, scope=first)
            p_lo = sb("p_lo", [P, 2, SEQ], F32R, scope=first)
            bt = sb("bt", [P, KC, 2, P], scope=first)
            ct = sb("ct", [P, 3, ST, 32], scope=first)
            mag = sb("mag", [P, ST], scope=first)
            with ExitStack() as s:
                vp = sb("vp", [P, 2, SEQ + 2], scope=s)
                yc = sb("yc", [P, 2, SEQ], scope=s)
                rs2 = sb("rs2", [P, 2, SEQ], scope=s)
                e_tab = sb("e_tab", [P, EB, 2, SEQ], scope=s)
                e_t1 = sb("e_t1", [P, EB, 2, P], scope=s)
                e_t2 = sb("e_t2", [P, EB, 2, P], scope=s)
                e_one = sb("e_one", [P, ST, 2], scope=s)
                s5b = sb("s5b", [P, 2, ST, S5_CH], scope=s)
                bb = sb("bb", [P, 2, ST, 32], scope=s)
                sm = sb("sm", [P, 16, ST], scope=s)
            with ExitStack() as s:
                posi = sb("posi", [P, SEQ], I32, scope=s)
                ang = sb("ang", [P, 3, SEQ], scope=s)
                rope_c = sb("rope_c", [P, SEQ], scope=s)
                rope_s = sb("rope_s", [P, SEQ], scope=s)
                cos_rs = sb("cos_rs", [P, SEQ], scope=s)
                sin_rs = sb("sin_rs", [P, SEQ], scope=s)
                swap = sb("swap", [32, 2, SEQ], scope=s)
                qk = sb("qk", [P, 2, NG, 2, SEQ], scope=s)
                vv = sb("vv", [P, TT, NG, 2 * DH], scope=s)
                lg0 = sb("lg0", [P, NG, P], scope=s)
                lg1 = sb("lg1", [P, NG, SEQ], scope=s)
                pt = sb("pt", [P, 3, 3 * P], scope=s)
                nmax = sb("nmax", [P, TT], scope=s)
                nbias = sb("nbias", [P, TT], scope=s)
                den = sb("den", [P, TT], scope=s)
                rden = sb("rden", [P, TT], scope=s)
                ot = sb("ot", [P, TT, DH], scope=s)
            with ExitStack() as s:
                e_ring = sb("e_ring", [P, LSLOTS, LB, 2, SEQ], scope=s)
                u5 = sb("u5", [P, KC, SEQ], scope=s)
                y5 = sb("y5", [P, KC, SEQ], scope=s)
                z5 = sb("z5", [P, 2, 2, SEQ], scope=s)
                n1 = [sb("n1", [P, 2, SEQ], scope=s), p_in]
                n2 = [sb(f"n2{i}", [P, 2, SEQ], scope=s) for i in range(2)]
        with ExitStack() as s:
            src = sb("src", [P, 2, 2, SEQ], scope=s)
            ks = sb("ks", [P, 2, 2, SEQ], scope=s)
            vs = sb("vs", [P, 2, TT, KVH * HD], scope=s)
            kcmp = sb("kcmp", [P, 2, NCMP], scope=s)
            vcmp = sb("vcmp", [NCMP, KVH, HD], scope=s)
            cmp_bias = sb("cmp_bias", [P, TT * NCMP, NH], scope=s)
            tbl = sb("tbl", [P, NH, SEQ], scope=s)
            gate = sb("gate", [P, TT, 3 * NH], scope=s)
            with ExitStack() as t:
                w1 = sb("w1", [P, CL, 2 * HD], scope=t)
                blk = sb("blk", [P, CL, 2, NCMP], scope=t)
                w2 = sb("w2", [P, 2, HD], scope=t)
                hg = sb("hg", [P, 2, 2 * NCMP], scope=t)
                hraw = sb("hraw", [2 * NCMP, 2, P], scope=t)
                posc = sb("posc", [P, 2, CL], scope=t)
                rel = sb("rel", [NBUCKET + 1, NH], scope=t)
                oh = sb("oh", [NBUCKET + 1, NDIST], scope=t)
                bv = sb("bv", [NH, NDIST], scope=t)
            with ExitStack() as t:
                q2 = sb("q2", [P, NQ, SEQ], scope=t)
                wg = sb("wg", [P, KC, 3 * NH], scope=t)
                wg_hi = sb("wg_hi", [P, KC, 3 * NH], F32R, scope=t)
                wg_lo = sb("wg_lo", [P, KC, 3 * NH], F32R, scope=t)
                lg = sb("lg", [P, 2, 2, 3 * P], scope=t)
                lgc = sb("lgc", [P, 2, TT, NCMP], scope=t)
                ptn = sb("ptn", [P, 2, 2, 3 * P], scope=t)
                ptc = sb("ptc", [NCMP, 2, SEQ], scope=t)
                nm = sb("nm", [P, 2, 3, TT], scope=t)
                dn = sb("dn", [P, 2, 3, TT], scope=t)
                fac = sb("fac", [P, 2, 3, TT], scope=t)
                oc = sb("oc", [P, 2, TT, 2, HD], scope=t)

        w1v = tbl[:].rearrange("p n k -> p (n k)").rearrange("p (l d) -> p l d", l=CL)

        spare = lg[:].rearrange("p b r k -> p (b r k)")

        def norm_buffers(n, width):
            if n > 4 and n % 2:
                flat = [spare[:, 512 * i:512 * i + 512] for i in range(3)] + [sq[:, 1].rearrange("p c t -> p (c t)")]
            else:
                flat = [t_.rearrange("p c t -> p (c t)") for t_ in (ta[:], tb[:], tc[:], sq[:, 0])]
            return [t_[:, 0:width] for t_ in flat]

        psum = ctx.enter_context(nc.psum_tensor("psum", [P, 8, 512], F32))
        DB = [psum[:, b] for b in range(4)]
        U = [psum[:, 4], psum[:, 5]]
        MB = psum[:, 6]
        XB = psum[:, 7]
        U3 = [U[0], U[1], XB]

        def two(ap):
            return ap.rearrange("p (c t) -> p c t", c=2)

        sem = {name: ctx.enter_context(nc.semaphore(name)) for name in SEM_NAMES}
        e_landed = [ctx.enter_context(nc.semaphore(f"e_landed{i}")) for i in range(LSLOTS)]
        raw_landed = [ctx.enter_context(nc.semaphore(f"raw_landed{i}")) for i in range(RING)]

        def col(name, c=0, n=1):
            return vec[:, VCOL[name] + c:VCOL[name] + c + n]

        def cst(name, n):
            return con[:, CCOL[name]:CCOL[name] + n]

        ident = cst("ident", P)

        def hbase(r):
            return PAIRS * (r - 1)

        def chunk(ap, c, n=1):
            return ap[:, bass.ds(c, n), :]

        block = ctx.enter_context(nc.Block())

        @block.sync
        def _(sp):
            for u in range(RING):
                sp.dma_start(raw[:, u], A["weights"][u]).then_inc(raw_landed[u], 16)
                if u == 0:
                    sp.wait_ge(sem["h_landed"], 16 * PAIRS)
                    sp.dma_start(con[:], A["con"]).then_inc(sem["con_landed"], 16)
            full = NU // RING
            with sp.Fori(1, full) as k:
                for u in range(RING):
                    sp.wait_ge(sem["lo_ready"], RING * k + (u + 1 - RING))
                    sp.dma_start(raw[:, u:u + 1], A["weights"][bass.ds(RING * k + u, 1)]
                                 .rearrange("o p n -> p o n")).then_inc(raw_landed[u], 16)
            for g in range(RING * full, NU):
                sp.wait_ge(sem["lo_ready"], g + 1 - RING)
                sp.dma_start(raw[:, g % RING], A["weights"][g]).then_inc(raw_landed[g % RING], 16)
            out_v = A["out"].rearrange("(c p) t -> p c t", p=P)
            for m in range(PAIRS):
                sp.wait_ge(sem["h_ready"], hbase(R_FFN3) + m + 1)
                sp.dma_start(out_v[:, 2 * m:2 * m + 2, :], h[:, 2 * m:2 * m + 2, :]).then_inc(sem["out_stored"], 16)
            sp.wait_ge(sem["out_stored"], 16 * PAIRS)

        @block.tensor
        def _(pe):
            def exact(out, a, b, start, stop):
                (a_hi, a_lo), (b_hi, b_lo) = a, b
                nc.tensor.matmul(out, a_hi, b_hi, start=start, stop=False, skip_group_check=True)
                nc.tensor.matmul(out, a_hi, b_lo, start=False, stop=False, skip_group_check=True)
                return nc.tensor.matmul(out, a_lo, b_hi, start=False, stop=stop, skip_group_check=True)

            def slot(g0):
                s = g0 % RING
                return w_hi[:, s], w_lo[:, s]

            def wide(ws, c, m):
                return tuple(w[:, c * 256 + m * P:c * 256 + (m + 1) * P] for w in ws)

            RES = {"sc_out": R_SC, "wo": R_WO, "glu": R_GLU, "nwo": R_NWO}
            PB = [XB, DB[0], DB[1], DB[2]]

            def up_unit(g0, k, x, bank, arrive=None, mid=None):
                pe.wait_ge(sem["lo_ready"], g0 + 1 + RING * k)
                ws = slot(g0)
                for m in range(2):
                    for c in range(KC):
                        if arrive is not None and m == 0 and c % 2 == 0:
                            pe.wait_ge(arrive[0], arrive[1] + arrive[2] * (c // 2 + 1))
                        last = exact(bank[:, m * SEQ:(m + 1) * SEQ], wide(ws, c, m),
                                     (x_hi[x][:, c], x_lo[x][:, c]), c == 0, c == KC - 1)
                    if m == 0 and mid is not None:
                        mid()
                last.then_inc(sem["unit_done"], 1)

            def token_unit(g0, k, x, bank, mid=None):
                pe.wait_ge(sem["lo_ready"], g0 + 1 + RING * k)
                wh, wl = slot(g0)
                for t in range(TT):
                    for c in range(KC):
                        last = exact(bank[:, t * 256:(t + 1) * 256],
                                     tuple(xx[x][:, c, t * P:(t + 1) * P] for xx in (x_hi, x_lo)),
                                     (wh[:, c * 256:(c + 1) * 256], wl[:, c * 256:(c + 1) * 256]),
                                     c == 0, c == KC - 1)
                    if t == 0 and mid is not None:
                        mid()
                last.then_inc(sem["unit_done"], 1)

            def down_unit(g0, k, hid_count, tell=False):
                pe.wait_ge(sem["lo_ready"], g0 + 1 + RING * k)
                pe.wait_ge(sem["hid_lo_ready"], hid_count)
                wh, wl = slot(g0)
                for m in range(KC):
                    for c in range(2):
                        cols = slice(c * D + m * P, c * D + (m + 1) * P)
                        last = exact(DB[m // 2][:, (m % 2) * SEQ:(m % 2 + 1) * SEQ], (wh[:, cols], wl[:, cols]),
                                     (hid_hi[:, c], hid_lo[:, c]), False, c == 1)
                    if tell and m % 2 and m < KC - 1:
                        last.then_inc(sem["acc_done"], 1)
                last.then_inc(sem["unit_done"], 1)

            def clear_sums():
                for b in range(4):
                    nc.tensor.matmul(DB[b], zero[:, 0:P], zero[:], start=True, stop=False, skip_group_check=True)

            def keep_warm(n, bank):
                for _ in range(n):
                    nc.tensor.matmul(bank, zero[:, 0:P], zero[:], start=True, stop=True, skip_group_check=True)

            def norm_sum(n):
                pe.wait_ge(sem["sq_used"], 3 * (n + 1))
                pe.wait_ge(sem["rs_ready"], n)
                for t in range(TT):
                    for q in range(2):
                        last = nc.tensor.matmul(MB[:, t:t + 1], ssum[:, q, t * P:(t + 1) * P], ones[:, 0:1],
                                                start=q == 0, stop=q == 1, skip_group_check=True)
                last.then_inc(sem["sum_ready"], 1)

            def norm_bcast(n):
                pe.wait_ge(sem["diag_ready"], n + 1)
                nc.tensor.matmul(MB[:, SEQ:2 * SEQ], ones[:], diag[:].rearrange("p t q -> p (t q)"),
                                 start=True, stop=True, skip_group_check=True).then_inc(sem["bcast_ready"], 1)

            def residual_units(stage, x, arrive, mid=None):
                for m in range(PAIRS):
                    if m >= 2:
                        pe.wait_ge(sem["h_ready"], hbase(RES[stage]) + m - 1)
                    up_unit(BASE[stage] + m, 0, x, U[m % 2], arrive if m == 0 else None, mid if m == 0 else None)
                pe.wait_ge(sem["h_ready"], hbase(RES[stage]) + PAIRS - 1)

            def turn_b():
                pe.wait_ge(sem["bb_ready"], 4)
                pe.wait_ge(sem["relu_ready"], MLP_PAIRS)
                for b in range(4):
                    for i in range(4):
                        n_ = 4 * b + i
                        last = nc.tensor.transpose([MB, XB, U[1], U[0]][b][:, i * P:(i + 1) * P],
                                                   bb[:, n_ % 2, 4 * (n_ // 2):4 * (n_ // 2) + 4, :]
                                                   .rearrange("p j q -> p (j q)"), ident)
                    last.then_inc(sem["bt_done"], 1)

            def mlp(l, n):
                name = f"mlp{l}"
                g, hb, x = BASE[name], HID_BASE[name], XBUF[n]
                up_unit(g, 0, x, U[0], (sem["xl_ready"], XBASE[n], 1), lambda: norm_sum(n))
                norm_bcast(n)
                clear_sums()
                keep_warm(14, XB)
                with pe.Fori(0, (MLP_PAIRS - 1) // RING) as k:
                    for t in range(RING):
                        pe.wait_ge(sem["relu_ready"], MLP_PAIRS * l + RING * k + t + 1)
                        up_unit(g + 1 + 2 * t, 2 * k, x, U[0])
                        down_unit(g + 2 + 2 * t, 2 * k, hb + RING * k + t + 1)
                if l == 0:
                    turn_b()
                down_unit(g + 2 * MLP_PAIRS - 1, 0, hb + MLP_PAIRS, tell=True)

            def bias_tables():
                pe.wait_ge(sem["bias_in_landed"], 32)
                pe.wait_ge(sem["rel_ready"], 1)
                nc.tensor.matmul(XB[0:NH, 0:NDIST], rel[:], oh[:], start=True, stop=True,
                                 skip_group_check=True).then_inc(sem["bv_done"], 1)

            def ffn(f, n, normed=True, r=None):
                name = f"ffn{f}"
                r = n if r is None else r
                g, hb, x = BASE[name], HID_BASE[name], XBUF[r]
                up_unit(g, 0, x, U[0], (sem["xl_ready"], XBASE[r], 1), (lambda: norm_sum(n)) if normed else None)
                if normed:
                    norm_bcast(n)
                up_unit(g + 1, 0, x, U[1])
                clear_sums()
                keep_warm(8, XB)
                with pe.Fori(0, FFN_PAIRS - 1) as k:
                    pe.wait_ge(sem["a_scaled"], FFN_PAIRS * f + k + 1)
                    up_unit(g + 2, k, x, U[0])
                    pe.wait_ge(sem["b_gated"], FFN_PAIRS * f + k + 1)
                    up_unit(g + 3, k, x, U[1])
                    down_unit(g + 4, k, hb + k + 1)
                if f == 1:
                    bias_tables()
                down_unit(g + 3 * FFN_PAIRS - 1, 0, hb + FFN_PAIRS, tell=True)

            def ple(l, n):
                name = f"ple{l}"
                g = BASE[name]
                pe.wait_ge(sem["lo_ready"], g + 1)
                pe.wait_ge(sem["p_lo_ready"], l + 1)
                pe.wait_ge(sem["bt_ready"], 4)
                wh, wl = slot(g)
                for m in range(PAIRS):
                    if m:
                        pe.wait_ge(sem["h_ready"], hbase(n) + m)
                    for q in range(2):
                        for c in range(2):
                            cols = slice(c * D + (2 * m + q) * P, c * D + (2 * m + q + 1) * P)
                            last = exact(PB[m][:, q * SEQ:(q + 1) * SEQ], (wh[:, cols], wl[:, cols]),
                                         (p_hi[:, c], p_lo[:, c]), c == 0, c == 1)
                last.then_inc(sem["unit_done"], 1)
                for m in range(PAIRS):
                    if m >= 2:
                        pe.wait_ge(sem["gate_scaled"], PAIRS * l + m - 1)
                    if m == 1:
                        norm_bcast(n)
                    up_unit(g + 1 + m, 0, XBUF[n], U[m % 2], (sem["xl_ready"], XBASE[n], 1) if m == 0 else None,
                            (lambda: norm_sum(n)) if m == 0 else None)
                pe.wait_ge(sem["gate_scaled"], PAIRS * (l + 1) - 1)

            pe.wait_ge(sem["fill_done"], 4)
            keep_warm(36, XB)
            n = R_IN

            def conv_triple(g0, k, j, first):
                if not first:
                    pe.wait_ge(sem["c_copied"], j)
                up_unit(g0, k, 0, U[0], (sem["xl_ready"], XBASE[n], 1) if first else None,
                        (lambda: norm_sum(n)) if first else None)
                if first:
                    norm_bcast(n)
                else:
                    pe.wait_ge(sem["v_raw"], j)
                up_unit(g0 + 1, k, 0, U[1])
                if not first:
                    pe.wait_ge(sem["b_scaled"], j)
                up_unit(g0 + 2, k, 0, XB)

            conv_triple(0, 0, 0, True)
            with pe.Fori(0, PAIRS - 1) as k:
                conv_triple(3, k, k + 1, False)
            pe.wait_ge(sem["c_copied"], PAIRS)
            residual_units("sc_out", 1, (sem["y_lo"], 0, 1))

            mlp(0, R_SC)
            ple(0, R_MLP0)

            n = R_PLE0
            g = BASE["qkv"]
            TBK = [DB[3], MB]

            def turn(hd, side, b):
                if b == 0:
                    pe.wait_ge(sem["exp_done"], 2 * (hd + 1))
                pe.wait_ge(sem["pt_copied"], 3 * hd + b - 1 if side or b else 3 * hd)
                for gr in range(NG):
                    part = lg0[:, gr, :] if b == 0 else lg1[:, gr, (b - 1) * P:b * P]
                    last = nc.tensor.transpose(TBK[(NG * side + b) % 2][:, gr * P:(gr + 1) * P], part, ident)
                last.then_inc(sem["pt_done"], 1)

            def values(hd, side):
                pe.wait_ge(sem["pt_copied"], 3 * (hd + 1))
                pe.wait_ge(sem["o_scaled"], 2 * hd)
                if side:
                    pe.wait_ge(sem["o_lo"], hd)
                else:
                    pe.wait_ge(sem["masked"], 2 * (hd + 2))
                dims = slice(side * DH, (side + 1) * DH)
                for gr in range(NG):
                    nc.tensor.matmul(DB[2][:, SEQ:SEQ + DH], pt[:, 0, gr * P:(gr + 1) * P], vv[:, 0, gr, dims],
                                     start=gr == 0, stop=gr == NG - 1, skip_group_check=True)
                for b in range(2):
                    for gr in range(NG):
                        last = nc.tensor.matmul(DB[2][:, SEQ + DH:SEQ + 2 * DH], pt[:, 1 + b, gr * P:(gr + 1) * P],
                                                vv[:, b, gr, dims], start=b == 0 and gr == 0,
                                                stop=b == 1 and gr == NG - 1, skip_group_check=True)
                last.then_inc(sem["pv_done"], 1)

            def turn_out(hd):
                pe.wait_ge(sem["o_scaled"], 2 * (hd + 1))
                for t in range(TT):
                    last = nc.tensor.transpose(DB[2][:, t * P:(t + 1) * P], ot[:, t, :], ident)
                last.then_inc(sem["ot_done"], 1)

            def scores_of(i, side):
                pe.wait_ge(sem["qk_ready"], 6 * i + 3 * side + 3)
                hd = 2 * i + side
                pe.wait_ge(sem["masked"], 2 * hd)
                if side == 0:
                    pe.wait_ge(sem["o_lo"], hd)
                for gr in range(NG):
                    nc.tensor.matmul(DB[0][:, gr * P:(gr + 1) * P], qk[:, side, gr, 0, 0:P], qk[:, side, gr, 1, 0:P],
                                     start=True, stop=True, skip_group_check=True)
                for gr in range(NG):
                    bank = DB[1 + gr // 2][:, (gr % 2) * SEQ:(gr % 2 + 1) * SEQ]
                    last = nc.tensor.matmul(bank, qk[:, side, gr, 0, P:SEQ], qk[:, side, gr, 1, :],
                                            start=True, stop=True, skip_group_check=True)
                last.then_inc(sem["s_done"], 1)

            def attend(i, u):
                a, b = 2 * i, 2 * i + 1
                if u == 0:
                    scores_of(i, 1)
                    turn(a, 0, 0)
                    turn(a, 0, 1)
                elif u == 1:
                    turn(a, 0, 2)
                elif u == 2:
                    values(a, 0)
                    turn(b, 1, 0)
                elif u == 3:
                    turn(b, 1, 1)
                    turn_out(a)
                elif u == 4:
                    turn(b, 1, 2)
                elif u == 5:
                    values(b, 1)
                elif u == 6:
                    turn_out(b)

            def qkv_units(k, i, before, first):
                for u in range(9):
                    bank = U3[u % 3]
                    if not first:
                        if u < 3:
                            pe.wait_ge(sem["v_copied"], 3 * i + u - 2)
                        else:
                            pe.wait_ge(sem["swapped"], 6 * i + u - 2)
                    elif u >= 3:
                        pe.wait_ge(sem["swapped"], u - 2)
                    if u < 6:
                        up_unit(g + u, k, XBUF[n], bank, (sem["xl_ready"], XBASE[n], 1) if first and u == 0 else None,
                                (lambda: norm_sum(n)) if first and u == 0 else None)
                        if first and u == 0:
                            norm_bcast(n)
                    else:
                        token_unit(g + u, k, XBUF[n], bank)
                    if before is not None:
                        attend(before, u)

            qkv_units(0, 0, None, True)
            with pe.Fori(0, HEAD_PAIRS - 1) as k:
                scores_of(k, 0)
                qkv_units(3 * k + 3, k + 1, k, False)
            scores_of(HEAD_PAIRS - 1, 0)
            pe.wait_ge(sem["v_copied"], 3 * HEAD_PAIRS)
            for u in range(7):
                attend(HEAD_PAIRS - 1, u)
            residual_units("wo", 1, (sem["o_lo"], 0, 2))

            mlp(1, R_WO)
            ple(1, R_MLP1)

            keep_warm(28, DB[3])
            norm_sum(R_PLE1)
            keep_warm(10, DB[3])
            norm_bcast(R_PLE1)
            keep_warm(12, DB[3])
            ffn(0, R_FIN)

            keep_warm(20, XB)
            norm_sum(R_FFN0)
            keep_warm(6, XB)
            norm_bcast(R_FFN0)
            keep_warm(6, XB)

            def drive(j):
                c, q = j // 4, 32 * (j % 4)
                pe.wait_ge(sem["u5_ready"], c + 1)
                if j >= 4:
                    pe.wait_ge(sem["drive"], j - 3)
                for ri in range(2):
                    last = nc.tensor.matmul([U[0], U[1], XB, MB][j % 4][:, ri * SEQ:(ri + 1) * SEQ], bt[q:q + 32, c, ri, :],
                                            u5[q:q + 32, c, :], start=True, stop=True, skip_group_check=True)
                last.then_inc(sem["bu_done"], 1)

            def outputs(j):
                c, q = j // 4, 32 * (j % 4)
                pe.wait_ge(sem["turned_back"], 2 * (j + 1))
                if c >= 4 and j % 4 == 0:
                    pe.wait_ge(sem["y_in"], c - 3)
                out = DB[c % 4][q:q + 32, 0:SEQ]
                nc.tensor.matmul(out, ct[:, 0, j, :], n1[j % 2][:, 0], start=True, stop=False, skip_group_check=True)
                nc.tensor.matmul(out, ct[:, 1, j, :], n2[j % 2][:, 0], start=False, stop=False, skip_group_check=True)
                nc.tensor.matmul(out, ct[:, 2, j, :], n1[j % 2][:, 1], start=False, stop=False, skip_group_check=True)
                nc.tensor.matmul(out, ct[:, 2, j, :], n2[j % 2][:, 1], start=False, stop=True,
                                 skip_group_check=True).then_inc(sem["y_done"], 1)

            drive(0)
            drive(1)
            drive(2)
            for j in range(ST):
                if j + 3 < ST:
                    drive(j + 3)
                if j == 0:
                    keep_warm(20, DB[3])
                outputs(j)
            residual_units("glu", 1, (sem["g_lo"], 0, 2))
            ffn(1, R_GLU)

            n, g, x = R_FFN1, BASE["kv"], XBUF[R_FFN1]

            def head_sum(count, width):
                pe.wait_ge(sem["k_sq"], count)
                nc.tensor.matmul(XB[:, 0:width], cst("half", P), norm_buffers(count, width)[1],
                                 start=True, stop=True, skip_group_check=True).then_inc(sem["k_sum"], 1)

            def compress(kind):
                pe.wait_ge(sem["blk_ready"], kind + 1)
                pe.wait_ge(sem["cmpw_landed"], 64)
                for l in range(CL):
                    for half in range(2):
                        rows = slice(half * HD, (half + 1) * HD)
                        last = nc.tensor.matmul([MB, U[0]][half][0:2 * NCMP, 0:P],
                                                blk[rows, l, :, :].rearrange("p c n -> p (c n)"),
                                                [w1, w1v][kind][rows, l, :],
                                                start=l == 0, stop=l == CL - 1, skip_group_check=True)
                        if l == CL - 1:
                            last.then_inc(sem["hid_done"], 1)
                pe.wait_ge(sem["hid_copied"], kind + 1)
                for half in range(2):
                    last = nc.tensor.transpose(MB[:, half * 2 * NCMP:(half + 1) * 2 * NCMP],
                                               hraw[:, half, :], ident[0:2 * NCMP, 0:2 * NCMP])
                last.then_inc(sem["hid_turned"], 1)

            up_unit(g, 0, x, U[0], (sem["xl_ready"], XBASE[n], 1), lambda: norm_sum(n))
            norm_bcast(n)
            up_unit(g + 1, 0, x, U[1])
            pe.wait_ge(sem["src_ready"], 1)
            up_unit(g + 2, 0, x, U[0])
            pe.wait_ge(sem["src_ready"], 2)
            token_unit(g + 3, 0, x, U[1])
            pe.wait_ge(sem["bv_copied"], 1)
            head_sum(1, 512)
            pe.wait_ge(sem["k_scaled"], 1)
            up_unit(g + 4, 0, x, U[0])
            pe.wait_ge(sem["vs_ready"], 1)
            token_unit(g + 5, 0, x, U[1])
            head_sum(2, 512)
            compress(0)
            keep_warm(10, U[1])
            pe.wait_ge(sem["hg_ready"], 1)
            for half in range(2):
                rows = slice(half * HD, (half + 1) * HD)
                last = nc.tensor.matmul(MB[rows, 128:128 + 2 * NCMP], w2[:, 0, :], hg[:, half, :],
                                        start=True, stop=True, skip_group_check=True)
            last.then_inc(sem["w2_done"], 1)
            head_sum(3, 2 * NCMP)
            keep_warm(6, U[1])
            compress(1)
            keep_warm(4, U[1])
            pe.wait_ge(sem["hg_ready"], 2)
            for kh in range(KVH):
                a, half = kh // 2, kh % 2
                last = nc.tensor.matmul(MB[0:NCMP, 256 + kh * HD:256 + (kh + 1) * HD],
                                        hg[:, half, a * NCMP:(a + 1) * NCMP], w2[:, 1, :],
                                        start=True, stop=True, skip_group_check=True)
            last.then_inc(sem["w2_done"], 1)
            ffn(2, R_FFN1, normed=False, r="kv")

            n, g, x = R_FFN2, BASE["qg"], XBUF[R_FFN2]
            for u in range(4):
                if u >= 2:
                    pe.wait_ge(sem["k_scaled"], u + 2)

                def between(u=u):
                    if u == 0:
                        norm_sum(n)
                    else:
                        head_sum(3 + u, 512)
                up_unit(g + u, 0, x, U[u % 2], (sem["xl_ready"], XBASE[n], 1) if u == 0 else None, between)
                if u == 0:
                    norm_bcast(n)
                    keep_warm(8, DB[3])
            keep_warm(10, DB[3])
            pe.wait_ge(sem["wg_lo_ready"], 1)
            pe.wait_ge(sem["k_scaled"], 6)
            for t in range(TT):
                for c in range(KC):
                    last = exact(U[0][:, t * 64:t * 64 + 3 * NH],
                                 tuple(xx[x][:, c, t * P:(t + 1) * P] for xx in (x_hi, x_lo)),
                                 (wg_hi[:, c, :], wg_lo[:, c, :]), c == 0, c == KC - 1)
            last.then_inc(sem["gate_done"], 1)
            head_sum(7, 512)
            keep_warm(28, DB[3])

            pe.wait_ge(sem["gate_all"], 1)
            pe.wait_ge(sem["k_ready"], 7)

            def n_scores(hd):
                if hd >= 2:
                    pe.wait_ge(sem["n_log"], hd - 1)
                b, a, rows = hd % 2, hd // 8, slice((hd % 2) * HD, (hd % 2 + 1) * HD)
                q = q2[rows, hd // 2]
                for br in range(2):
                    bank = DB[2 * br + b]
                    nc.tensor.matmul(bank[:, 0:P], q[:, 0:P], ks[rows, br, a, 0:P], start=True, stop=True,
                                     skip_group_check=True)
                    nc.tensor.matmul(bank[:, P:P + SEQ], q[:, P:SEQ], ks[rows, br, a, :], start=True, stop=True,
                                     skip_group_check=True)
                for t in range(TT):
                    last = nc.tensor.matmul(DB[b][:, 3 * P + t * NCMP:3 * P + (t + 1) * NCMP],
                                            q[:, t * P:(t + 1) * P], kcmp[rows, a, :], start=True, stop=True,
                                            skip_group_check=True)
                last.then_inc(sem["n_s"], 1)

            def n_turn(hd):
                b = hd % 2
                if hd >= 2:
                    pe.wait_ge(sem["n_lo"], hd // 2)
                if hd:
                    pe.wait_ge(sem["n_tv"], hd)
                    pe.wait_ge(sem["n_ta"], hd)
                keep_warm(3 if hd else 16, U[0])
                pe.wait_ge(sem["n_exp"], hd + 1)
                for br in range(2):
                    for j in range(3):
                        last = nc.tensor.transpose(U[br][:, j * P:(j + 1) * P], lg[:, b, br, j * P:(j + 1) * P],
                                                   ident)
                for t in range(TT):
                    last = nc.tensor.transpose(MB[0:NCMP, t * P:(t + 1) * P], lgc[:, b, t, :], ident)
                last.then_inc(sem["n_t"], 1)

            def n_values(hd):
                b, kh = hd % 2, 2 * (hd // 8) + hd % 2
                if hd:
                    pe.wait_ge(sem["n_part"], 3 * hd)
                pe.wait_ge(sem["n_tv"], hd + 1)
                pe.wait_ge(sem["n_ta"], hd + 1)
                dims = slice(kh * HD, (kh + 1) * HD)

                def out(br, t):
                    at = (br * TT + t) * HD
                    return XB[:, at:at + HD]
                for t in range(TT):
                    nc.tensor.matmul(out(0, t), ptc[:, b, t * P:(t + 1) * P], vcmp[:, kh, :], start=True, stop=True,
                                     skip_group_check=True)
                for br in range(2):
                    pb_ = ptn[:, b, br]
                    nc.tensor.matmul(out(1 + br, 0), pb_[:, 0:P], vs[:, br, 0, dims], start=True, stop=True,
                                     skip_group_check=True)
                    nc.tensor.matmul(out(1 + br, 1), pb_[:, P:2 * P], vs[:, br, 0, dims], start=True, stop=False,
                                     skip_group_check=True)
                    last = nc.tensor.matmul(out(1 + br, 1), pb_[:, 2 * P:3 * P], vs[:, br, 1, dims], start=False,
                                            stop=True, skip_group_check=True)
                last.then_inc(sem["n_pv"], 1)

            def n_turn_out(ch):
                pe.wait_ge(sem["n_part"], 6 * ch + 6)
                if ch:
                    pe.wait_ge(sem["n_lo"], ch)
                for t in range(TT):
                    last = nc.tensor.transpose(MB[:, SEQ + t * P:SEQ + (t + 1) * P],
                                               oc[:, ch % 2, t].rearrange("p e d -> p (e d)"), ident)
                last.then_inc(sem["n_ot"], 1)

            n_scores(0)
            for step in range(NH + 1):
                if step:
                    n_turn(step - 1)
                if step + 1 < NH:
                    n_scores(step + 1)
                if step:
                    n_values(step - 1)
                if step and step % 2 == 0:
                    n_turn_out(step // 2 - 1)
            residual_units("nwo", 0, (sem["n_lo"], 0, 2))
            ffn(3, R_NWO)

        @block.scalar
        def _(act):
            copy = lambda out, in_, **kw: nc.scalar.activation(out, in_, ACT.Copy, **kw)

            def done(g0, k=0):
                act.wait_ge(sem["unit_done"], g0 + 1 + RING * k)

            def split(g0, k=0):
                g = g0 + RING
                if isinstance(k, int) and g + RING * k >= NU:
                    return
                act.wait_ge(sem["unit_done"], g0 + 1 + RING * k)
                act.wait_ge(raw_landed[g % RING], 16 * (g // RING + 1) + 16 * k)
                copy(w_hi[:, g % RING], raw[:, g % RING]).then_inc(sem["hi_ready"], 1)

            def x_high(r, m, waits=True):
                for q in range(2):
                    c = 2 * m + q
                    last = copy(x_hi[XBUF[r]][:, c], h[:, c], scale=col(GAIN[r], c))
                last.then_inc(sem["xh_ready"], 1)

            def squares(r, m):
                if r > 0 or m >= 2:
                    act.wait_ge(sem["sq_used"], 3 * r + (m - 1 if m < 2 else 1))
                nc.scalar.activation(sq[:, m % 2], h[:, 2 * m:2 * m + 2], ACT.Square).then_inc(sem["sq_ready"], 1)

            def residual(r, m, x=True):
                act.wait_ge(sem["h_ready"], hbase(r) + m + 1)
                if x:
                    x_high(r, m)
                squares(r, m)

            def norm(n):
                act.wait_ge(sem["bcast_ready"], n + 1)
                for q in range(2):
                    last = copy(rs[:, q], MB[:, SEQ:2 * SEQ])
                last.then_inc(sem["rs_ready"], 1)

            def residual_stage(stage, r):
                for m in range(PAIRS):
                    done(BASE[stage] + m)
                    residual(r, m)
                    if m < 2:
                        split(BASE[stage] + m)
                for m in range(2, PAIRS):
                    split(BASE[stage] + m)

            def mlp(l, r):
                g, first = BASE[f"mlp{l}"], MLP_PAIRS * l

                def square(i):
                    act.wait_ge(sem["relu_ready"], first + i + 1)
                    nc.scalar.activation(tb[:], ta[:], ACT.Square).then_inc(sem["act_ready"], 1)

                def high(i):
                    act.wait_ge(sem["act_ready"], first + i + 1)
                    copy(hid_hi[:], tb[:]).then_inc(sem["hid_hi_ready"], 1)

                act.wait_ge(sem["p_landed"], 16 * (l + 1))
                if l:
                    act.wait_ge(sem["unit_done"], BASE["ple0"] + 1)
                copy(p_hi[:], p_in[:]).then_inc(sem["p_hi_ready"], 1)
                norm(r)
                square(0)
                high(0)
                split(g)
                with act.Fori(0, (MLP_PAIRS - 1) // RING) as k:
                    for t in range(RING):
                        i = RING * k + t + 1
                        square(i)
                        split(g + 1 + 2 * t, 2 * k)
                        done(g + 2 + 2 * t, 2 * k)
                        high(i)
                        split(g + 2 + 2 * t, 2 * k)
                def b_copy(n):
                    act.wait_ge(sem["bt_done"], n + 1)
                    copy(bt[:, 2 * n:2 * n + 2].rearrange("p c r s -> p (c r s)"),
                         [MB, XB, U[1], U[0]][n]).then_inc(sem["bt_ready"], 1)

                if l == 0:
                    for n in range(4):
                        b_copy(n)
                last = g + 2 * MLP_PAIRS - 1
                for m in range(PAIRS):
                    residual(R_MLP0 if l == 0 else R_MLP1, m)
                split(last)

            def bias_store():
                act.wait_ge(sem["bv_done"], 1)
                copy(bv[:], XB[0:NH, 0:NDIST]).then_inc(sem["bv_copied"], 1)
                act.dma_start(w1[:], A["cmp_w1"][0]).then_inc(sem["cmpw_landed"], 16)
                act.dma_start(posc[:], A["cmp_pos"]).then_inc(sem["cmpw_landed"], 16)
                act.dma_start(w2[:], A["cmp_w2"]).then_inc(sem["cmpw_landed"], 16)
                act.dma_start(w1v, A["cmp_w1"][1]).then_inc(sem["cmpw_landed"], 16)
                act.wait_ge(sem["bv_copied"], 1)
                act.dma_start(A["bias_rows"],
                              bv[:].unsqueeze(1).broadcast_to([NH, P, NDIST])).then_inc(sem["bias_stored"], 16)

            def ffn(f, r, n, x=True):
                g, first = BASE[f"ffn{f}"], FFN_PAIRS * f

                def silu(i):
                    act.wait_ge(sem["a_scaled"], first + i + 1)
                    nc.scalar.activation(tb[:], ta[:], ACT.Silu).then_inc(sem["silu_ready"], 1)

                def high(i):
                    act.wait_ge(sem["prod_ready"], first + i + 1)
                    copy(hid_hi[:], tc[:]).then_inc(sem["hid_hi_ready"], 1)

                if n is not None:
                    norm(n)
                silu(0)
                split(g)
                high(0)
                split(g + 1)

                def pair(k):
                    silu(k + 1)
                    split(g + 2, k)
                    split(g + 3, k)
                    done(g + 4, k)
                    high(k + 1)
                    split(g + 4, k)

                with act.Fori(0, FFN_PAIRS - 1 - (f == 3)) as k:
                    pair(k)
                if f == 3:
                    pair(FFN_PAIRS - 2)
                if f == 1:
                    bias_store()
                if r != R_FFN3:
                    for m in range(PAIRS):
                        residual(r, m, x)
                split(g + 3 * FFN_PAIRS - 1)

            def ple(l, n, r, x=True):
                g = BASE[f"ple{l}"]
                split(g)
                norm(n)
                for m in range(PAIRS):
                    act.wait_ge(sem["gate_scaled"], PAIRS * l + m + 1)
                    nc.scalar.activation(tb[:], ta[:], ACT.Sigmoid).then_inc(sem["gate_ready"], 1)
                    residual(r, m, x)
                    if m < 2:
                        split(g + 1 + m)
                for m in range(2, PAIRS):
                    split(g + 1 + m)

            h_v = A["x"].rearrange("(c p) t -> p c t", p=P)
            act.dma_start(vec[:], A["vec"]).then_inc(sem["vec_landed"], 16)
            for m in range(PAIRS):
                act.dma_start(h[:, 2 * m:2 * m + 2], h_v[:, 2 * m:2 * m + 2]).then_inc(sem["h_landed"], 16)
            act.dma_start(s5b[:], A["s5b"]).then_inc(sem["misc_landed"], 16)
            act.dma_start(p_in[:], A["p"][0].rearrange("(c p) t -> p c t", p=P)).then_inc(sem["p_landed"], 16)
            act_fn = nc.scalar.activation
            act.wait_ge(sem["vec_landed"], 16)
            act_fn(sm[:, 0], col("ldt", 0, ST), ACT.Exp).then_inc(sem["sm_act"], 1)
            act.wait_ge(sem["h_landed"], 16 * PAIRS)
            x_high(R_IN, 0)
            act.wait_ge(raw_landed[0], 16)
            copy(w_hi[:, 0], raw[:, 0]).then_inc(sem["hi_ready"], 1)
            for m in range(1, PAIRS):
                x_high(R_IN, m)
            for m in range(PAIRS):
                squares(R_IN, m)
            for g in range(1, RING):
                act.wait_ge(raw_landed[g], 16)
                copy(w_hi[:, g], raw[:, g]).then_inc(sem["hi_ready"], 1)
            act.wait_ge(sem["sm_dve"], S5_R)
            act_fn(sm[:, 8], sm[:, 5], ACT.Abs).then_inc(sem["sm_act"], 1)
            act_fn(e_one[:, :, 1], sm[:, 5], ACT.Sin).then_inc(sem["sm_act"], 1)
            act.wait_ge(sem["sm_act"], 3)
            act.wait_ge(sem["fill_done"], 4)
            act_fn(e_one[:, :, 0], sm[:, 8], ACT.Sin, scale=-1.0, bias=halfpi[:]).then_inc(sem["sm_act"], 1)
            act.wait_ge(sem["fill_done"], 7)
            for ri in range(2):
                for g2 in range(2):
                    rows = slice(g2 * S5_STATE, (g2 + 1) * S5_STATE)
                    act.dma_start(ct[rows, 2 * ri, :, g2 * S5_CH:(g2 + 1) * S5_CH],
                                  A["s5c"][rows, ri]).then_inc(sem["misc_landed"], 16)

            def conv_triple(g0, k, j):
                done(g0, k)
                copy(tb[:], two(U[0])).then_inc(sem["c_copied"], 1)
                split(g0, k)
                split(g0 + 1, k)
                act.wait_ge(sem["y_ready"], j + 1)
                copy(x_hi[1][:, bass.ds(2 * j, 2), :], tc[:]).then_inc(sem["y_hi"], 1)
                split(g0 + 2, k)

            norm(R_IN)
            conv_triple(0, 0, 0)
            with act.Fori(0, PAIRS - 1) as k:
                conv_triple(3, k, k + 1)
            act.dma_start(posi[:], A["positions"].partition_broadcast(P)).then_inc(sem["pos_landed"], 16)
            act.wait_ge(sem["misc_landed"], 80)
            copy(ct[:, 1], ct[:, 0], scale=-1.0).then_inc(sem["ct_ready"], 1)
            copy(ct[:, 2], ct[:, 2], scale=-1.0).then_inc(sem["ct_ready"], 1)
            residual_stage("sc_out", R_SC)
            mlp(0, R_SC)
            act.wait_ge(sem["rope_step"], 6)
            act_fn(ang[:, 0], ang[:, 1], ACT.Abs).then_inc(sem["sin_ready"], 1)
            act_fn(rope_s[:], ang[:, 1], ACT.Sin).then_inc(sem["sin_ready"], 1)
            act.wait_ge(sem["sin_ready"], 2)
            act_fn(rope_c[:], ang[:, 0], ACT.Sin, scale=-1.0, bias=halfpi[:]).then_inc(sem["sin_ready"], 1)
            ple(0, R_MLP0, R_PLE0)
            act.wait_ge(sem["p_lo_ready"], 1)
            act.dma_start(p_in[:], A["p"][1].rearrange("(c p) t -> p c t", p=P)).then_inc(sem["p_landed"], 16)

            g = BASE["qkv"]

            def exps(hd):
                act.wait_ge(sem["bias_ready"], hd + 1)
                act_fn(lg0[:], lg0[:], ACT.Exp, scale=SCALE, bias=nbias[:, 0:1],
                       accum_out=den[:, 0:1]).then_inc(sem["exp_done"], 1)
                act_fn(lg1[:], lg1[:], ACT.Exp, scale=SCALE, bias=nbias[:, 1:2],
                       accum_out=den[:, 1:2]).then_inc(sem["exp_done"], 1)

            TBK = [DB[3], MB]

            def pt_copy(hd, side, b):
                act.wait_ge(sem["pt_done"], 3 * hd + b + 1)
                if b == 0:
                    act.wait_ge(sem["pv_done"], hd)
                copy(pt[:, b], TBK[(NG * side + b) % 2][:, 0:NG * P]).then_inc(sem["pt_copied"], 1)

            def scale_out(hd):
                act.wait_ge(sem["pv_done"], hd + 1)
                act.wait_ge(sem["rden_ready"], hd + 1)
                act.wait_ge(sem["ot_done"], hd)
                for t in range(TT):
                    copy(ot[:, t], DB[2][:, SEQ + t * DH:SEQ + (t + 1) * DH],
                         scale=rden[:, t:t + 1]).then_inc(sem["o_scaled"], 1)

            def out_high(hd):
                act.wait_ge(sem["ot_done"], hd + 1)
                copy(x_hi[1][:, bass.ds(hd, 1), :].rearrange("p o t -> p (o t)"),
                     DB[2][:, 0:SEQ]).then_inc(sem["o_hi"], 1)

            def value_copy(g0, k, i, gr):
                done(g0, k)
                if gr == 0:
                    act.wait_ge(sem["pv_done"], 2 * i)
                bank = U3[(6 + gr) % 3]
                for t in range(TT):
                    last = copy(vv[:, t, gr], bank[:, t * SEQ:(t + 1) * SEQ], scale=rs_tok[:, t:t + 1])
                last.then_inc(sem["v_copied"], 1)

            def attend(i, u):
                a, b = 2 * i, 2 * i + 1
                if u == 0:
                    pt_copy(a, 0, 0)
                    pt_copy(a, 0, 1)
                elif u == 1:
                    pt_copy(a, 0, 2)
                    exps(b)
                elif u == 2:
                    scale_out(a)
                    pt_copy(b, 1, 0)
                elif u == 3:
                    pt_copy(b, 1, 1)
                    out_high(a)
                elif u == 4:
                    pt_copy(b, 1, 2)
                elif u == 5:
                    scale_out(b)
                elif u == 6:
                    out_high(b)

            def qkv_units(k, i, before):
                for u in range(9):
                    if u >= 6:
                        value_copy(g + u, k, i, u - 6)
                    split(g + u, k)
                    if before is not None:
                        attend(before, u)

            norm(R_PLE0)
            qkv_units(0, 0, None)
            with act.Fori(0, HEAD_PAIRS - 1) as k:
                exps(2 * k)
                qkv_units(3 * k + 3, k + 1, k)
            exps(2 * (HEAD_PAIRS - 1))
            for u in range(7):
                attend(HEAD_PAIRS - 1, u)
            residual_stage("wo", R_WO)

            mlp(1, R_WO)
            ple(1, R_MLP1, R_PLE1, x=False)
            norm(R_PLE1)
            for m in range(PAIRS):
                residual(R_FIN, m)
            ffn(0, R_FFN0, R_FIN, x=False)

            def load_rotation(b):
                if b >= LSLOTS:
                    act.wait_ge(sem["turned_back"], 2 * LB * (b - LSLOTS + 1))
                width = LB * 2 * SEQ
                at = b % (EB // LB) * width
                act.dma_start(e_ring[:, b % LSLOTS].rearrange("p j r t -> p (j r t)"),
                              A["e_table"][b * LB // EB][:, at:at + width]).then_inc(e_landed[b % LSLOTS], 16)

            for b in range(LSLOTS):
                load_rotation(b)
            norm(R_FFN0)

            def gelu(c):
                act.wait_ge(sem["y_in"], c + 1)
                act_fn(y5[:, c], ta[:, 0], ACT.Gelu_apprx_tanh).then_inc(sem["gelu_done"], 1)
                act.wait_ge(sem["gelu_done"], c + 1)
                copy(x_hi[1][:, c], y5[:, c]).then_inc(sem["g_hi"], 1)

            for j in range(ST):
                if j % LB == LB - 1 and j // LB + LSLOTS < ST // LB:
                    load_rotation(j // LB + LSLOTS)
                if j % 4 == 2 and j >= 6:
                    gelu(j // 4 - 1)
            gelu(KC - 1)
            for m in range(PAIRS):
                done(BASE["glu"] + m)
                act_fn(tb[:], two(U[m % 2]), ACT.Sigmoid).then_inc(sem["gate_ready"], 1)
                residual(R_GLU, m)
                if m < 2:
                    split(BASE["glu"] + m)
            for m in range(2, PAIRS):
                split(BASE["glu"] + m)

            act.dma_start(oh[:], A["onehot"]).then_inc(sem["bias_in_landed"], 16)
            act.dma_start(rel[0:NBUCKET], A["rel_bias"]).then_inc(sem["bias_in_landed"], 16)
            ffn(1, R_FFN1, R_GLU)

            g = BASE["kv"]
            norm(R_FFN1)

            def key_norm_act(count, width, part):
                flat = norm_buffers(count, width)
                if part == 0:
                    act.wait_ge(sem["k_scaled"], count)
                    act_fn(flat[1], flat[0], ACT.Square).then_inc(sem["k_sq"], 1)
                else:
                    act.wait_ge(sem["k_mean"], count)
                    act_fn(flat[1], flat[2], ACT.Ln).then_inc(sem["k_ln"], 1)
                    act.wait_ge(sem["k_ln"], count)
                    act_fn(flat[1], flat[1], ACT.Exp, scale=-0.5).then_inc(sem["k_exp"], 1)

            def values_copy(u, br):
                done(g + u)
                for t in range(TT):
                    last = copy(vs[:, br, t], U[1][:, t * SEQ:(t + 1) * SEQ], scale=rs_tok[:, t:t + 1])
                last.then_inc(sem["vs_ready"], 1)

            for m in range(PAIRS):
                x_high("kv", m)
            split(g)
            split(g + 1)
            key_norm_act(1, 512, 0)
            split(g + 2)
            values_copy(3, 0)
            split(g + 3)
            key_norm_act(1, 512, 1)
            key_norm_act(2, 512, 0)
            split(g + 4)
            values_copy(5, 1)
            split(g + 5)
            key_norm_act(2, 512, 1)

            def hidden(kind):
                act.wait_ge(sem["hid_done"], 2 * (kind + 1))
                for half in range(2):
                    last = copy(hraw[:, half], [MB, U[0]][half][0:2 * NCMP, 0:P])
                last.then_inc(sem["hid_copied"], 1)
                act.wait_ge(sem["hid_turned"], kind + 1)
                act_fn(hg[:].rearrange("p e n -> p (e n)"), MB[:, 0:4 * NCMP],
                       ACT.Gelu_apprx_tanh).then_inc(sem["hg_ready"], 1)

            hidden(0)
            key_norm_act(3, 2 * NCMP, 0)
            key_norm_act(3, 2 * NCMP, 1)
            act.wait_ge(sem["w2_done"], 1)
            hidden(1)
            act.wait_ge(sem["w2_done"], 2)
            copy(vcmp[:].rearrange("c k d -> c (k d)"), MB[0:NCMP, 256:512]).then_inc(sem["vc_ready"], 1)
            act.dma_start(wg[:], A["gate_w"]).then_inc(sem["wg_landed"], 16)
            act.wait_ge(sem["bias_stored"], 16)
            rows_ = bass.AP(A["bias_rows"].tensor, P - 1, [[NDIST - 1, P], [P * NDIST, NH], [1, SEQ]])
            act.dma_start(tbl[:], rows_).then_inc(sem["tbl_landed"], 16)
            ffn(2, R_FFN2, None)

            g = BASE["qg"]
            act.wait_ge(sem["wg_landed"], 16)
            copy(wg_hi[:], wg[:]).then_inc(sem["wg_hi_ready"], 1)
            norm(R_FFN2)
            for u in range(4):
                if u:
                    key_norm_act(3 + u, 512, 1)
                key_norm_act(4 + u, 512, 0)
                split(g + u)
            act.wait_ge(sem["gate_done"], 1)
            for t in range(TT):
                last = act_fn(gate[:, t], U[0][:, t * 64:t * 64 + 3 * NH], ACT.Sigmoid, scale=rs_tok[:, t:t + 1])
            last.then_inc(sem["gate_sig"], 1)
            key_norm_act(7, 512, 1)

            act.wait_ge(sem["k_ready"], 7)

            def n_copy(hd):
                b = hd % 2
                act.wait_ge(sem["n_t"], hd + 1)
                if hd >= 2:
                    act.wait_ge(sem["n_pv"], hd - 1)
                copy(ptn[:, b, 0], U[0][:, 0:3 * P])
                copy(ptc[:, b], MB[0:NCMP, 0:SEQ]).then_inc(sem["n_ta"], 1)

            def n_exp(hd):
                b = hd % 2
                act.wait_ge(sem["n_max"], hd + 1)
                for t in range(TT):
                    act_fn(lgc[:, b, t], lgc[:, b, t], ACT.Exp, bias=nm[:, b, 0, t:t + 1],
                           accum_out=dn[:, b, 0, t:t + 1])
                for br in range(2):
                    act_fn(lg[:, b, br, 0:P], lg[:, b, br, 0:P], ACT.Exp, bias=nm[:, b, 1 + br, 0:1],
                           accum_out=dn[:, b, 1 + br, 0:1])
                    last = act_fn(lg[:, b, br, P:3 * P], lg[:, b, br, P:3 * P], ACT.Exp,
                                  bias=nm[:, b, 1 + br, 1:2], accum_out=dn[:, b, 1 + br, 1:2])
                last.then_inc(sem["n_exp"], 1)

            def n_high(ch):
                act.wait_ge(sem["n_ot"], ch + 1)
                copy(x_hi[0][:, ch], MB[:, SEQ:2 * SEQ]).then_inc(sem["n_hi"], 1)

            for step in range(NH + 1):
                if step:
                    n_copy(step - 1)
                if step < NH:
                    n_exp(step)
                if step and step % 2 == 0:
                    n_high(step // 2 - 1)
            residual_stage("nwo", R_NWO)
            ffn(3, R_FFN3, R_NWO)

        @block.gpsimd
        def _(pool):
            def fill(ap, value):
                pool.memset(ap, value).then_inc(sem["fill_done"], 1)

            fill(ones[:], 1.0)
            fill(nhalf[:], -0.5)
            fill(zero[:], 0.0)
            fill(halfpi[:], math.pi / 2)
            fill(vp[:], 0.0)
            fill(bb[:], 0.0)
            fill(ct[:], 0.0)

            def add_squares(r):
                if r:
                    pool.wait_ge(sem["sum_ready"], r)
                for m in range(3):
                    pool.wait_ge(sem["sq_ready"], PAIRS * r + m + 2)
                    if m == 0:
                        pool.tensor_tensor(ssum[:], sq[:, 0], sq[:, 1], ALU.add).then_inc(sem["sq_used"], 1)
                    else:
                        pool.wait_ge(sem["sq_used"], 3 * r + m)
                        pool.tensor_tensor(ssum[:], ssum[:], sq[:, (m + 1) % 2], ALU.add).then_inc(sem["sq_used"], 1)

            def norm(n):
                add_squares(n)
                pool.wait_ge(sem["var_ready"], n + 1)
                pool.tensor_tensor(rs_tok[:], var_tok[:], nhalf[:], ALU.pow).then_inc(sem["rst_ready"], 1)

            per = 1 + 5 * 8

            def rotations(b):
                pool.wait_ge(sem["e_stored"], 16 * b)
                pool.tensor_copy(e_tab[:, :, :, 0:1].rearrange("p j r o -> p j (r o)"),
                                 e_one[:, bass.ds(EB * b, EB), :]).then_inc(sem["e_step"], 1)
                for lv in range(8):
                    n = 1 << lv
                    lo, hi = e_tab[:, :, :, 0:n], e_tab[:, :, :, n:2 * n]
                    step = e_tab[:, :, :, n - 1:n]
                    at = 1 + 5 * lv
                    pool.wait_ge(sem["e_step"], per * b + at)
                    pool.tensor_tensor(e_t1[:, :, :, 0:n], lo, step[:, :, 0:1].broadcast_to([P, EB, 2, n]),
                                       ALU.mult).then_inc(sem["e_step"], 1)
                    pool.tensor_tensor(e_t2[:, :, 0, 0:n], lo[:, :, 1], step[:, :, 1].broadcast_to([P, EB, n]),
                                       ALU.mult).then_inc(sem["e_step"], 1)
                    pool.tensor_tensor(e_t2[:, :, 1, 0:n], lo[:, :, 0], step[:, :, 1].broadcast_to([P, EB, n]),
                                       ALU.mult).then_inc(sem["e_step"], 1)
                    pool.wait_ge(sem["e_step"], per * b + at + 3)
                    pool.tensor_tensor(hi[:, :, 0], e_t1[:, :, 0, 0:n], e_t2[:, :, 0, 0:n],
                                       ALU.subtract).then_inc(sem["e_step"], 1)
                    pool.tensor_tensor(hi[:, :, 1], e_t1[:, :, 1, 0:n], e_t2[:, :, 1, 0:n],
                                       ALU.add).then_inc(sem["e_step"], 1)
                pool.wait_ge(sem["e_step"], per * b + per)
                pool.dma_start(A["e_table"][bass.ds(b, 1)].rearrange("o p n -> p (o n)"),
                               e_tab[:].rearrange("p j r t -> p (j r t)")).then_inc(sem["e_stored"], 16)

            norm(R_IN)
            pool.wait_ge(sem["sm_act"], 4)
            with pool.Fori(0, 3) as b:
                rotations(b)
            norm(R_SC)
            with pool.Fori(3, ST // EB) as b:
                rotations(b)
            norm(R_MLP0)
            norm(R_PLE0)

            def rotate(i, u):
                side, gr = u // NG, u % NG
                n = 6 * i + u
                pool.wait_ge(sem["swapped"], n + 1)
                pool.tensor_tensor(swap[:], swap[:], sin_rs[0:32].unsqueeze(1).broadcast_to([32, 2, SEQ]),
                                   ALU.mult).then_inc(sem["sin_part"], 1)
                pool.wait_ge(sem["sin_part"], n + 1)
                pool.wait_ge(sem["qk_main"], n + 1)
                pool.tensor_tensor(qk[0:32, side, gr], qk[0:32, side, gr], swap[:],
                                   ALU.add).then_inc(sem["qk_ready"], 1)

            pool.wait_ge(sem["rope_rs"], 2)
            with pool.Fori(0, HEAD_PAIRS) as i:
                for u in range(6):
                    rotate(i, u)
            norm(R_WO)
            norm(R_MLP1)
            norm(R_PLE1)
            norm(R_FIN)
            norm(R_FFN0)

            for j in range(ST):
                pool.wait_ge(sem["z_ready"], 2 * (j + 1))
                if j >= 2:
                    pool.wait_ge(sem["y_done"], j - 1)
                e = e_ring[:, (j // LB) % LSLOTS, j % LB]
                z = z5[:, j % 2]
                pool.tensor_tensor(n1[j % 2][:], z, e[:, 0:1].broadcast_to([P, 2, SEQ]), ALU.mult).then_inc(sem["turned_back"], 1)
                pool.tensor_tensor(n2[j % 2][:, 0], z[:, 1], e[:, 1], ALU.mult)
                pool.tensor_tensor(n2[j % 2][:, 1], z[:, 0], e[:, 1], ALU.mult).then_inc(sem["turned_back"], 1)
            norm(R_GLU)
            norm(R_FFN1)
            norm(R_FFN2)
            norm(R_NWO)

        @block.vector
        def _(dve):
            tt, stt, ts = dve.tensor_tensor, dve.scalar_tensor_tensor, dve.tensor_scalar
            rs_b = rs[:]

            def done(g0, k=0):
                dve.wait_ge(sem["unit_done"], g0 + 1 + RING * k)

            def split(g0, k=0):
                g = g0 + RING
                if isinstance(k, int) and g + RING * k >= NU:
                    return
                dve.wait_ge(sem["hi_ready"], g + 1 + RING * k)
                tt(w_lo[:, g % RING], raw[:, g % RING], w_hi[:, g % RING].bitcast(F32),
                   ALU.subtract).then_inc(sem["lo_ready"], 1)

            def x_low(r, m):
                dve.wait_ge(sem["xh_ready"], XBASE[r] + m + 1)
                for q in range(2):
                    c = 2 * m + q
                    last = stt(x_lo[XBUF[r]][:, c], h[:, c], col(GAIN[r], c), x_hi[XBUF[r]][:, c].bitcast(F32),
                               ALU.mult, ALU.subtract)
                last.then_inc(sem["xl_ready"], 1)

            def add(m, part, scale=1.0):
                pair = h[:, 2 * m:2 * m + 2]
                stt(pair, part, scale, pair, ALU.mult, ALU.add).then_inc(sem["h_ready"], 1)

            def norm(n):
                dve.wait_ge(sem["sum_ready"], n + 1)
                ts(var_tok[:], MB[:, 0:TT], 1.0 / D, EPS, ALU.mult, ALU.add).then_inc(sem["var_ready"], 1)
                dve.wait_ge(sem["rst_ready"], n + 1)
                if n == R_IN:
                    dve.wait_ge(sem["con_landed"], 16)
                tt(diag[:], ident.unsqueeze(1).broadcast_to([P, TT, P]),
                   rs_tok[:].unsqueeze(2).broadcast_to([P, TT, P]), ALU.mult).then_inc(sem["diag_ready"], 1)

            def residual_stage(stage, r):
                for m in range(PAIRS):
                    done(BASE[stage] + m)
                    add(m, two(U[m % 2]))
                    x_low(r, m)
                    if m < 2:
                        split(BASE[stage] + m)
                split(BASE[stage] + 2)

            def last_sums(g, r, scale, x):
                for m in range(PAIRS + 1):
                    if m < PAIRS:
                        if m < PAIRS - 1:
                            dve.wait_ge(sem["acc_done"], 3 * DOWN[r] + m + 1)
                        else:
                            done(g)
                        add(m, two(DB[m]), scale)
                    if m and x:
                        x_low(r, m - 1)

            DOWN = {R_MLP0: 0, R_MLP1: 1, R_FFN0: 2, R_FFN1: 3, R_FFN2: 4, R_FFN3: 5}

            count = [0]

            def link(ins):
                ins.then_inc(sem["sm_dve"], 1)
                count[0] += 1
                dve.wait_ge(sem["sm_dve"], count[0])

            are, aim = col("are", 0, ST), col("aim", 0, ST)

            def input_matrices():
                dve.wait_ge(sem["misc_landed"], 80)
                dve.wait_ge(sem["sm_act"], 4)
                cosa, sina = e_one[:, :, 0], e_one[:, :, 1]
                link(tt(sm[:, 9], mag[:], cosa, ALU.mult))
                link(tt(sm[:, 10], mag[:], sina, ALU.mult))
                link(ts(sm[:, 9], sm[:, 9], -1.0, None, ALU.add))
                link(tt(sm[:, 11], are, are, ALU.mult))
                link(tt(sm[:, 12], aim, aim, ALU.mult))
                link(tt(sm[:, 11], sm[:, 11], sm[:, 12], ALU.add))
                link(dve.reciprocal(sm[:, 12], sm[:, 11]))
                link(tt(sm[:, 13], sm[:, 9], are, ALU.mult))
                link(tt(sm[:, 14], sm[:, 10], aim, ALU.mult))
                link(tt(sm[:, 13], sm[:, 13], sm[:, 14], ALU.add))
                link(tt(sm[:, 13], sm[:, 13], sm[:, 12], ALU.mult))
                link(tt(sm[:, 14], sm[:, 10], are, ALU.mult))
                link(tt(sm[:, 15], sm[:, 9], aim, ALU.mult))
                link(tt(sm[:, 14], sm[:, 14], sm[:, 15], ALU.subtract))
                link(tt(sm[:, 14], sm[:, 14], sm[:, 12], ALU.mult))
                t_a = ta[:].rearrange("p c t -> p (c t)").rearrange("p (j q) -> p j q", q=S5_CH)
                t_b = tc[:].rearrange("p c t -> p (c t)").rearrange("p (j q) -> p j q", q=S5_CH)
                z_re = sm[:, 13].unsqueeze(2).broadcast_to([P, ST, S5_CH])
                z_im = sm[:, 14].unsqueeze(2).broadcast_to([P, ST, S5_CH])
                for ri, (x0, x1, op) in enumerate(((0, 1, ALU.subtract), (1, 0, ALU.add))):
                    link(tt(t_a, s5b[:, x0], z_re, ALU.mult))
                    link(tt(t_b, s5b[:, x1], z_im, ALU.mult))
                    for g2 in range(2):
                        rows = slice(g2 * S5_STATE, (g2 + 1) * S5_STATE)
                        tt(bb[rows, ri, :, g2 * S5_CH:(g2 + 1) * S5_CH], t_a[rows], t_b[rows],
                           op).then_inc(sem["bb_ready"], 1)
                    dve.wait_ge(sem["bb_ready"], 2 * (ri + 1))

            def mlp(l, n, r, late):
                g, first, hb = BASE[f"mlp{l}"], MLP_PAIRS * l, HID_BASE[f"mlp{l}"]

                def relu(g0, k):
                    done(g0, k)
                    stt(ta[:], two(U[0]), 0.0, rs_b, ALU.max, ALU.mult).then_inc(sem["relu_ready"], 1)

                def low(i):
                    dve.wait_ge(sem["hid_hi_ready"], hb + i + 1)
                    tt(hid_lo[:], tb[:], hid_hi[:].bitcast(F32), ALU.subtract).then_inc(sem["hid_lo_ready"], 1)

                norm(n)
                split(late)
                dve.wait_ge(sem["rs_ready"], n + 1)
                relu(g, 0)
                low(0)
                split(g)
                dve.wait_ge(sem["p_hi_ready"], l + 1)
                tt(p_lo[:], p_in[:], p_hi[:].bitcast(F32), ALU.subtract).then_inc(sem["p_lo_ready"], 1)
                if l == 0:
                    input_matrices()
                with dve.Fori(0, (MLP_PAIRS - 1) // RING) as k:
                    for t in range(RING):
                        relu(g + 1 + 2 * t, 2 * k)
                        split(g + 1 + 2 * t, 2 * k)
                        low(RING * k + t + 1)
                        split(g + 2 + 2 * t, 2 * k)
                last_sums(g + 2 * MLP_PAIRS - 1, r, 1.0, True)
                split(g + 2 * MLP_PAIRS - 1)

            def ffn(f, n, r, x=True, late=None):
                g, first, hb = BASE[f"ffn{f}"], FFN_PAIRS * f, HID_BASE[f"ffn{f}"]

                def first_half(g0, k):
                    done(g0, k)
                    tt(ta[:], two(U[0]), rs_b, ALU.mult).then_inc(sem["a_scaled"], 1)

                def second_half(g0, k, i):
                    done(g0, k)
                    tt(tc[:], two(U[1]), rs_b, ALU.mult).then_inc(sem["b_gated"], 1)
                    dve.wait_ge(sem["silu_ready"], first + i + 1)
                    dve.wait_ge(sem["b_gated"], first + i + 1)
                    tt(tc[:], tb[:], tc[:], ALU.mult).then_inc(sem["prod_ready"], 1)

                def low(i):
                    dve.wait_ge(sem["hid_hi_ready"], hb + i + 1)
                    tt(hid_lo[:], tc[:], hid_hi[:].bitcast(F32), ALU.subtract).then_inc(sem["hid_lo_ready"], 1)

                if n is not None:
                    norm(n)
                    if late is not None:
                        split(late)
                    dve.wait_ge(sem["rs_ready"], n + 1)
                first_half(g, 0)
                split(g)
                second_half(g + 1, 0, 0)
                low(0)
                split(g + 1)

                def pair(k):
                    first_half(g + 2, k)
                    split(g + 2, k)
                    second_half(g + 3, k, k + 1)
                    split(g + 3, k)
                    low(k + 1)
                    split(g + 4, k)

                with dve.Fori(0, FFN_PAIRS - 1 - (f == 3)) as k:
                    pair(k)
                if f == 3:
                    pair(FFN_PAIRS - 2)
                if f == 1:
                    dve.wait_ge(sem["bias_in_landed"], 32)
                    dve.memset(rel[NBUCKET:NBUCKET + 1], NEG).then_inc(sem["rel_ready"], 1)
                last_sums(g + 3 * FFN_PAIRS - 1, r, 0.5, x)
                split(g + 3 * FFN_PAIRS - 1)

            def gated(count, other, m):
                dve.wait_ge(sem["gate_ready"], count)
                tt(tc[:], tb[:], other, ALU.mult).then_inc(sem["gated"], 1)
                dve.wait_ge(sem["gated"], count)
                add(m, tc[:])

            def ple(l, n, r, x=True):
                g = BASE[f"ple{l}"]
                split(g)
                norm(n)
                dve.wait_ge(sem["rs_ready"], n + 1)
                for m in range(PAIRS):
                    done(g + 1 + m)
                    tt(ta[:], two(U[m % 2]), rs_b, ALU.mult).then_inc(sem["gate_scaled"], 1)
                    gated(PAIRS * l + m + 1, two([XB, DB[0], DB[1], DB[2]][m]), m)
                    if x:
                        x_low(r, m)
                    if m < 2:
                        split(g + 1 + m)
                for m in range(2, PAIRS):
                    split(g + 1 + m)

            dve.wait_ge(sem["sm_act"], 1)
            link(tt(sm[:, 1], are, sm[:, 0], ALU.mult))
            link(ts(sm[:, 1], sm[:, 1], 2.0 ** -S5_HALVINGS, None, ALU.mult))
            link(dve.tensor_copy(sm[:, 2], sm[:, 1]))
            for n in (6, 5, 4, 3, 2):
                link(ts(sm[:, 2], sm[:, 2], 1.0 / n, 1.0, ALU.mult, ALU.add))
                link(tt(sm[:, 2], sm[:, 2], sm[:, 1], ALU.mult))
            for _ in range(S5_HALVINGS):
                link(stt(sm[:, 2], sm[:, 2], 2.0, sm[:, 2], ALU.add, ALU.mult))
            link(ts(mag[:], sm[:, 2], 1.0, None, ALU.add))
            link(tt(sm[:, 3], aim, sm[:, 0], ALU.mult))
            link(ts(sm[:, 4], sm[:, 3], 1.0 / (2 * math.pi), ROUND, ALU.mult, ALU.add))
            link(ts(sm[:, 4], sm[:, 4], -ROUND, None, ALU.add))
            link(stt(sm[:, 5], sm[:, 4], -TWO_PI_1, sm[:, 3], ALU.mult, ALU.add))
            link(stt(sm[:, 5], sm[:, 4], -TWO_PI_2, sm[:, 5], ALU.mult, ALU.add))
            link(stt(sm[:, 5], sm[:, 4], -TWO_PI_3, sm[:, 5], ALU.mult, ALU.add))
            link(ts(sm[:, 5], sm[:, 5], 3.1415925, -3.1415925, ALU.min, ALU.max))
            assert count[0] == S5_R

            def first_split(g):
                dve.wait_ge(sem["hi_ready"], g + 1)
                tt(w_lo[:, g], raw[:, g], w_hi[:, g].bitcast(F32), ALU.subtract).then_inc(sem["lo_ready"], 1)

            for m in range(2):
                x_low(R_IN, m)
            first_split(0)
            for m in range(2, PAIRS):
                x_low(R_IN, m)
            for g in range(1, RING):
                first_split(g)

            norm(R_IN)
            dve.wait_ge(sem["rs_ready"], 1)
            tt(rs2[:], rs[:], rs[:], ALU.mult).then_inc(sem["rs2_ready"], 1)
            dve.wait_ge(sem["fill_done"], 7)
            dve.wait_ge(sem["rs2_ready"], 1)

            def conv_triple(g0, k, j):
                done(g0 + 1, k)
                v = vp[:, :, 2:SEQ + 2]
                dve.wait_ge(sem["c_copied"], j + 1)
                split(g0, k)
                tt(v, tb[:], two(U[1]), ALU.mult).then_inc(sem["v_raw"], 1)
                dve.wait_ge(sem["v_raw"], j + 1)
                tt(v, v, rs2[:], ALU.mult).then_inc(sem["v_ready"], 1)
                dve.wait_ge(sem["v_ready"], j + 1)
                for tap in range(3):
                    if tap:
                        dve.wait_ge(sem["tap_done"], 6 * j + 2 * tap)
                    for q in range(2):
                        w = vec[:, bass.ds(VCOL["conv"] + (2 - tap) * KC + q + 2 * j, 1)]
                        x_ = vp[:, q, 2 - tap:SEQ + 2 - tap]
                        if tap:
                            ins = stt(yc[:, q], x_, w, yc[:, q], ALU.mult, ALU.add)
                        else:
                            ins = ts(yc[:, q], x_, w, None, ALU.mult)
                        ins.then_inc(sem["tap_done"], 1)
                split(g0 + 1, k)
                done(g0 + 2, k)
                tt(tc[:], two(XB), rs_b, ALU.mult).then_inc(sem["b_scaled"], 1)
                dve.wait_ge(sem["b_scaled"], j + 1)
                dve.wait_ge(sem["tap_done"], 6 * j + 6)
                tt(tc[:], tc[:], yc[:], ALU.mult).then_inc(sem["y_ready"], 1)
                dve.wait_ge(sem["y_hi"], j + 1)
                yh = x_hi[1][:, bass.ds(2 * j, 2), :].bitcast(F32)
                tt(x_lo[1][:, bass.ds(2 * j, 2), :], tc[:], yh, ALU.subtract).then_inc(sem["y_lo"], 1)
                split(g0 + 2, k)

            conv_triple(0, 0, 0)
            with dve.Fori(0, PAIRS - 1) as k:
                conv_triple(3, k, k + 1)
            residual_stage("sc_out", R_SC)

            mlp(0, R_SC, R_MLP0, BASE["sc_out"] + 3)

            def step(ins, n):
                ins.then_inc(sem["rope_step"], 1)
                dve.wait_ge(sem["rope_step"], n)

            dve.wait_ge(sem["pos_landed"], 16)
            step(dve.tensor_copy(ang[:, 0], posi[:]), 1)
            step(ts(ang[:, 1], ang[:, 0], cst("invf", 1), None, ALU.mult), 2)
            step(ts(ang[:, 2], ang[:, 1], 1.0 / (2 * math.pi), ROUND, ALU.mult, ALU.add), 3)
            step(ts(ang[:, 2], ang[:, 2], -ROUND, None, ALU.add), 4)
            dve.scalar_tensor_tensor(ang[:, 1], ang[:, 2], -TWO_PI_1, ang[:, 1], ALU.mult, ALU.add)\
                .then_inc(sem["rope_ready"], 1)
            dve.wait_ge(sem["rope_ready"], 1)
            stt(ang[:, 1], ang[:, 2], -TWO_PI_2, ang[:, 1], ALU.mult, ALU.add).then_inc(sem["rope_ready"], 1)
            dve.wait_ge(sem["rope_ready"], 2)
            step(stt(ang[:, 1], ang[:, 2], -TWO_PI_3, ang[:, 1], ALU.mult, ALU.add), 5)
            step(ts(ang[:, 1], ang[:, 1], 3.1415925, -3.1415925, ALU.min, ALU.max), 6)
            ple(0, R_MLP0, R_PLE0)

            dve.wait_ge(sem["sin_ready"], 3)
            norm(R_PLE0)
            dve.wait_ge(sem["rs_ready"], R_PLE0 + 1)
            dve.wait_ge(sem["e_stored"], 16 * (ST // EB))
            tt(cos_rs[:], rope_c[:], rs[:, 0], ALU.mult).then_inc(sem["rope_rs"], 1)
            stt(sin_rs[:], rope_s[:], cst("sgn", 1), rs[:, 0], ALU.mult, ALU.mult).then_inc(sem["rope_rs"], 1)
            dve.wait_ge(sem["rope_rs"], 2)

            g = BASE["qkv"]
            half_swap = [(p + ROPE // 2) % ROPE for p in range(ROPE)]

            def softmax_in(hd):
                dve.wait_ge(sem["s_done"], hd + 1)
                dve.wait_ge(sem["pt_done"], 3 * hd)
                tt(lg0[:].rearrange("p g k -> p (g k)"), DB[0][:, 0:NG * P], cst("mask0", NG * P),
                   ALU.add).then_inc(sem["masked"], 1)
                tt(lg1[:].rearrange("p g k -> p (g k)"), psum[:, 1:3].rearrange("p b n -> p (b n)")[:, 0:NG * SEQ],
                   cst("mask1", NG * SEQ), ALU.add).then_inc(sem["masked"], 1)
                dve.wait_ge(sem["masked"], 2 * (hd + 1))
                for t, part in enumerate((lg0, lg1)):
                    dve.tensor_reduce(nmax[:, t:t + 1], part[:], AX.XY, ALU.max,
                                      negate=True).then_inc(sem["max_done"], 1)
                dve.wait_ge(sem["max_done"], 2 * (hd + 1))
                ts(nbias[:], nmax[:], SCALE, None, ALU.mult).then_inc(sem["bias_ready"], 1)

            def denominators(hd):
                dve.wait_ge(sem["exp_done"], 2 * (hd + 1))
                dve.wait_ge(sem["o_scaled"], 2 * hd)
                dve.reciprocal(rden[:], den[:]).then_inc(sem["rden_ready"], 1)

            def out_low(hd):
                dve.wait_ge(sem["o_hi"], hd + 1)
                out = x_lo[1][:, bass.ds(hd, 1), :].rearrange("p o t -> p (o t)")
                hi = x_hi[1][:, bass.ds(hd, 1), :].rearrange("p o t -> p (o t)").bitcast(F32)
                tt(out, DB[2][:, 0:SEQ], hi, ALU.subtract).then_inc(sem["o_lo"], 1)

            def rope(g0, k, i, u, first):
                side, gr = u // NG, u % NG
                done(g0, k)
                dve.wait_ge(sem["qk_ready"], 6 * i + u)
                bank = two(U3[u % 3])
                if not first:
                    dve.wait_ge(sem["s_done"], 2 * i - 1 + side)
                tt(qk[:, side, gr], bank, cos_rs[:].unsqueeze(1).broadcast_to([P, 2, SEQ]),
                   ALU.mult).then_inc(sem["qk_main"], 1)
                dve.stream_shuffle(swap[:], bank[0:32], half_swap).then_inc(sem["swapped"], 1)

            def attend(i, u):
                a, b = 2 * i, 2 * i + 1
                if u == 0:
                    denominators(a)
                elif u == 1:
                    softmax_in(b)
                elif u == 3:
                    denominators(b)
                    out_low(a)
                elif u == 6:
                    out_low(b)

            def qkv_units(k, i, before, first):
                for u in range(9):
                    if u < 6:
                        rope(g + u, k, i, u, first)
                    split(g + u, k)
                    if before is not None:
                        attend(before, u)

            qkv_units(0, 0, None, True)
            with dve.Fori(0, HEAD_PAIRS - 1) as k:
                softmax_in(2 * k)
                qkv_units(3 * k + 3, k + 1, k, False)
            softmax_in(2 * (HEAD_PAIRS - 1))
            for u in range(7):
                attend(HEAD_PAIRS - 1, u)
            residual_stage("wo", R_WO)

            mlp(1, R_WO, R_MLP1, BASE["wo"] + 3)
            ple(1, R_MLP1, R_PLE1, x=False)

            norm(R_PLE1)
            dve.wait_ge(sem["rs_ready"], R_PLE1 + 1)
            for m in range(PAIRS + 1):
                if m < PAIRS:
                    for q in range(2):
                        c = 2 * m + q
                        last = stt(h[:, c], h[:, c], col("final", c), rs[:, 0], ALU.mult, ALU.mult)
                    last.then_inc(sem["h_ready"], 1)
                if m:
                    x_low(R_FIN, m - 1)
            ffn(0, R_FIN, R_FFN0, x=False)

            norm(R_FFN0)
            dve.wait_ge(sem["rs_ready"], R_FFN0 + 1)
            for c in range(KC):
                stt(u5[:, c], h[:, c], col("s5mix", c), rs[:, 0], ALU.mult, ALU.mult).then_inc(sem["u5_ready"], 1)

            def skip(c):
                dve.wait_ge(sem["y_done"], 4 * c + 4)
                stt(ta[:, 0], u5[:, c], col("s5d", c), DB[c % 4][:, 0:SEQ], ALU.mult,
                    ALU.add).then_inc(sem["y_in"], 1)

            def gelu_low(c):
                dve.wait_ge(sem["g_hi"], c + 1)
                tt(x_lo[1][:, c], y5[:, c], x_hi[1][:, c].bitcast(F32), ALU.subtract).then_inc(sem["g_lo"], 1)

            m1, m2 = [tb, sq[:, 0]], [tc, sq[:, 1]]

            def turn(j):
                b = j // LB
                if j % LB == 0:
                    dve.wait_ge(e_landed[b % LSLOTS], 16 * (b // LSLOTS + 1))
                e = e_ring[:, b % LSLOTS, j % LB]
                dve.wait_ge(sem["bu_done"], j + 1)
                if j >= 2:
                    dve.wait_ge(sem["z_ready"], 2 * (j - 1))
                bu = two([U[0], U[1], XB, MB][j % 4])
                tt(m1[j % 2][:], bu, e[:, 0:1].broadcast_to([P, 2, SEQ]), ALU.mult).then_inc(sem["turned"], 1)
                tt(m2[j % 2][:, 0], bu[:, 1], e[:, 1], ALU.mult).then_inc(sem["turned"], 1)
                tt(m2[j % 2][:, 1], bu[:, 0], e[:, 1], ALU.mult).then_inc(sem["drive"], 1)

            turn(0)
            for j in range(ST):
                if j + 1 < ST:
                    turn(j + 1)
                m1_, m2_ = m1[j % 2], m2[j % 2]
                dve.wait_ge(sem["turned"], 2 * (j + 1))
                tt(m1_[:, 0], m1_[:, 0], m2_[:, 0], ALU.add).then_inc(sem["summed"], 1)
                dve.wait_ge(sem["drive"], j + 1)
                tt(m1_[:, 1], m1_[:, 1], m2_[:, 1], ALU.subtract).then_inc(sem["summed"], 1)
                if j >= 2:
                    dve.wait_ge(sem["turned_back"], 2 * (j - 1))
                decay = mag[:, j:j + 1].broadcast_to([P, SEQ])
                for ri in range(2):
                    dve.wait_ge(sem["summed"], 2 * j + 1 + ri)
                    dve.tensor_tensor_scan(z5[:, j % 2, ri], decay, m1_[:, ri], 0.0, ALU.mult,
                                           ALU.add).then_inc(sem["z_ready"], 1)
                if j % 4 == 2 and j >= 6:
                    skip(j // 4 - 1)
                if j % 4 == 3 and j >= 7:
                    gelu_low(j // 4 - 1)
            skip(KC - 1)
            gelu_low(KC - 1)
            for m in range(PAIRS):
                done(BASE["glu"] + m)
                gated(2 * PAIRS + m + 1, y5[:, 2 * m:2 * m + 2], m)
                x_low(R_GLU, m)
                if m < 2:
                    split(BASE["glu"] + m)
            split(BASE["glu"] + 2)
            ffn(1, R_GLU, R_FFN1, late=BASE["glu"] + 3)

            g = BASE["kv"]
            norm(R_FFN1)
            dve.wait_ge(sem["rs_ready"], R_FFN1 + 1)

            def blocks(kind):
                dve.wait_ge(sem["src_ready"], kind + 1)
                dve.wait_ge(sem["cmpw_landed"], 64)
                if kind:
                    dve.wait_ge(sem["hid_done"], 2)
                for a in range(2):
                    whole = src[:, kind, a, :]
                    windows = bass.AP(whole.tensor, whole.offset, [list(whole.ap[0]), [CS, NCMP], [1, CL]])
                    last = tt(blk[:, :, a, :].rearrange("p l n -> p n l"), windows,
                              posc[:, kind].unsqueeze(1).broadcast_to([P, NCMP, CL]), ALU.add)
                last.then_inc(sem["blk_ready"], 1)

            def flat(t_, width):
                return t_.rearrange("p c t -> p (c t)")[:, 0:width]

            def key_mean(n, width):
                dve.wait_ge(sem["k_sum"], n)
                ts(norm_buffers(n, width)[2], XB[:, 0:width], 1.0 / HD, EPS, ALU.mult, ALU.add).then_inc(sem["k_mean"], 1)

            def key_norm(n, width, gain, out):
                a, y, m_, t_ = norm_buffers(n, width)
                dve.wait_ge(sem["k_exp"], n)
                tt(t_, y, y, ALU.mult).then_inc(sem["k_step"], 1)
                dve.wait_ge(sem["k_step"], 3 * n - 2)
                stt(t_, t_, -0.5, m_, ALU.mult, ALU.mult).then_inc(sem["k_step"], 1)
                dve.wait_ge(sem["k_step"], 3 * n - 1)
                stt(y, t_, 1.5, y, ALU.add, ALU.mult).then_inc(sem["k_step"], 1)
                dve.wait_ge(sem["k_step"], 3 * n)
                stt(out, a, col(gain), y, ALU.mult, ALU.mult).then_inc(sem["k_ready"], 1)

            for kind in range(2):
                done(g + kind)
                tt(src[:, kind], two(U[kind]), rs_b, ALU.mult).then_inc(sem["src_ready"], 1)
                if kind == 0:
                    for m in range(PAIRS):
                        x_low("kv", m)
                    blocks(0)
                split(g + kind)
            done(g + 2)
            tt(ta[:], two(U[0]), rs_b, ALU.mult).then_inc(sem["k_scaled"], 1)
            split(g + 2)
            split(g + 3)
            key_mean(1, 512)
            key_norm(1, 512, "ksn", ks[:, 0].rearrange("p c t -> p (c t)"))
            done(g + 4)
            dve.wait_ge(sem["k_ready"], 1)
            tt(ta[:], two(U[0]), rs_b, ALU.mult).then_inc(sem["k_scaled"], 1)
            split(g + 4)
            split(g + 5)
            key_mean(2, 512)
            key_norm(2, 512, "kwn", ks[:, 1].rearrange("p c t -> p (c t)"))
            dve.wait_ge(sem["w2_done"], 1)
            dve.wait_ge(sem["k_ready"], 2)
            dve.tensor_copy(flat(ta[:], 2 * NCMP), MB[:, 128:128 + 2 * NCMP]).then_inc(sem["k_scaled"], 1)
            blocks(1)
            key_mean(3, 2 * NCMP)
            key_norm(3, 2 * NCMP, "kcn", kcmp[:].rearrange("p c n -> p (c n)"))
            dve.wait_ge(sem["k_ready"], 3)
            ffn(2, None, R_FFN2)

            g = BASE["qg"]
            dve.wait_ge(sem["wg_hi_ready"], 1)
            tt(wg_lo[:], wg[:], wg_hi[:].bitcast(F32), ALU.subtract).then_inc(sem["wg_lo_ready"], 1)
            norm(R_FFN2)
            dve.wait_ge(sem["rs_ready"], R_FFN2 + 1)

            def queries(u):
                key_norm(4 + u, 512, "qn", q2[:, 2 * u:2 * u + 2].rearrange("p c t -> p (c t)"))

            for u in range(4):
                if u:
                    key_mean(3 + u, 512)
                done(g + u)
                if u >= 2:
                    dve.wait_ge(sem["k_ready"], 2 + u)
                tt(norm_buffers(4 + u, 512)[0].rearrange("p (c t) -> p c t", c=2), two(U[u % 2]), rs_b,
                   ALU.mult).then_inc(sem["k_scaled"], 1)
                split(g + u)
                if u:
                    queries(u - 1)
            dve.wait_ge(sem["gate_sig"], 1)
            for t in range(TT):
                last = ts(gate[:, t, 0:NH], gate[:, t, 0:NH], con[:, CCOL["anyc"] + t:CCOL["anyc"] + t + 1], None,
                          ALU.mult)
            last.then_inc(sem["gate_all"], 1)
            key_mean(7, 512)
            queries(3)

            dve.wait_ge(sem["tbl_landed"], 16)
            dve.wait_ge(sem["k_ready"], 7)
            ends = slice(CL - 1, SEQ, CS)
            seen = len(range(P)[ends])
            dve.memset(cmp_bias[:, seen:NCMP], NEG)
            dve.tensor_copy(cmp_bias[:, 0:seen], tbl[:, :, P + CL - 1:SEQ:CS].rearrange("p n c -> p c n"))
            dve.tensor_copy(cmp_bias[:, NCMP:], tbl[:, :, ends].rearrange("p n c -> p c n"))\
                .then_inc(sem["cb_ready"], 1)
            dve.wait_ge(sem["cb_ready"], 1)
            dve.wait_ge(sem["gate_all"], 1)

            def logits(hd):
                b = hd % 2
                dve.wait_ge(sem["n_s"], hd + 1)
                if hd >= 2:
                    dve.wait_ge(sem["n_t"], hd - 1)
                near, far = tbl[:, hd, P:2 * P], tbl[:, hd, :]
                stt(lgc[:, b].rearrange("p t c -> p (t c)"), DB[b][:, 3 * P:3 * P + TT * NCMP], NSCALE,
                    cmp_bias[:, :, hd], ALU.mult, ALU.add)
                for br in range(2):
                    bank = DB[2 * br + b]
                    stt(lg[:, b, br, 0:P], bank[:, 0:P], NSCALE, near, ALU.mult, ALU.add)
                    last = stt(lg[:, b, br, P:3 * P], bank[:, P:3 * P], NSCALE, far, ALU.mult, ALU.add)
                last.then_inc(sem["n_log"], 1)
                dve.wait_ge(sem["n_log"], hd + 1)
                dve.tensor_reduce(nm[:, b, 0, :], lgc[:, b], AX.X, ALU.max, negate=True)
                for br in range(2):
                    dve.tensor_reduce(nm[:, b, 1 + br, 0:1], lg[:, b, br, 0:P], AX.X, ALU.max, negate=True)
                    last = dve.tensor_reduce(nm[:, b, 1 + br, 1:2], lg[:, b, br, P:3 * P], AX.X, ALU.max, negate=True)
                last.then_inc(sem["n_max"], 1)

            def window_copy(hd):
                dve.wait_ge(sem["n_t"], hd + 1)
                if hd >= 2:
                    dve.wait_ge(sem["n_pv"], hd - 1)
                dve.tensor_copy(ptn[:, hd % 2, 1], U[1][:, 0:3 * P]).then_inc(sem["n_tv"], 1)

            def combine(hd):
                b = hd % 2
                dve.wait_ge(sem["n_exp"], hd + 1)
                dve.reciprocal(fac[:, b].rearrange("p r t -> p (r t)"),
                               dn[:, b].rearrange("p r t -> p (r t)")).then_inc(sem["n_rec"], 1)
                dve.wait_ge(sem["n_rec"], hd + 1)
                tt(fac[:, b], fac[:, b], gate[:].rearrange("p t (r n) -> p r t n", n=NH)[:, :, :, hd],
                   ALU.mult).then_inc(sem["n_fac"], 1)
                dve.wait_ge(sem["n_pv"], hd + 1)
                dve.wait_ge(sem["n_fac"], hd + 1)
                for br in range(3):
                    if br:
                        dve.wait_ge(sem["n_part"], 3 * hd + br)
                    for t in range(TT):
                        at = (br * TT + t) * HD
                        out = oc[:, hd // 2 % 2, t, b]
                        f = fac[:, b, br, t:t + 1]
                        if br:
                            last = stt(out, XB[:, at:at + HD], f, out, ALU.mult, ALU.add)
                        else:
                            last = ts(out, XB[:, at:at + HD], f, None, ALU.mult)
                    last.then_inc(sem["n_part"], 1)

            def n_low(ch):
                dve.wait_ge(sem["n_hi"], ch + 1)
                tt(x_lo[0][:, ch], MB[:, SEQ:2 * SEQ], x_hi[0][:, ch].bitcast(F32),
                   ALU.subtract).then_inc(sem["n_lo"], 1)

            for step in range(NH + 1):
                if step:
                    window_copy(step - 1)
                if step < NH:
                    logits(step)
                if step:
                    combine(step - 1)
                if step and step % 2 == 0:
                    n_low(step // 2 - 1)
            residual_stage("nwo", R_NWO)
            ffn(3, R_NWO, R_FFN3, x=False, late=BASE["nwo"] + 3)


def _wide(w):
    return w.reshape(KC, P, 256).transpose(1, 0, 2).reshape(P, UNIT)


def _deep(w):
    return w.reshape(2, P, D).transpose(1, 0, 2).reshape(P, UNIT)


def _units(i):
    w = i["sc_w_in"][0]
    for j in range(PAIRS):
        for part in (1, 2, 0):
            yield _wide(w[:, part * D + 256 * j:part * D + 256 * (j + 1)])

    def square(w):
        for m in range(PAIRS):
            yield _wide(w[:, 256 * m:256 * (m + 1)])

    def mlp(l):
        up, down = i["mlp_w_up"][l], i["mlp_w_down"][l]
        for n in range(MLP_PAIRS + 1):
            if n < MLP_PAIRS:
                yield _wide(up[:, 256 * n:256 * (n + 1)])
            if n:
                yield _deep(down[256 * (n - 1):256 * n])

    def ple(l):
        yield _deep(i["ple_w_proj"][l])
        yield from square(i["ple_w_gate"][l])

    def ffn(w_in, w_out):
        for n in range(FFN_PAIRS + 1):
            if n < FFN_PAIRS:
                yield _wide(w_in[:, 256 * n:256 * (n + 1)])
                yield _wide(w_in[:, D_FF2 + 256 * n:D_FF2 + 256 * (n + 1)])
            if n:
                yield _deep(w_out[256 * (n - 1):256 * n])

    yield from square(i["sc_w_out"][0])
    yield from mlp(0)
    yield from ple(0)
    w = i["attn_w_qkv"][0].reshape(D, 3, NG, HEADS, DH)
    for pair in range(HEAD_PAIRS):
        for side in range(2):
            for gr in range(NG):
                yield _wide(w[:, 0:2, gr, 2 * pair + side].reshape(D, 256))
        for gr in range(NG):
            yield _wide(w[:, 2, gr, 2 * pair:2 * pair + 2].reshape(D, 256))
    yield from square(i["attn_w_o"][0])
    yield from mlp(1)
    yield from ple(1)
    yield from ffn(i["ffn1_w_in_2"][0], i["ffn1_w_out_2"][0])
    yield from square(i["s5_w_glu_2"][0])
    yield from ffn(i["ffn2_w_in_2"][0], i["ffn2_w_out_2"][0])
    for u in range(6):
        yield _wide(i["w_kv_2"][:, 256 * u:256 * (u + 1)])
    yield from ffn(i["ffn1_w_in_2"][1], i["ffn1_w_out_2"][1])
    heads = head_order()
    wq = i["w_qg_2"][0][:, :D].reshape(D, NH, HD)[:, heads].reshape(D, D)
    yield from square(wq)
    yield from square(i["w_o_2"][0].reshape(NH, HD, D)[heads].reshape(D, D))
    yield from ffn(i["ffn2_w_in_2"][1], i["ffn2_w_out_2"][1])


def _constants():
    c = np.zeros((P, NCON), np.float32)
    put = lambda name, v: c.__setitem__((slice(None), slice(CCOL[name], CCOL[name] + v.shape[1])), v)
    put("ident", np.eye(P, dtype=np.float32))
    put("half", np.kron(np.eye(2), np.ones((HD, HD))).astype(np.float32))
    q, k = np.arange(SEQ)[:, None], np.arange(SEQ)[None, :]
    near, far = [], []
    for window, dil in GROUPS:
        ok = (k <= q) & ((q - k) % dil == 0) & ((q - k) // dil <= window // dil)
        m = np.where(ok, 0.0, NEG).astype(np.float32)
        near.append(m[:P, :P])
        far.append(m[P:])
    put("mask0", np.concatenate(near, 1))
    put("mask1", np.concatenate(far, 1))
    tok = np.arange(P)[:, None] + P * np.arange(TT)[None, :]
    put("anyc", (tok >= CL - 1).astype(np.float32))
    half = ROPE // 2
    inv = np.float32(THETA) ** (np.float32(-2.0) * np.arange(half, dtype=np.float32) / np.float32(ROPE))
    f, s = np.zeros((P, 1), np.float32), np.zeros((P, 1), np.float32)
    f[:half, 0] = f[half:ROPE, 0] = inv
    s[:half], s[half:ROPE] = -1.0, 1.0
    put("invf", f)
    put("sgn", s)
    return c


def _onehot(dist):
    n = np.maximum(dist, 0)
    exact = NBUCKET // 2
    logv = np.log(np.maximum(n, 1).astype(np.float32) / exact) / np.float32(math.log(MAXDIST / exact))
    large = np.minimum(exact + (logv * (NBUCKET - exact)).astype(np.int32), NBUCKET - 1)
    bucket = np.where(dist < 0, NBUCKET, np.where(n < exact, n, large))
    return (np.arange(NBUCKET + 1).reshape((-1,) + (1,) * dist.ndim) == bucket).astype(np.float32)


def _features(v):
    return v.reshape(KC, P).T


def _states(v):
    v = v.reshape((ST, P) + v.shape[2:])
    return v.transpose((1, 0) + tuple(range(2, v.ndim)))


def _layout(i):
    heads = head_order()
    vec = np.concatenate(
        [_features(v) for v in (i["norm_mix"][0], i["norm_mlp"][0], i["norm_ple"][0], i["norm_mix"][1],
                                i["norm_mlp"][1], i["norm_ple"][1], i["norm_final"], i["ffn1_norm_2"][0],
                                i["mix_norm_2"][0], i["ffn2_norm_2"][0], i["kv_norm_2"], i["ffn1_norm_2"][1],
                                i["mix_norm_2"][1], i["ffn2_norm_2"][1], *i["sc_w_conv"][0], i["s5_d_2"][0].reshape(-1))]
        + [np.concatenate([v, v]).reshape(P, 1) for v in (i["q_norm_2"][0], i["k_norm_cmp_2"], i["k_norm_slc_2"],
                                                          i["k_norm_win_2"])]
        + [_states(i["s5_a_re_2"][0]), _states(i["s5_a_im_2"][0]),
           _states(np.broadcast_to(i["s5_log_dt_2"][0][:, None], (S5_G, S5_STATE)))], 1)
    gate_w = i["w_qg_2"][0][:, D:].reshape(D, NH, 3)[:, heads].transpose(0, 2, 1).reshape(KC, P, 3 * NH)
    twice = lambda v: np.concatenate([v, v], 0)
    return {
        "x": i["x"][0].T,
        "p": i["p"][:, 0].transpose(0, 2, 1),
        "positions": i["positions"],
        "weights": np.stack(list(_units(i))),
        "vec": vec,
        "con": _constants(),
        "s5b": np.stack([_states(i["s5_b_re_2"][0]), _states(i["s5_b_im_2"][0])], 1),
        "s5c": np.stack([_states(i["s5_c_re_2"][0].transpose(0, 2, 1)), _states(i["s5_c_im_2"][0].transpose(0, 2, 1))],
                        1),
        "rel_bias": i["rel_bias_2"][:, heads],
        "onehot": _onehot(SEQ - 1 - np.arange(NDIST)),
        "cmp_w1": np.stack([twice(w.transpose(1, 0, 2)) for w in (i["cmp_k_w1_2"], i["cmp_v_w1_2"])]),
        "cmp_w2": np.stack([i["cmp_k_w2_2"], i["cmp_v_w2_2"]], 1),
        "cmp_pos": np.stack([twice(i["cmp_pos_k_2"].T), twice(i["cmp_pos_v_2"].T)], 1),
        "gate_w": gate_w.transpose(1, 0, 2),
    }


def kernel(**inputs):
    from concourse import bacc
    from concourse.bass_utils import run_bass_kernel_spmd

    nc = bacc.Bacc("TRN2", target_bir_lowering=False, num_devices=1)
    arrays, A = {}, {}
    for name, a in _layout({k: np.asarray(v) for k, v in inputs.items()}).items():
        arrays[f"in_{name}"] = np.ascontiguousarray(a)
        A[name] = nc.dram_tensor(f"in_{name}", arrays[f"in_{name}"].shape, mybir.dt.from_np(a.dtype),
                                 kind="ExternalInput").ap()
    A["e_table"] = nc.dram_tensor("e_table", [ST // EB, P, EB * 2 * SEQ], F32, kind="Internal").ap()
    A["bias_rows"] = nc.dram_tensor("bias_rows", [NH, P, NDIST], F32, kind="Internal").ap()
    A["out"] = nc.dram_tensor("out", [D, SEQ], F32, kind="ExternalOutput").ap()
    program(nc, A)
    r = run_bass_kernel_spmd(nc, [arrays], core_ids=[0])
    return np.ascontiguousarray(np.asarray(r.results[0]["out"]).T).reshape(1, SEQ, D)
```
